# Optimizing a Trainium2 kernel written in Bass

```python
import math
import jax
import jax.numpy as jnp
from jax import lax
import numpy as np
import jax, jax.numpy as jnp

D_MODEL = 1024
BATCH = 1
SEQ = 256
DEPTH = 2

N_A_LAYERS = DEPTH // 2
N_B_LAYERS = DEPTH - N_A_LAYERS

SSM_EXPAND = 2
D_INNER = SSM_EXPAND * D_MODEL
SSM_HEAD_DIM = 64
SSM_HEADS = D_INNER // SSM_HEAD_DIM
SSM_GROUPS = 4
SSM_HEADS_PER_GROUP = SSM_HEADS // SSM_GROUPS
SSM_STATE = 128
SSM_CONV = 4
SSM_CHUNK = 128
SSM_CONV_DIM = D_INNER + 2 * SSM_GROUPS * SSM_STATE
SSM_IN_DIM = D_INNER + SSM_CONV_DIM + SSM_HEADS

ATT_HEAD_DIM = 64
ATT_HEADS = D_MODEL // (2 * ATT_HEAD_DIM)
ATT_V_DIM = 2 * ATT_HEAD_DIM
ATT_BLOCK = 128
K_DIM = ATT_HEADS * 2 * ATT_HEAD_DIM
V_TOTAL = ATT_HEADS * ATT_V_DIM

NUM_BUCKETS = 32
MAX_DISTANCE = 128

FFN_DIM = 256 * ((8 * D_MODEL // 3 + 255) // 256)
FFN_CONV = 3

EPS = 1e-6


def rms_norm(x, g):
    xf = x.astype(jnp.float32)
    y = xf * lax.rsqrt(jnp.mean(xf * xf, axis=-1, keepdims=True) + EPS)
    return y.astype(x.dtype) * g

def causal_dwconv(u, w, b):
    k_w = w.shape[0]
    s = u.shape[1]
    up = jnp.pad(u, ((0, 0), (k_w - 1, 0), (0, 0)))
    y = up[:, 0:s] * w[0]
    for k in range(1, k_w):
        y = y + up[:, k:k + s] * w[k]
    return y + b

def segsum(a):
    t = a.shape[-1]
    cs = jnp.cumsum(a, axis=-1)
    d = cs[..., :, None] - cs[..., None, :]
    mask = jnp.tril(jnp.ones((t, t), dtype=bool))
    return jnp.where(mask, d, -jnp.inf)

def ssd_chunked(xdt, a, bm, cm):
    b, s, h, p = xdt.shape
    g, r, l = SSM_GROUPS, SSM_HEADS_PER_GROUP, SSM_CHUNK
    c = s // l
    xc = xdt.reshape(b, c, l, g, r, p)
    ac = a.reshape(b, c, l, g, r).transpose(0, 3, 4, 1, 2)
    bc = bm.reshape(b, c, l, g, SSM_STATE)
    cc = cm.reshape(b, c, l, g, SSM_STATE)
    a_cs = jnp.cumsum(ac, axis=-1)
    decay_in = jnp.exp(segsum(ac))
    cb = jnp.einsum('bclgn,bcsgn->bcgls', cc, bc)
    y_diag = jnp.einsum('bcgls,bgrcls,bcsgrp->bclgrp', cb, decay_in, xc)
    decay_states = jnp.exp(a_cs[..., -1:] - a_cs)
    states = jnp.einsum('bclgn,bgrcl,bclgrp->bcgrpn', bc, decay_states, xc)
    states0 = jnp.concatenate([jnp.zeros_like(states[:, :1]), states], axis=1)
    chunk_tot = jnp.pad(a_cs[..., -1], ((0, 0), (0, 0), (0, 0), (1, 0)))
    decay_chunk = jnp.exp(segsum(chunk_tot))
    new_states = jnp.einsum('bgrzc,bcgrpn->bzgrpn', decay_chunk, states0)
    states_in = new_states[:, :-1]
    y_off = jnp.einsum('bclgn,bcgrpn,bgrcl->bclgrp', cc, states_in, jnp.exp(a_cs))
    return (y_diag + y_off).reshape(b, s, h, p)

def mamba2_mixer(x, ln_g, in_w, conv_w, conv_b, dt_bias, a_log, d_skip, norm_g, out_w):
    b, s, _ = x.shape
    zxbcdt = rms_norm(x, ln_g) @ in_w
    z = zxbcdt[..., :D_INNER]
    xbc = zxbcdt[..., D_INNER:D_INNER + SSM_CONV_DIM]
    dt = zxbcdt[..., D_INNER + SSM_CONV_DIM:]
    xbc = jax.nn.silu(causal_dwconv(xbc, conv_w, conv_b))
    gn = SSM_GROUPS * SSM_STATE
    xs = xbc[..., :D_INNER].reshape(b, s, SSM_HEADS, SSM_HEAD_DIM)
    bm = xbc[..., D_INNER:D_INNER + gn].reshape(b, s, SSM_GROUPS, SSM_STATE)
    cm = xbc[..., D_INNER + gn:].reshape(b, s, SSM_GROUPS, SSM_STATE)
    dt = jax.nn.softplus(dt.astype(jnp.float32) + dt_bias.astype(jnp.float32))
    a = dt * (-jnp.exp(a_log.astype(jnp.float32)))
    xs32 = xs.astype(jnp.float32)
    y = ssd_chunked(xs32 * dt[..., None], a, bm.astype(jnp.float32), cm.astype(jnp.float32))
    y = y + xs32 * d_skip.astype(jnp.float32)[:, None]
    y = y.reshape(b, s, D_INNER) * jax.nn.silu(z.astype(jnp.float32))
    y = rms_norm(y.reshape(b, s, SSM_GROUPS, D_INNER // SSM_GROUPS),
                 norm_g.reshape(SSM_GROUPS, D_INNER // SSM_GROUPS)).reshape(b, s, D_INNER)
    return y @ out_w

def conv_ffn(x, ln_g, up_w, conv_w, conv_b, down_w):
    u = causal_dwconv(rms_norm(x, ln_g) @ up_w, conv_w, conv_b)
    gate, up = u[..., :FFN_DIM], u[..., FFN_DIM:]
    return (jax.nn.silu(gate) * up) @ down_w

def shared_kv(x, kv_ln_g, kv_w, k_norm_g):
    b, s, _ = x.shape
    kv = rms_norm(x, kv_ln_g) @ kv_w
    k = kv[..., :K_DIM].reshape(b, s, ATT_HEADS, 2, ATT_HEAD_DIM)
    v = kv[..., K_DIM:].reshape(b, s, ATT_HEADS, ATT_V_DIM)
    return rms_norm(k, k_norm_g), v

def t5_bucket(dist):
    n = jnp.maximum(dist, 0)
    max_exact = NUM_BUCKETS // 2
    nf = jnp.maximum(n, 1).astype(jnp.float32)
    large = max_exact + (jnp.log(nf / max_exact) / math.log(MAX_DISTANCE / max_exact)
                         * (NUM_BUCKETS - max_exact)).astype(jnp.int32)
    large = jnp.minimum(large, NUM_BUCKETS - 1)
    return jnp.where(n < max_exact, n, large)

def diff_attention(x, k, v, rel_bias, ln_g, q_w, q_norm_g, lam_vecs, subln_g, out_w, lam_init):
    b, s, _ = x.shape
    q = (rms_norm(x, ln_g) @ q_w).reshape(b, s, ATT_HEADS, 2, ATT_HEAD_DIM)
    q = rms_norm(q, q_norm_g)
    lv = lam_vecs.astype(jnp.float32)
    lam = jnp.exp(jnp.sum(lv[0] * lv[1])) - jnp.exp(jnp.sum(lv[2] * lv[3])) + lam_init
    scale = ATT_HEAD_DIM ** -0.5
    nb = s // ATT_BLOCK
    qb = q.reshape(b, nb, ATT_BLOCK, ATT_HEADS, 2, ATT_HEAD_DIM).transpose(1, 0, 2, 3, 4, 5)
    kpos = jnp.arange(s)

    def block(args):
        qblk, i = args
        qpos = i * ATT_BLOCK + jnp.arange(ATT_BLOCK)
        dist = qpos[:, None] - kpos[None, :]
        bias = rel_bias[t5_bucket(dist)].astype(jnp.float32).transpose(2, 0, 1)
        logits = jnp.einsum('bqhcd,bkhcd->bhcqk', qblk, k).astype(jnp.float32) * scale
        logits = logits + bias[None, :, None]
        logits = jnp.where(dist >= 0, logits, -jnp.inf)
        p = jax.nn.softmax(logits, axis=-1)
        attn = p[:, :, 0] - lam * p[:, :, 1]
        return jnp.einsum('bhqk,bkhd->bqhd', attn.astype(v.dtype), v)

    o = lax.map(block, (qb, jnp.arange(nb)))
    o = o.transpose(1, 0, 2, 3, 4).reshape(b, s, ATT_HEADS, ATT_V_DIM)
    o = rms_norm(o, subln_g) * (1.0 - lam_init)
    return o.reshape(b, s, V_TOTAL) @ out_w

def first_inputs(seed: int = 0) -> dict:
    key = jax.random.key(seed)
    ks = jax.random.split(key, 32)
    f32 = jnp.float32

    def nrm(k, shape, scale):
        return jax.random.normal(k, shape, f32) * scale

    def gain(k, shape):
        return 1.0 + 0.02 * jax.random.normal(k, shape, f32)

    na, nb = N_A_LAYERS, N_B_LAYERS
    dt = jnp.exp(jax.random.uniform(ks[6], (na, SSM_HEADS), f32)
                 * (math.log(0.1) - math.log(0.001)) + math.log(0.001))
    return {
        'x': nrm(ks[0], (BATCH, SEQ, D_MODEL), 1.0),
        'ssm_ln_g': gain(ks[1], (na, D_MODEL)),
        'ssm_in_w': nrm(ks[2], (na, D_MODEL, SSM_IN_DIM), D_MODEL ** -0.5),
        'ssm_conv_w': nrm(ks[3], (na, SSM_CONV, SSM_CONV_DIM), SSM_CONV ** -0.5),
        'ssm_conv_b': nrm(ks[4], (na, SSM_CONV_DIM), 0.02),
        'ssm_dt_bias': dt + jnp.log(-jnp.expm1(-dt)),
        'ssm_a_log': jnp.log(jax.random.uniform(ks[7], (na, SSM_HEADS), f32, 1.0, 16.0)),
        'ssm_d': gain(ks[8], (na, SSM_HEADS)),
        'ssm_norm_g': gain(ks[9], (na, D_INNER)),
        'ssm_out_w': nrm(ks[10], (na, D_INNER, D_MODEL), D_INNER ** -0.5),
        'kv_ln_g': gain(ks[11], (D_MODEL,)),
        'kv_w': nrm(ks[12], (D_MODEL, K_DIM + V_TOTAL), D_MODEL ** -0.5),
        'k_norm_g': gain(ks[13], (ATT_HEAD_DIM,)),
        'rel_bias': nrm(ks[14], (NUM_BUCKETS, ATT_HEADS), 0.5),
        'attn_ln_g': gain(ks[15], (nb, D_MODEL)),
        'q_w': nrm(ks[16], (nb, D_MODEL, K_DIM), D_MODEL ** -0.5),
        'q_norm_g': gain(ks[17], (nb, ATT_HEAD_DIM)),
        'lam_vecs': nrm(ks[18], (nb, 4, ATT_HEAD_DIM), 0.1),
        'subln_g': gain(ks[19], (nb, ATT_V_DIM)),
        'attn_out_w': nrm(ks[20], (nb, V_TOTAL, D_MODEL), V_TOTAL ** -0.5),
        'ffn_ln_g': gain(ks[21], (DEPTH, D_MODEL)),
        'ffn_up_w': nrm(ks[22], (DEPTH, D_MODEL, 2 * FFN_DIM), D_MODEL ** -0.5),
        'ffn_conv_w': nrm(ks[23], (DEPTH, FFN_CONV, 2 * FFN_DIM), FFN_CONV ** -0.5),
        'ffn_conv_b': nrm(ks[24], (DEPTH, 2 * FFN_DIM), 0.02),
        'ffn_down_w': nrm(ks[25], (DEPTH, FFN_DIM, D_MODEL), FFN_DIM ** -0.5),
    }

def first_block(x, ssm_ln_g, ssm_in_w, ssm_conv_w, ssm_conv_b, ssm_dt_bias, ssm_a_log, ssm_d,
              ssm_norm_g, ssm_out_w, kv_ln_g, kv_w, k_norm_g, rel_bias, attn_ln_g, q_w,
              q_norm_g, lam_vecs, subln_g, attn_out_w, ffn_ln_g, ffn_up_w, ffn_conv_w,
              ffn_conv_b, ffn_down_w):
    k_sh, v_sh = None, None
    for layer in range(DEPTH):
        if layer < N_A_LAYERS:
            i = layer
            mix = mamba2_mixer(x, ssm_ln_g[i], ssm_in_w[i], ssm_conv_w[i], ssm_conv_b[i],
                               ssm_dt_bias[i], ssm_a_log[i], ssm_d[i], ssm_norm_g[i],
                               ssm_out_w[i])
        else:
            j = layer - N_A_LAYERS
            if j == 0:
                k_sh, v_sh = shared_kv(x, kv_ln_g, kv_w, k_norm_g)
            lam_init = 0.8 - 0.6 * math.exp(-0.3 * layer)
            mix = diff_attention(x, k_sh, v_sh, rel_bias, attn_ln_g[j], q_w[j], q_norm_g[j],
                                 lam_vecs[j], subln_g[j], attn_out_w[j], lam_init)
        x = x + mix.astype(x.dtype)
        ff = conv_ffn(x, ffn_ln_g[layer], ffn_up_w[layer], ffn_conv_w[layer],
                      ffn_conv_b[layer], ffn_down_w[layer])
        x = x + ff.astype(x.dtype)
    return x


DEPTH_2 = 1

N_HEADS = 8
HEAD_DIM = 64
N_KV_HEADS = 2
IDX_HEADS = 8
IDX_DIM = 64
TOPK_MAX = 256
Q_BLOCK = 64
N_BUCKETS = 32
D_RNN = D_MODEL
N_RNN_BLOCKS = 8
RNN_BLOCK = D_RNN // N_RNN_BLOCKS
RNN_CONV = 4
LRU_C = 8.0
D_FF = 2816

ATTN_WIDTH = N_HEADS * HEAD_DIM
KV_WIDTH = N_KV_HEADS * HEAD_DIM
SPLITS = (ATTN_WIDTH, KV_WIDTH, KV_WIDTH, IDX_HEADS * IDX_DIM, IDX_DIM, IDX_HEADS, D_RNN, D_RNN, D_MODEL, D_MODEL)
N_IN = 5448


def rms_norm_2(x, g):
    x32 = x.astype(jnp.float32)
    y = x32 * lax.rsqrt(jnp.mean(x32 * x32, axis=-1, keepdims=True) + EPS)
    return (y * g.astype(jnp.float32)).astype(x.dtype)

def causal_dwconv_2(x, w, b):
    width = w.shape[0]
    seq = x.shape[1]
    xp = jnp.pad(x, ((0, 0), (width - 1, 0), (0, 0)))
    y = xp[:, 0:seq] * w[0]
    for k in range(1, width):
        y = y + xp[:, k:k + seq] * w[k]
    return y + b

def t5_bucket_2(rel):
    max_exact = N_BUCKETS // 2
    n = jnp.maximum(rel, 0)
    nf = jnp.maximum(n, 1).astype(jnp.float32)
    large = max_exact + (jnp.log(nf / max_exact) / math.log(MAX_DISTANCE / max_exact)
                         * (N_BUCKETS - max_exact)).astype(jnp.int32)
    large = jnp.minimum(large, N_BUCKETS - 1)
    return jnp.where(n < max_exact, n, large)

def dsa_attention(q, k, v, q_idx, k_idx, w_idx, rel_bias):
    B, S = q.shape[0], q.shape[1]
    n_sel = min(TOPK_MAX, S // 4)
    nb = S // Q_BLOCK
    G = N_HEADS // N_KV_HEADS
    pos = jnp.arange(S, dtype=jnp.int32)
    gather = jax.vmap(lambda t_b, i_b: t_b[i_b])

    def to_blocks(t):
        return jnp.moveaxis(t.reshape((B, nb, Q_BLOCK) + t.shape[2:]), 1, 0)

    def block(args):
        qb, qib, wb, tb = args
        dots = jnp.einsum('bqhd,bsd->bqhs', qib, k_idx).astype(jnp.float32) * (IDX_DIM ** -0.5)
        score = jnp.einsum('bqh,bqhs->bqs', wb.astype(jnp.float32) * (IDX_HEADS ** -0.5), jax.nn.relu(dots))
        causal = pos[None, :] <= tb[:, None]
        score = jnp.where(causal[None], score, -jnp.inf)
        _, sel = lax.top_k(score, n_sel)
        valid = sel <= tb[None, :, None]
        ks = gather(k, sel)
        vs = gather(v, sel)
        qg = qb.reshape(B, Q_BLOCK, N_KV_HEADS, G, HEAD_DIM)
        logits = jnp.einsum('bqhgd,bqnhd->bqhgn', qg, ks).astype(jnp.float32) * (HEAD_DIM ** -0.5)
        bucket = t5_bucket_2(tb[None, :, None] - sel)
        bias = rel_bias[bucket].astype(jnp.float32)
        bias = bias.reshape(B, Q_BLOCK, n_sel, N_KV_HEADS, G).transpose(0, 1, 3, 4, 2)
        logits = jnp.where(valid[:, :, None, None, :], logits + bias, -jnp.inf)
        p = jax.nn.softmax(logits, axis=-1).astype(vs.dtype)
        o = jnp.einsum('bqhgn,bqnhd->bqhgd', p, vs)
        return o.reshape(B, Q_BLOCK, N_HEADS * HEAD_DIM)

    out = lax.map(block, (to_blocks(q), to_blocks(q_idx), to_blocks(w_idx), pos.reshape(nb, Q_BLOCK)))
    return jnp.moveaxis(out, 0, 1).reshape(B, S, N_HEADS * HEAD_DIM)

def rg_lru(x, w_rg, b_rg, w_ig, b_ig, lam):
    B, S = x.shape[0], x.shape[1]
    xb = x.reshape(B, S, N_RNN_BLOCKS, RNN_BLOCK)
    r = jax.nn.sigmoid(jnp.einsum('bsnc,ncd->bsnd', xb, w_rg).reshape(B, S, D_RNN) + b_rg)
    i = jax.nn.sigmoid(jnp.einsum('bsnc,ncd->bsnd', xb, w_ig).reshape(B, S, D_RNN) + b_ig)
    log_a = -LRU_C * r.astype(jnp.float32) * jax.nn.softplus(-lam.astype(jnp.float32))
    a = jnp.exp(log_a)
    mult = jnp.sqrt(-jnp.expm1(2.0 * log_a))
    u = x.astype(jnp.float32) * i.astype(jnp.float32) * mult

    def combine(left, right):
        a1, b1 = left
        a2, b2 = right
        return a1 * a2, a2 * b1 + b2

    _, h = lax.associative_scan(combine, (a, u), axis=1)
    return h.astype(x.dtype)

def second_inputs(seed: int = 0) -> dict:
    key = jax.random.key(seed)
    ks = jax.random.split(key, 32)
    f32 = jnp.float32

    def nrm(k, shape, scale):
        return jax.random.normal(k, shape, f32) * scale

    L = DEPTH_2
    a0 = jax.random.uniform(ks[13], (L, D_RNN), f32, 0.9, 0.999)
    p = a0 ** (1.0 / LRU_C)
    lam = jnp.log(p) - jnp.log1p(-p)
    return {
        "x": nrm(ks[0], (BATCH, SEQ, D_MODEL), 1.0),
        "c": nrm(ks[1], (BATCH, D_MODEL), 1.0),
        "w_ada": nrm(ks[2], (L, D_MODEL, 6 * D_MODEL), D_MODEL ** -0.5),
        "b_ada": nrm(ks[3], (L, 6 * D_MODEL), 0.02),
        "g_mix": 1.0 + nrm(ks[4], (L, D_MODEL), 0.02),
        "w_in": nrm(ks[5], (L, D_MODEL, N_IN), D_MODEL ** -0.5),
        "b_in": nrm(ks[6], (L, N_IN), 0.01),
        "rel_bias": nrm(ks[7], (N_BUCKETS, N_HEADS), 0.5),
        "conv_rnn_w": nrm(ks[8], (L, RNN_CONV, D_RNN), RNN_CONV ** -0.5),
        "conv_rnn_b": nrm(ks[9], (L, D_RNN), 0.01),
        "w_rg": nrm(ks[10], (L, N_RNN_BLOCKS, RNN_BLOCK, RNN_BLOCK), RNN_BLOCK ** -0.5),
        "b_rg": nrm(ks[11], (L, D_RNN), 0.01),
        "w_ig": nrm(ks[12], (L, N_RNN_BLOCKS, RNN_BLOCK, RNN_BLOCK), RNN_BLOCK ** -0.5),
        "b_ig": nrm(ks[14], (L, D_RNN), 0.01),
        "lru_lambda": lam,
        "w_o_attn": nrm(ks[15], (L, ATTN_WIDTH, D_MODEL), ATTN_WIDTH ** -0.5),
        "w_o_rnn": nrm(ks[16], (L, D_RNN, D_MODEL), D_RNN ** -0.5),
        "w_out": nrm(ks[17], (L, D_MODEL, D_MODEL), D_MODEL ** -0.5),
        "g_ffn": 1.0 + nrm(ks[18], (L, D_MODEL), 0.02),
        "w_up": nrm(ks[19], (L, D_MODEL, 2 * D_FF), D_MODEL ** -0.5),
        "conv_ffn_w": nrm(ks[20], (L, FFN_CONV, 2 * D_FF), FFN_CONV ** -0.5),
        "conv_ffn_b": nrm(ks[21], (L, 2 * D_FF), 0.01),
        "w_down": nrm(ks[22], (L, D_FF, D_MODEL), D_FF ** -0.5),
        "g_final": 1.0 + nrm(ks[23], (D_MODEL,), 0.02),
    }

def second_block(x, c, w_ada, b_ada, g_mix, w_in, b_in, rel_bias, conv_rnn_w, conv_rnn_b,
              w_rg, b_rg, w_ig, b_ig, lru_lambda, w_o_attn, w_o_rnn, w_out, g_ffn,
              w_up, conv_ffn_w, conv_ffn_b, w_down, g_final):
    B, S = x.shape[0], x.shape[1]
    cuts = []
    acc = 0
    for width in SPLITS[:-1]:
        acc += width
        cuts.append(acc)
    c_act = jax.nn.silu(c)
    h = x
    for l in range(DEPTH_2):
        mod = jnp.dot(c_act, w_ada[l]) + b_ada[l]
        sh1, sc1, ga1, sh2, sc2, ga2 = [m[:, None, :] for m in jnp.split(mod, 6, axis=-1)]

        xn = rms_norm_2(h, g_mix[l]) * (1.0 + sc1) + sh1
        proj = jnp.dot(xn, w_in[l]) + b_in[l]
        q, k, v, qi, ki, wi, xr, yr, gate_a, gate_b = jnp.split(proj, cuts, axis=-1)

        attn = dsa_attention(
            q.reshape(B, S, N_HEADS, HEAD_DIM),
            k.reshape(B, S, N_KV_HEADS, HEAD_DIM),
            v.reshape(B, S, N_KV_HEADS, HEAD_DIM),
            qi.reshape(B, S, IDX_HEADS, IDX_DIM), ki, wi, rel_bias)

        xr = causal_dwconv_2(xr, conv_rnn_w[l], conv_rnn_b[l])
        rnn = rg_lru(xr, w_rg[l], b_rg[l], w_ig[l], b_ig[l], lru_lambda[l]) * jax.nn.gelu(yr)

        merged = (jax.nn.sigmoid(gate_a) * jnp.dot(attn, w_o_attn[l])
                  + jax.nn.sigmoid(gate_b) * jnp.dot(rnn, w_o_rnn[l]))
        h = h + ga1 * jnp.dot(merged, w_out[l])

        xn = rms_norm_2(h, g_ffn[l]) * (1.0 + sc2) + sh2
        up = causal_dwconv_2(jnp.dot(xn, w_up[l]), conv_ffn_w[l], conv_ffn_b[l])
        val, gte = jnp.split(up, 2, axis=-1)
        h = h + ga2 * jnp.dot(jax.nn.silu(gte) * val, w_down[l])
    return rms_norm_2(h, g_final)


def setup_inputs(seed=0):
    out = dict(first_inputs(seed))
    for name, value in second_inputs(seed + 1).items():
        if name != "x":
            out[name + "_2"] = value
    return out


def reference(
    x, ssm_ln_g, ssm_in_w, ssm_conv_w, ssm_conv_b, ssm_dt_bias, ssm_a_log, ssm_d, ssm_norm_g,
    ssm_out_w, kv_ln_g, kv_w, k_norm_g, rel_bias, attn_ln_g, q_w, q_norm_g, lam_vecs, subln_g,
    attn_out_w, ffn_ln_g, ffn_up_w, ffn_conv_w, ffn_conv_b, ffn_down_w, c_2, w_ada_2, b_ada_2,
    g_mix_2, w_in_2, b_in_2, rel_bias_2, conv_rnn_w_2, conv_rnn_b_2, w_rg_2, b_rg_2, w_ig_2,
    b_ig_2, lru_lambda_2, w_o_attn_2, w_o_rnn_2, w_out_2, g_ffn_2, w_up_2, conv_ffn_w_2,
    conv_ffn_b_2, w_down_2, g_final_2,
):
    x = first_block(
        x, ssm_ln_g, ssm_in_w, ssm_conv_w, ssm_conv_b, ssm_dt_bias, ssm_a_log, ssm_d,
        ssm_norm_g, ssm_out_w, kv_ln_g, kv_w, k_norm_g, rel_bias, attn_ln_g, q_w, q_norm_g,
        lam_vecs, subln_g, attn_out_w, ffn_ln_g, ffn_up_w, ffn_conv_w, ffn_conv_b, ffn_down_w,
    )
    return second_block(
        x, c_2, w_ada_2, b_ada_2, g_mix_2, w_in_2, b_in_2, rel_bias_2, conv_rnn_w_2,
        conv_rnn_b_2, w_rg_2, b_rg_2, w_ig_2, b_ig_2, lru_lambda_2, w_o_attn_2, w_o_rnn_2,
        w_out_2, g_ffn_2, w_up_2, conv_ffn_w_2, conv_ffn_b_2, w_down_2, g_final_2,
    )


_drawn_inputs = setup_inputs


def setup_inputs(seed=0):
    import zlib

    import numpy as np

    out = dict(_drawn_inputs(seed))
    spreads = {}
    factors = {'ssm_d': 3.976,
     'kv_ln_g': 3.937,
     'k_norm_g': 5.424,
     'attn_ln_g': 5.41,
     'q_norm_g': 5.448,
     'subln_g': 5.476,
     'ffn_ln_g': 2.894,
     'ffn_conv_b': 2.849,
     'g_mix_2': 4.929,
     'b_in_2': 6.929,
     'conv_rnn_b_2': 8.0,
     'b_rg_2': 61.268,
     'b_ig_2': 48.455,
     'g_ffn_2': 6.378,
     'conv_ffn_b_2': 33.894,
     'g_final_2': 7.986,
     'rel_bias_2': 3.173}
    for name, (base, spread) in spreads.items():
        noise = np.random.default_rng([zlib.crc32(name.encode()), seed]).standard_normal(out[name].shape)
        drawn = base * np.exp(spread * noise) if base else spread * noise
        out[name] = jnp.asarray(drawn.astype(out[name].dtype))
    for name, factor in factors.items():
        out[name] = (out[name] * factor).astype(out[name].dtype)
    return out
```

```python
from contextlib import ExitStack

import numpy as np

import concourse.bass as bass
from concourse import mybir

F32 = mybir.dt.float32
F32R = mybir.dt.float32r
ACT = mybir.ActivationFunctionType
ALU = mybir.AluOpType
AX = mybir.AxisListType

P = 128
D = 1024
T = 256
KD = D // P
DI = 2048
XBC = DI + 2 * 4 * 128
SSM_H = 32
FF = 2816
NF = FF // P
SLOT = 2048
RING = 3
LEAD = 2
PRING = 6
EPS = 1e-6
NEG = -1.0e30
TAKEN = -3.0e38
LAM_INIT = 0.8 - 0.6 * float(np.exp(-0.3 * 1))
TOPK = 64

VECS = [
    ("ssm_ln", 8), ("conv_w", 4 * 24), ("conv_b", 24), ("ssm_d", 16), ("ssm_norm", 16),
    ("kv_ln", 8), ("k_norm", 1), ("attn_ln", 8), ("q_norm", 1), ("subln", 1),
    ("ffn_ln0", 8), ("ffn_ln1", 8),
    ("up_w0", 3 * 44), ("up_b0", 44), ("up_w1", 3 * 44), ("up_b1", 44), ("up_w2", 3 * 44), ("up_b2", 44),
    ("b_ada", 48), ("g_mix", 8), ("b_q", 4), ("b_kk", 2), ("b_ki", 1), ("b_qi", 4),
    ("b_xr", 8), ("b_yr", 8), ("b_ga", 8), ("b_gb", 8),
    ("rnn_w", 4 * 8), ("rnn_b", 8), ("b_rg", 8), ("b_ig", 8), ("lru", 8), ("g_ffn", 8),
    ("g_final", 8), ("c", 8),
    ("dt_bias", 32), ("a_log", 32), ("b_wi", 8), ("b_v", 128),
]
VOFF = {}
_at = 0
for _name, _n in VECS:
    VOFF[_name] = _at
    _at += _n
NVEC = _at

TWO, ONE, FOUR, PAIR3 = "two", "one", "four", "pair3"


class Plan:

    def __init__(self):
        self.slabs, self.groups, self.halves, self.miscs = 0, 0, 0, 0
        self.S, self.G, self.H, self.M, self.N, self.kind = {}, {}, {}, {}, {}, {}
        self.size = []
        self.order = []

    def stream(self, name, n, kind, source=None):
        self.S[name], self.G[name], self.H[name], self.N[name], self.kind[name] = (
            self.slabs, self.groups, self.halves, n, kind)
        self.slabs += n
        self.order.append((name, n))
        if kind == TWO:
            self.groups += 2 * n
            self.halves += n
            self.size += [SLOT] * n
        elif kind == FOUR:
            self.groups += 4 * n
            self.halves += 3 * n
            self.size += [SLOT] * n
        elif kind == ONE:
            self.groups += n
            self.size += [SLOT] * n
        else:
            self.groups += 2 * (n // 3)
            self.halves += n // 3
            self.size += [SLOT, SLOT, 6 * 256] * (n // 3)

    def misc(self, name, n=1):
        self.G[name], self.M[name] = self.groups, self.miscs
        self.groups += n
        self.miscs += n

    def open(self, name):
        self.G[name] = self.groups
        self.groups += 1

    def close(self, name):
        self.M[name] = self.miscs
        self.miscs += 1


def make_plan():
    pl = Plan()
    pl.misc("n0")
    pl.misc("tz", 2)
    pl.misc("dt")
    pl.stream("xbc", 12, TWO)
    pl.misc("e12")
    pl.misc("cb", 4)
    for g in range(4):
        pl.misc(f"xt{g}", 2)
        pl.misc(f"sega{g}", 2)
        if g:
            pl.misc(f"gn{g-1}")
        pl.stream(f"za{g}", 1, TWO)
        pl.misc(f"y0{g}")
        pl.misc(f"segb{g}", 2)
        pl.misc(f"yo{g}")
        pl.stream(f"zb{g}", 1, TWO)
        pl.misc(f"y1{g}")
        pl.misc(f"yt{g}", 2)
    pl.misc("gn3")
    pl.stream("so", 8, ONE)
    pl.misc("n1")
    pl.stream("up0", NF, TWO)
    pl.stream("dn0", 12, PAIR3)
    pl.misc("n2")
    pl.stream("k", 4, TWO)
    pl.stream("v", 4, TWO)
    pl.misc("kss", 8)
    pl.stream("q", 4, TWO)
    pl.misc("qss", 8)
    for h in range(9):
        if h < 8:
            pl.misc(f"sc{h}", 2)
        if h >= 1:
            pl.misc(f"at{h-1}")
            pl.misc(f"pv{h-1}")
    pl.misc("os", 8)
    pl.stream("ao", 4, TWO)
    pl.misc("n3")
    pl.stream("up1", NF, TWO)
    pl.stream("dn1", 12, PAIR3)
    pl.misc("n4")
    pl.misc("wi")
    pl.stream("q2", 2, TWO)
    pl.stream("kk", 1, TWO)
    pl.stream("kiv", 1, TWO)
    pl.stream("qi", 2, TWO)
    pl.misc("ix", 8)
    pl.stream("yr", 4, TWO)
    for s in range(4):
        pl.stream(f"xr{s}", 1, TWO)
        if s:
            pl.misc(f"ri{s-1}", 4)
    pl.misc("ri3", 4)
    pl.stream("ga", 4, TWO)
    pl.stream("gb", 4, TWO)
    for h in range(9):
        if h < 8:
            pl.misc(f"lg{h}")
        if h >= 1:
            pl.misc(f"pt{h-1}")
            if (h - 1) % 2 == 0:
                pl.open(f"po{(h-1)//2}")
            else:
                pl.close(f"po{(h-1)//2}")
    pl.stream("woa", 2, FOUR)
    pl.stream("wor", 4, TWO)
    pl.stream("wout", 4, TWO)
    pl.misc("n5")
    pl.stream("up2", NF, TWO)
    pl.stream("dn2", 12, PAIR3)
    pl.misc("n6")
    return pl


PL = make_plan()
ADA = {**{f"z{half}{gr}": 1 for gr in range(4) for half in "ab"},
       "so": 8, "dn0": 12, "k": 4, "v": 4, "q": 4, "ao": 4, "dn1": 4}
assert sum(ADA.values()) == 48


def repeat(eng, n, stage, lag=0, rolled=True):
    full = n // RING
    if rolled and full >= 3:
        for s in range(RING):
            stage(0, s)
        with eng.Fori(1, full) as i:
            for j in range(RING):
                stage(i, j)
        for s in range(full * RING, n + lag):
            stage(s // RING, s % RING)
    else:
        for s in range(n + lag):
            stage(s // RING, s % RING)


def inside(i, j, back, n):
    return not isinstance(i, int) or 0 <= RING * i + j - back < n


def build_program(nc, io, out):
    with ExitStack() as ctx:
        def sb(name, shape, dt=F32):
            return ctx.enter_context(nc.sbuf_tensor(name, shape, dt))

        def sem(name):
            return ctx.enter_context(nc.semaphore(name))

        raw = sb("raw", [P, RING, SLOT])
        wwi = sb("wwi", [P, KD, 8])
        rel_sb = sb("rel_sb", [33, 2, 8])
        blk = sb("blk", [P, P])
        m8s = sb("m8s", [P, 2, 8])
        wh = sb("wh", [P, RING, SLOT], F32R)
        wl = sb("wl", [P, RING, SLOT], F32R)
        x = sb("x", [P, KD, T])
        xh = sb("xh", [P, KD, T], F32R)
        xl = sb("xl", [P, KD, T], F32R)
        actr = sb("actr", [P, 2 * NF * T], F32R)
        FN = 50 * 256
        work = sb("work", [P, FN])
        ada_w = sb("ada_w", [P, 2, 512])
        vecs = sb("vecs", [P, NVEC])
        ones = sb("ones", [P, P])
        ident = sb("ident", [P, P])
        tri = sb("tri", [P, 3, P])
        later = sb("later", [P, P])
        eps_t = sb("eps_t", [P, 1])
        small = sb("small", [P, 688])
        ps = ctx.enter_context(nc.psum_tensor("ps", [P, PRING, 512], F32))
        adaP = ctx.enter_context(nc.psum_tensor("adaP", [P, 64], F32))

        def vec(name, i=0, n=1):
            return vecs[:, VOFF[name] + i:VOFF[name] + i + n]

        def vdyn(name, i):
            return vecs[:, bass.ds(i + VOFF[name], 1)] if not isinstance(i, int) else vec(name, i)

        def W(off, *dims):
            n = int(np.prod(dims))
            assert off + n <= FN, (off, dims)
            a = work[:, off:off + n]
            if len(dims) == 2:
                a = a.rearrange("p (a b) -> p a b", b=dims[1])
            if len(dims) == 3:
                a = a.rearrange("p (a b c) -> p a b c", b=dims[1], c=dims[2])
            return a

        def R(off, a, b):
            return actr[:, off:off + a * b].rearrange("p (a b) -> p a b", b=b)

        KB = 256
        landed = [sem(f"landed{r}") for r in range(RING)]
        hi_done, lo_done = sem("hi_done"), sem("lo_done")
        slab_done, half_done = sem("slab_done"), sem("half_done")
        misc_done = sem("misc_done")
        free = [sem(f"free{r}") for r in range(PRING)]
        vecs_in, x_in, small_in = sem("vecs_in"), sem("x_in"), sem("small_in")
        ada_in = [sem("ada_in0"), sem("ada_in1")]
        ada_used = sem("ada_used")
        const_pool, const_done = sem("const_pool"), sem("const_done")
        sq_done, acc_done = sem("sq_done"), sem("acc_done")
        rstd_done, xn_done, xs_done = sem("rstd_done"), sem("xn_done"), sem("xs_done")
        xh_done, xl_done = sem("xh_done"), sem("xl_done")
        lam_in_sem, wri_in = sem("lam_in"), sem("wri_in")
        out_done = sem("out_done")
        (cact_done, ea_done, lam_done, sp_done, spe_done, tz_out, pre_done, conv_step, xbc_done, a_done,
         ysq_done, segl_done, decay_done, xdte_done, low_done, yh_done, yn_done, gated_done, grst_done,
         bt_in, gsil_done, h_done, hh_done, kq2_done, kqn_done, arst_done, vt_done, min_done,
         exp_done, attn_done, osq_done, on_done, oh_done, ol_done, wwi_in, qkv2_done, qkv2_done2,
         score_step, mask_done, xrraw_done, prer_done, xrc_done, lra_done, tanh_done, m2_done, mult_done,
         scan_done, rnn_done, rh_done, rl_done, min2_done, exp2_done, attn2_done, ah_done, al_done,
         merged_done, mh_done, ml_done) = [sem(n) for n in (
            "cact_done ea_done lam_done sp_done spe_done tz_out pre_done conv_step xbc_done a_done "
            "ysq_done segl_done decay_done xdte_done low_done yh_done yn_done gated_done grst_done "
            "bt_in gsil_done h_done hh_done kq2_done kqn_done arst_done vt_done min_done "
            "exp_done attn_done osq_done on_done oh_done ol_done wwi_in qkv2_done qkv2_done2 "
            "score_step mask_done xrraw_done prer_done xrc_done lra_done tanh_done m2_done mult_done "
            "scan_done rnn_done rh_done rl_done min2_done exp2_done attn2_done ah_done al_done "
            "merged_done mh_done ml_done").split()]
        ytok_done = [sem("ytok0_done"), sem("ytok1_done")]
        dve_step, act_step, pool_step = sem("dve_step"), sem("act_step"), sem("pool_step")

        class Steps:

            def __init__(self, eng, s):
                self.eng, self.s, self.n = eng, s, 0

            def add(self, ins):
                self.n += 1
                ins.then_inc(self.s, 1)
                return self.n

            def wait(self, n=None):
                self.eng.wait_ge(self.s, self.n if n is None else n)

        def bank(g):
            return ps[:, g % PRING, :]

        def acquire(eng, g0, i=0):
            if not (isinstance(i, int) and g0 // PRING + i == 0):
                eng.wait_ge(free[g0 % PRING], g0 // PRING + i)

        def given_back(eng, g0, i=0):
            eng.wait_ge(free[g0 % PRING], g0 // PRING + i + 1)

        def give_back(ins, g0):
            ins.then_inc(free[g0 % PRING], 1)

        def wait_misc(eng, name, n=0):
            eng.wait_ge(misc_done, PL.M[name] + n + 1)

        def wait_tile(eng, name, i, j, t, tiles=2):
            if t == tiles - 1:
                eng.wait_ge(slab_done, PL.S[name] + RING * i + j + 1)
            else:
                eng.wait_ge(half_done, PL.H[name] + (tiles - 1) * (RING * i + j) + t + 1)

        def tile_group(name, j, t, tiles=2):
            return PL.G[name] + tiles * j + t

        total = PL.slabs

        def split_hi(act, b, i=0):
            if isinstance(i, int) and b + RING * i >= total:
                return
            n = PL.size[b + (RING * i if isinstance(i, int) else RING)]
            act.wait_ge(landed[b % RING], 16 * (b // RING + i + 1))
            if not isinstance(i, int) or b + RING * i >= RING:
                act.wait_ge(slab_done, b + RING * i - RING + 1)
            nc.scalar.activation(wh[:, b % RING, 0:n], raw[:, b % RING, 0:n], ACT.Copy).then_inc(hi_done, 1)

        def split_lo(dve, b, i=0):
            if isinstance(i, int) and b + RING * i >= total:
                return
            n = PL.size[b + (RING * i if isinstance(i, int) else RING)]
            dve.wait_ge(hi_done, b + RING * i + 1)
            nc.vector.tensor_tensor(wl[:, b % RING, 0:n], raw[:, b % RING, 0:n],
                                    wh[:, b % RING, 0:n].bitcast(F32), ALU.subtract).then_inc(lo_done, 1)

        xn = W(0, KD, T)
        sq = W(8 * KB, 2, T)
        acc = W(10 * KB, T)
        rms = W(11 * KB, T)
        rstd = W(12 * KB, T)
        onehot = W(19 * KB, 384)
        wdt = W(21 * KB, KD, 32)
        lam_in = W(22 * KB, 4, 64)
        pre = W(13 * KB, 6, T)
        gsil = W(19 * KB, 3, T)
        hbuf = W(22 * KB, 3, T)
        hh, hl = R(0, NF, T), R(NF * T, NF, T)
        bvr = W(47 * KB, 2, 384)
        xbc = W(26 * KB, 24, T)
        cbm = W(0, 4, 384)
        xdte = W(6 * KB, 512)
        yoffs = W(8 * KB, 512)
        zs = W(13 * KB, 4, T)
        ynr = W(17 * KB, 2, T)
        xdt = W(19 * KB, 2, 512)
        segl = W(42 * KB, 8, P)
        decay = W(46 * KB, 2, 512)
        ytok = [W(23 * KB, 512), W(10 * KB, 512)]
        grms, grst = W(12 * KB, T), W(25 * KB, T)
        yh, yl = R(0, 16, T), R(16 * T, 16, T)
        kf, qf = W(13 * KB, 8, T), W(21 * KB, 8, T)
        vt = W(29 * KB, 2, 1024)
        bt = W(37 * KB, 8, T)
        kq2 = W(0, 8, T)
        arms, arst = W(45 * KB, 2, T), W(47 * KB, 2, T)
        logit = W(0, 4, 384)
        At = W(6 * KB, 2, 384)
        ATt = W(9 * KB, 2, 384)
        onr = W(0, 2, T)
        x2h, x2l = R(0, 8, T), R(8 * T, 8, T)
        oh, ol = R(16 * T, 8, T), R(24 * T, 8, T)
        q2f = W(13 * KB, 4, T)
        kkf = W(17 * KB, 2, T)
        kif = W(19 * KB, T)
        v2t = W(20 * KB, 2, P)
        qif = W(21 * KB, 4, T)
        score = W(25 * KB, 2, 384)
        mneg = W(28 * KB, T)
        rel = W(29 * KB, 2, 384)
        selb = W(32 * KB, 384)
        gyr = W(34 * KB, 8, T)
        bt2 = W(42 * KB, 8, T)
        wri = W(0, 2, 1024)
        gaf, gbf = W(0, 8, T), W(34 * KB, 8, T)
        xrraw = W(21 * KB, 2, T)
        xrc = W(42 * KB, 4, T)
        rg = W(8 * KB, 2, T)
        ig = W(10 * KB, 2, T)
        lra = W(29 * KB, 2, T)
        lrm = W(23 * KB, 2, T)
        lrh = W(26 * KB, 2, T)
        logit2 = W(8 * KB, 2, 384)
        At2 = W(26 * KB, 2, 384)
        ATt2 = W(22 * KB, 2, 384)
        rh, rl = R(0, 8, T), R(8 * T, 8, T)
        ah, al = R(16 * T, 4, T), R(20 * T, 4, T)
        mh, ml = R(24 * T, 8, T), R(32 * T, 8, T)
        taken = [0]

        def S(*dims):
            n = int(np.prod(dims))
            a = small[:, taken[0]:taken[0] + n]
            taken[0] += n
            return a.rearrange("p (a b) -> p a b", b=dims[1]) if len(dims) == 2 else a

        dt_t, a_t, sp1, sp2, sp3, sp4 = S(2, 32), S(2, 32), S(64), S(64), S(64), S(64)
        e12, ea = S(64), S(32)
        lam2, lam4, negl, sgs = S(2), S(2), S(1), S(1)
        mod, gs1, gs2, cact = S(48), S(8), S(8), S(8)
        negc, posc = S(8), S(8)
        lp1, lp2, lp3, lp4, lpa = S(8), S(8), S(8), S(8), S(8)
        wi_s = S(2, 8)
        m8 = S(8)
        mins, sums, recs, coef = S(2, 4), S(2, 4), S(2, 4), S(2, 2)
        scratch = nc.dram_tensor("bias_by_distance", (2, 8, P, 384), F32, kind="Internal")
        toeplitz = [bass.AP(scratch, 8 * P * 384 * b_ + 127, [[383, P], [P * 384, 8], [1, T]]) for b_ in range(2)]
        scratch = scratch.ap()

        def sources():
            out_ = []
            for name, n in PL.order:
                key, at = (name[:2], int(name[2:])) if name[:2] in ("za", "zb", "xr") else (name, 0)
                if key in ("za", "zb"):
                    key, at = "z", 2 * at + (key == "zb")
                out_.append((name, n, key, at))
            return out_

        block = ctx.enter_context(nc.Block())

        @block.sync
        def _(sp):
            sp.dma_start(x[:, :, :], io["x"]).then_inc(x_in, 16)
            sp.dma_start(vecs[:, :], io["vecs"]).then_inc(vecs_in, 16)
            sp.dma_start(wdt, io["w_dt"]).then_inc(small_in, 16)
            sp.dma_start(rel_sb[:, :, :], io["rel"]).then_inc(small_in, 16)
            sp.dma_start(onehot[0:33, :], io["onehot"]).then_inc(small_in, 16)
            sp.dma_start(lam_in, io["lam"]).then_inc(lam_in_sem, 16)
            sp.dma_start(wwi[:, :, :], io["w_wi"]).then_inc(wwi_in, 16)
            for name, n, key, at in sources():
                base = PL.S[name]

                def load(i, j):
                    b = base + j
                    if not isinstance(i, int) or b + RING * i >= RING:
                        sp.wait_ge(lo_done, b + RING * i - RING + 1)
                    s = RING * i + j
                    if PL.kind[name] == PAIR3:
                        src = io[key + "a"][2 * i + j] if j < 2 else io[key + "b"][i]
                    else:
                        src = io[key][s + at]
                    sp.dma_start(raw[:, b % RING, 0:src.shape[-1]], src).then_inc(landed[b % RING], 16)

                if PL.kind[name] == PAIR3:
                    for s in range(n):
                        load(s // RING, s % RING)
                else:
                    repeat(sp, n, load)
            sp.wait_ge(xn_done, 8 * 8)
            sp.dma_start(out, xn[:, :, :]).then_inc(out_done, 16)
            sp.wait_ge(out_done, 16)

        LOW0 = 16
        NCONST = 6

        @block.gpsimd
        def _(pool):
            step = Steps(pool, pool_step)
            step.add(nc.gpsimd.memset(ones[:, :], 1.0))
            step.add(nc.gpsimd.memset(tri[:, :, :], 1.0))
            step.add(nc.gpsimd.memset(ident[:, :], 0.0))
            step.add(nc.gpsimd.memset(blk[:, :], 0.0))
            step.add(nc.gpsimd.memset(eps_t[:, :], EPS))
            step.wait()
            for c in (0, 2):
                nc.gpsimd.affine_select(out=tri[:, c, :], in_=ones[:, :], pattern=[[1, P]], compare_op=ALU.is_ge,
                                        fill=0.0, base=0, channel_multiplier=-1).then_inc(const_done, 1)
            nc.gpsimd.affine_select(out=later[:, :], in_=ones[:, :], pattern=[[-1, P]], compare_op=ALU.is_ge,
                                    fill=0.0, base=-1, channel_multiplier=1).then_inc(const_done, 1)
            nc.gpsimd.affine_select(out=ident[:, :], in_=ident[:, :], pattern=[[-1, P]], compare_op=ALU.not_equal,
                                    fill=1.0, base=0, channel_multiplier=1).then_inc(const_done, 1)
            pool.wait_ge(const_done, NCONST - 2)
            nc.gpsimd.memset(blk[0:64, 0:64], 1.0).then_inc(const_done, 1)
            nc.gpsimd.memset(blk[64:128, 64:128], 1.0).then_inc(const_done, 1)
            for a in range(96):
                if a >= 2:
                    pool.wait_ge(ada_used, a - 1)
                pool.dma_start(ada_w[:, a % 2, :], io["w_ada"][a // 2][:, 512 * (a % 2):512 * (a % 2) + 512])\
                    .then_inc(ada_in[a % 2], 16)
            pool.wait_ge(acc_done, 7 * 5)
            step.add(nc.gpsimd.memset(mneg, 0.0))
            step.wait()
            nc.gpsimd.affine_select(out=mneg, in_=mneg, pattern=[[-1, T]], compare_op=ALU.is_ge,
                                    fill=NEG, base=P, channel_multiplier=1).then_inc(mask_done, 1)
            pool.wait_ge(xl_done, 8 * 6)
            wait_misc(pool, "wi")
            pool.dma_start(wri[:, 0, :], io["w_rg"]).then_inc(wri_in, 16)
            pool.dma_start(wri[:, 1, :], io["w_ig"]).then_inc(wri_in, 16)


        @block.tensor
        def _(pe):
            ada_n = [0]

            def ada(name, s):
                if s < ADA.get(name, 0):
                    n = ada_n[0]
                    ada_n[0] += 1
                    if n == 0:
                        pe.wait_ge(cact_done, 1)
                    for half in range(2):
                        pe.wait_ge(ada_in[half], 16 * (n + 1))
                        for k in range(4):
                            mm = nc.tensor.matmul(adaP[:, n:n + 1], ada_w[:, half, k * P:(k + 1) * P],
                                                  cact[:, 4 * half + k:4 * half + k + 1],
                                                  start=(half == 0 and k == 0), stop=(half == 1 and k == 3))
                        mm.then_inc(ada_used, 1)

            def mm3(o, w, xp, start, stop, tok):
                (w_h, w_l), (x_h, x_l) = w, xp
                for n, (a, b) in enumerate(((w_l, x_h), (w_h, x_l), (w_h, x_h))):
                    l, r = (b, a) if tok else (a, b)
                    mm = nc.tensor.matmul(o, l, r, start=start and n == 0, stop=stop and n == 2)
                return mm

            def stream(name, X, ready=None):
                n, kind = PL.N[name], PL.kind[name]
                base, g0 = PL.S[name], PL.G[name]
                tiles = {TWO: 2, ONE: 1, FOUR: 4, PAIR3: 2}[kind]
                kts = {TWO: 8, ONE: 16, FOUR: 4}.get(kind)

                def stage(i, j):
                    b = base + j
                    pe.wait_ge(lo_done, b + RING * i + 1)
                    r = b % RING
                    width = SLOT // kts if kind != PAIR3 else 256
                    for t in range(tiles):
                        first = isinstance(i, int) and i == 0 and j == 0 and t == 0
                        if kind == PAIR3:
                            g, gi = g0 + 2 * i + t, 0
                            if j == 0:
                                acquire(pe, g)
                            ks = range(8 * j, min(8 * j + 8, NF))
                            begin, end = j == 0, j == 2
                        else:
                            g, gi = g0 + tiles * j + t, i
                            if tiles * RING % PRING:
                                g, gi = g0 + tiles * (RING * i + j) + t, 0
                            acquire(pe, g, gi)
                            ks = range(kts)
                            begin = end = True
                        for k in ks:
                            if ready and (isinstance(i, int) and i == 0 and t == 0 and (first or kind == PAIR3)):
                                ready(k)
                            off = (k - ks[0]) * width + t * P
                            st, en = begin and k == ks[0], end and k == ks[-1]
                            wp = (wh[:, r, off:off + P], wl[:, r, off:off + P])
                            mm = mm3(bank(g)[:, 0:T], wp, (X[0][:, k, :], X[1][:, k, :]), st, en, False)
                        if t == tiles - 1:
                            mm.then_inc(slab_done, 1)
                        elif end:
                            mm.then_inc(half_done, 1)
                    if name in ADA:
                        ada(name, RING * i + j)

                repeat(pe, n, stage, rolled=kind == TWO)

            def stream_tok(name, X):
                for s in range(PL.N[name]):
                    b = PL.S[name] + s
                    pe.wait_ge(lo_done, b + 1)
                    r = b % RING
                    for t in range(2):
                        g = PL.G[name] + 2 * s + t
                        acquire(pe, g)
                        for k in range(KD):
                            mm = mm3(bank(g)[:, 0:256],
                                     (wh[:, r, k * 256:k * 256 + 256], wl[:, r, k * 256:k * 256 + 256]),
                                     (X[0][:, k, P * t:P * t + P], X[1][:, k, P * t:P * t + P]),
                                     k == 0, k == KD - 1, True)
                        mm.then_inc(half_done if t == 0 else slab_done, 1)
                    ada(name, s)

            def norm_sum(name, r):
                acquire(pe, PL.G[name])
                pe.wait_ge(acc_done, 7 * (r + 1))
                nc.tensor.matmul(bank(PL.G[name])[:, 0:T], ones[:, :], acc, start=True, stop=True)\
                    .then_inc(misc_done, 1)

            def x_ready(use):
                return lambda k: pe.wait_ge(xl_done, 8 * use + k + 1)

            pe.wait_ge(const_done, NCONST)
            norm_sum("n0", 0)
            pe.wait_ge(small_in, 48)
            for b_ in range(2):
                acquire(pe, PL.G["tz"] + b_)
                nc.tensor.matmul(bank(PL.G["tz"] + b_)[0:8, 0:384], rel_sb[0:33, b_, :], onehot[0:33, :],
                                 start=True, stop=True).then_inc(misc_done, 1)
            g = PL.G["dt"]
            acquire(pe, g)
            for c in range(2):
                for k in range(KD):
                    pe.wait_ge(xn_done, k + 1)
                    mm = nc.tensor.matmul(bank(g)[:, 32 * c:32 * c + 32], xn[:, k, P * c:P * c + P],
                                          wdt[:, k, :], start=(k == 0), stop=(k == KD - 1))
            mm.then_inc(misc_done, 1)
            stream("xbc", (xh, xl), x_ready(0))
            g = PL.G["e12"]
            acquire(pe, g)
            pe.wait_ge(a_done, 1)
            nc.tensor.matmul(bank(g)[:, 0:32], later[:, :], a_t[:, 0, :], start=True, stop=True)
            nc.tensor.matmul(bank(g)[:, 32:64], tri[:, 0, :], a_t[:, 1, :], start=True, stop=True)\
                .then_inc(misc_done, 1)
            pe.wait_ge(xbc_done, 24)
            for gr in range(4):
                g = PL.G["cb"] + gr
                acquire(pe, g)
                B, C = xbc[:, 16 + gr, :], xbc[:, 20 + gr, :]
                nc.tensor.matmul(bank(g)[:, 0:T], B[:, 0:P], C, start=True, stop=True)
                nc.tensor.matmul(bank(g)[:, T:384], B[:, P:T], C[:, P:T], start=True, stop=True)\
                    .then_inc(misc_done, 1)

            def group_norm_sum(gr):
                g = PL.G[f"gn{gr}"]
                acquire(pe, g)
                for t in range(4):
                    pe.wait_ge(ysq_done, 4 * gr + t + 1)
                    mm = nc.tensor.matmul(bank(g)[:, 0:T], ones[:, :], zs[:, t, :], start=(t == 0), stop=(t == 3))
                mm.then_inc(misc_done, 1)

            for gr in range(4):
                for c in range(2):
                    g = PL.G[f"xt{gr}"] + c
                    acquire(pe, g)
                    for t in range(4):
                        mm = nc.tensor.transpose(bank(g)[:, t * P:(t + 1) * P],
                                                 xbc[:, 4 * gr + t, c * P:(c + 1) * P], ident[:, :])
                    mm.then_inc(misc_done, 1)

                def segs(part):
                    for q in range(2):
                        g = PL.G[f"seg{part}{gr}"] + q
                        acquire(pe, g)
                        qq = 4 * gr + 2 * (part == "b") + q
                        pe.wait_ge(segl_done, 4 * (qq + 1))
                        for t in range(4):
                            mm = nc.tensor.matmul(bank(g)[:, t * P:(t + 1) * P], segl[:, 4 * (q % 2) + t, :],
                                                  tri[:, 0, :], start=True, stop=True)
                        mm.then_inc(misc_done, 1)

                def y_heads(c):
                    g = PL.G[f"y{c}{gr}"]
                    acquire(pe, g)
                    for q in range(2):
                        pe.wait_ge(decay_done, 4 * gr + 2 * c + q + 1)
                        for t in range(4):
                            h = 4 * q + t
                            mm = nc.tensor.matmul(bank(g)[:, 64 * h:64 * h + 64], decay[:, q, t * P:(t + 1) * P],
                                                  xdt[:, c, 64 * h:64 * h + 64], start=True, stop=True)
                    mm.then_inc(misc_done, 1)

                segs("a")
                if gr:
                    group_norm_sum(gr - 1)
                stream(f"za{gr}", (xh, xl))
                y_heads(0)
                segs("b")
                g = PL.G[f"yo{gr}"]
                acquire(pe, g)
                pe.wait_ge(xdte_done, gr + 1)
                nc.tensor.matmul(bank(g), cbm[:, gr, P:T], xdte, start=True, stop=True).then_inc(misc_done, 1)
                stream(f"zb{gr}", (xh, xl))
                y_heads(1)
                for c in range(2):
                    g = PL.G[f"yt{gr}"] + c
                    acquire(pe, g)
                    pe.wait_ge(ytok_done[c], gr + 1)
                    for t in range(4):
                        mm = nc.tensor.transpose(bank(g)[:, t * P:(t + 1) * P], ytok[c][:, t * P:(t + 1) * P],
                                                 ident[:, :])
                    mm.then_inc(misc_done, 1)
            group_norm_sum(3)
            stream("so", (yh, yl), lambda k: pe.wait_ge(low_done, k + 1))

            def ffn(f, norm, use, r):
                norm_sum(norm, r)
                stream(f"up{f}", (xh, xl), x_ready(use))
                stream(f"dn{f}", (hh, hl), lambda k: pe.wait_ge(low_done, LOW0 + NF * f + k + 1))

            ffn(0, "n1", 1, 1)
            norm_sum("n2", 2)
            stream("k", (xh, xl), x_ready(2))
            stream_tok("v", (xh, xl))

            def head_sums(name, n0):
                for h in range(8):
                    g = PL.G[name] + h
                    acquire(pe, g)
                    pe.wait_ge(kq2_done, n0 + h + 1)
                    nc.tensor.matmul(bank(g)[:, 0:T], blk[:, :], kq2[:, h, :], start=True, stop=True)\
                        .then_inc(misc_done, 1)

            head_sums("kss", 0)
            pe.wait_ge(xl_done, 8 * 4)
            stream("q", (x2h, x2l))
            head_sums("qss", 8)

            def transposes(name, A, done, n):
                g = PL.G[name]
                acquire(pe, g)
                pe.wait_ge(done, n)
                for t in range(3):
                    mm = nc.tensor.transpose(bank(g)[:, t * P:(t + 1) * P], A[:, t * P:(t + 1) * P], ident[:, :])
                mm.then_inc(misc_done, 1)

            for it in range(9):
                if it < 8:
                    for c in range(2):
                        g = PL.G[f"sc{it}"] + c
                        acquire(pe, g)
                        pe.wait_ge(kqn_done, 8 + it + 1)
                        rows = slice(64 * c, 64 * c + 64)
                        nc.tensor.matmul(bank(g)[:, 0:P], qf[rows, it, 0:P], kf[rows, it, 0:P], start=True, stop=True)
                        nc.tensor.matmul(bank(g)[:, P:384], qf[rows, it, P:T], kf[rows, it, :],
                                         start=True, stop=True).then_inc(misc_done, 1)
                if it >= 1:
                    h = it - 1
                    transposes(f"at{h}", At[:, h % 2, :], attn_done, h + 1)
                    g = PL.G[f"pv{h}"]
                    acquire(pe, g)
                    if h == 0:
                        pe.wait_ge(vt_done, 8)
                    given_back(pe, PL.G[f"at{h}"])
                    nc.tensor.matmul(bank(g)[:, 0:T], vt[:, 0, P * h:P * h + P], ATt[:, h % 2, 0:T],
                                     start=True, stop=False)
                    nc.tensor.matmul(bank(g)[:, P:T], vt[:, 1, P * h:P * h + P], ATt[:, h % 2, T:384],
                                     start=False, stop=True).then_inc(misc_done, 1)
            for h in range(8):
                g = PL.G["os"] + h
                acquire(pe, g)
                pe.wait_ge(osq_done, h + 1)
                nc.tensor.matmul(bank(g)[:, 0:T], ones[:, :], kf[:, h, :], start=True, stop=True).then_inc(misc_done, 1)
            stream("ao", (oh, ol), lambda k: pe.wait_ge(ol_done, k + 1))
            ffn(1, "n3", 4, 3)
            norm_sum("n4", 4)
            pe.wait_ge(wwi_in, 16)
            g = PL.G["wi"]
            acquire(pe, g)
            for c in range(2):
                for k in range(KD):
                    pe.wait_ge(xs_done, k + 1)
                    mm = nc.tensor.matmul(bank(g)[:, 8 * c:8 * c + 8], xn[:, k, P * c:P * c + P], wwi[:, k, :],
                                          start=(k == 0), stop=(k == KD - 1))
            mm.then_inc(misc_done, 1)
            stream("q2", (xh, xl), x_ready(5))
            stream("kk", (xh, xl))
            b, g = PL.S["kiv"], PL.G["kiv"]
            pe.wait_ge(lo_done, b + 1)
            acquire(pe, g)
            acquire(pe, g + 1)
            for k in range(KD):
                o = k * 256
                mm = mm3(bank(g)[:, 0:T], (wh[:, b % RING, o:o + P], wl[:, b % RING, o:o + P]),
                         (xh[:, k, :], xl[:, k, :]), k == 0, k == KD - 1, False)
            mm.then_inc(half_done, 1)
            for c in range(2):
                for k in range(KD):
                    o = k * 256 + P
                    mm = mm3(bank(g + 1)[:, P * c:P * c + P], (wh[:, b % RING, o:o + P], wl[:, b % RING, o:o + P]),
                             (xh[:, k, P * c:P * c + P], xl[:, k, P * c:P * c + P]), k == 0, k == KD - 1, True)
            mm.then_inc(slab_done, 1)
            stream("qi", (xh, xl))

            def dots(g, q_rows, k_rows):
                acquire(pe, g)
                nc.tensor.matmul(bank(g)[:, 0:P], q_rows[:, 0:P], k_rows[:, 0:P], start=True, stop=True)
                nc.tensor.matmul(bank(g)[:, P:384], q_rows[:, P:T], k_rows, start=True, stop=True)\
                    .then_inc(misc_done, 1)

            pe.wait_ge(qkv2_done, 11)
            for h in range(8):
                rows = slice(64 * (h % 2), 64 * (h % 2) + 64)
                dots(PL.G["ix"] + h, qif[rows, h // 2, :], kif[rows, :])
            stream("yr", (xh, xl))

            def gates(s):
                if s == 0:
                    pe.wait_ge(wri_in, 32)
                for w in range(2):
                    for t in range(2):
                        n = 2 * s + t
                        g = PL.G[f"ri{s}"] + 2 * w + t
                        acquire(pe, g)
                        pe.wait_ge(xrc_done, n + 1)
                        nc.tensor.matmul(bank(g)[:, 0:T], wri[:, w, n * P:(n + 1) * P], xrc[:, n % 4, :],
                                         start=True, stop=True).then_inc(misc_done, 1)

            for s in range(4):
                stream(f"xr{s}", (xh, xl))
                if s:
                    gates(s - 1)
            gates(3)
            stream("ga", (xh, xl))
            stream("gb", (xh, xl))
            for it in range(9):
                if it < 8:
                    rows = slice(64 * (it % 2), 64 * (it % 2) + 64)
                    dots(PL.G[f"lg{it}"], q2f[rows, it // 2, :], kkf[rows, it // 4, :])
                if it >= 1:
                    h = it - 1
                    transposes(f"pt{h}", At2[:, h % 2, :], attn2_done, h + 1)
                    g = PL.G[f"po{h//2}"]
                    if h % 2 == 0:
                        acquire(pe, g)
                    given_back(pe, PL.G[f"pt{h}"])
                    o = bank(g)[64 * (h % 2):64 * (h % 2) + 64, :]
                    kv = h // 4
                    nc.tensor.matmul(o[:, 0:T], v2t[:, 0, 64 * kv:64 * kv + 64], ATt2[:, h % 2, 0:T],
                                     start=True, stop=False)
                    mm = nc.tensor.matmul(o[:, P:T], v2t[:, 1, 64 * kv:64 * kv + 64], ATt2[:, h % 2, T:384],
                                          start=False, stop=True)
                    if h % 2:
                        mm.then_inc(misc_done, 1)
            stream("woa", (ah, al), lambda k: pe.wait_ge(al_done, k + 1))
            pe.wait_ge(rl_done, 8)
            stream("wor", (rh, rl))
            stream("wout", (mh, ml), lambda k: pe.wait_ge(ml_done, k + 1))
            ffn(2, "n5", 6, 5)
            norm_sum("n6", 6)

        @block.scalar
        def _(act):
            step = Steps(act, act_step)
            A = nc.scalar.activation

            def hi(name, s):
                split_hi(act, PL.S[name] + s + LEAD)

            def square(r, m, g=None):
                if g is None:
                    act.wait_ge(x_in, 16)
                else:
                    given_back(act, g)
                if m >= 2:
                    act.wait_ge(acc_done, 7 * r + max(1, m - 2))
                A(sq[:, m % 2, :], x[:, m, :], ACT.Square).then_inc(sq_done, 1)

            def norm(name, uses, shifts={}):
                g = PL.G[name]
                wait_misc(act, name)
                give_back(A(rms, bank(g)[:, 0:T], ACT.Sqrt, scale=1.0 / D, bias=eps_t[:, :]), g)
                for use in uses:
                    xo = (x2h if use == 3 else xh)
                    for m in range(KD):
                        act.wait_ge(xn_done, 8 * use + m + 1)
                        if use in shifts:
                            s0, n0 = shifts[use]
                            A(xn[:, m, :], xn[:, m, :], ACT.Identity, bias=mod[:, s0 + m:s0 + m + 1])\
                                .then_inc(xs_done, 1)
                            act.wait_ge(xs_done, n0 + m + 1)
                        A(xo[:, m, :], xn[:, m, :], ACT.Copy).then_inc(xh_done, 1)

            def residual(name, r, n, last_of):
                for s in range(n):
                    hi(name, s)
                    for m, g in last_of(s):
                        square(r, m, g)

            def tiles_two(name):
                return lambda s: [(2 * s + t, PL.G[name] + 2 * s + t) for t in range(2)]

            def tiles_pair3(name):
                return lambda s: [(2 * (s // 3) + t, PL.G[name] + 2 * (s // 3) + t) for t in range(2)] if s % 3 == 2 else []

            act.wait_ge(vecs_in, 16)
            act.wait_ge(const_done, NCONST)
            A(cact, vec("c", 0, 8), ACT.Silu).then_inc(cact_done, 1)
            for m in range(KD):
                square(0, m)
            split_hi(act, 0)
            split_hi(act, 1)
            A(ea, vec("a_log", 0, 32), ACT.Exp).then_inc(ea_done, 1)
            step.add(A(lpa, vec("lru", 0, 8), ACT.Abs))
            step.wait()
            A(lp2, lpa, ACT.Exp, scale=-1.0).then_inc(ea_done, 1)
            act.wait_ge(lam_done, 2)
            A(lam4, lam2, ACT.Exp).then_inc(ea_done, 1)
            norm("n0", [0])
            for b_ in range(2):
                wait_misc(act, "tz", b_)
                give_back(A(bvr[0:8, b_, :], bank(PL.G["tz"] + b_)[0:8, 0:384], ACT.Copy), PL.G["tz"] + b_)
            given_back(act, PL.G["tz"])
            given_back(act, PL.G["tz"] + 1)
            for b_ in range(2):
                act.dma_start(scratch[b_], bvr[0:8, b_, :].rearrange("h (a j) -> h a j", a=1).to_broadcast([8, P, 384]))\
                    .then_inc(tz_out, 16)
            given_back(act, PL.G["dt"])
            step.add(A(sp2, sp1, ACT.Abs))
            step.wait()
            A(sp3, sp2, ACT.Exp, scale=-1.0).then_inc(spe_done, 1)

            def xbc_stage(i, j):
                if inside(i, j, 0, 12):
                    split_hi(act, PL.S["xbc"] + j + LEAD, i)
                if inside(i, j, 1, 12):
                    for t in range(2):
                        given_back(act, tile_group("xbc", j - 1, t), i)
                        A(xbc[:, bass.ds(2 * (RING * i + j - 1) + t, 1), :] if not isinstance(i, int)
                          else xbc[:, 2 * (RING * i + j - 1) + t, :],
                          pre[:, 2 * ((j - 1) % RING) + t, :], ACT.Silu).then_inc(xbc_done, 1)
                if inside(i, j, 0, 12):
                    for t in range(2):
                        wait_tile(act, "xbc", i, j, t)
                        c = 2 * (RING * i + j) + t
                        A(pre[:, 2 * (j % RING) + t, :], bank(tile_group("xbc", j, t))[:, 0:T], ACT.Identity,
                          scale=vdyn("conv_w", 3 * 24 + c), bias=vdyn("conv_b", c)).then_inc(pre_done, 1)

            act.wait_ge(tz_out, 32)
            repeat(act, 12, xbc_stage, 1)
            g = PL.G["e12"]
            wait_misc(act, "e12")
            give_back(A(e12, bank(g)[:, 0:64], ACT.Exp), g)

            def exps(gr, part):
                for q in range(2):
                    g = PL.G[f"seg{part}{gr}"] + q
                    wait_misc(act, f"seg{part}{gr}", q)
                    if part == "b":
                        wait_misc(act, f"y0{gr}")
                    elif gr:
                        wait_misc(act, f"y1{gr-1}")
                    give_back(A(decay[:, q, :], bank(g), ACT.Exp), g)

            def group_norm(gr):
                g = PL.G[f"gn{gr}"]
                wait_misc(act, f"gn{gr}")
                give_back(A(grms, bank(g)[:, 0:T], ACT.Sqrt, scale=1.0 / 512, bias=eps_t[:, :]), g)
                for t in range(4):
                    act.wait_ge(yn_done, 4 * gr + t + 1)
                    A(yh[:, 4 * gr + t, :], ynr[:, t % 2, :], ACT.Copy).then_inc(yh_done, 1)

            def silu_z(name, gr, o):
                hi(name, 0)
                for t in range(2):
                    wait_tile(act, name, 0, 0, t)
                    give_back(A(zs[:, o + t, :], bank(PL.G[name] + t)[:, 0:T], ACT.Silu), PL.G[name] + t)

            for gr in range(4):
                exps(gr, "a")
                if gr:
                    group_norm(gr - 1)
                silu_z(f"za{gr}", gr, 0)
                g = PL.G[f"y0{gr}"]
                wait_misc(act, f"y0{gr}")
                A(ytok[0], bank(g), ACT.Copy).then_inc(ytok_done[0], 1)
                act.wait_ge(ytok_done[0], gr + 1)
                act.sem_inc(free[g % PRING], 1)
                exps(gr, "b")
                silu_z(f"zb{gr}", gr, 2)
                for t in range(4):
                    act.wait_ge(gated_done, 4 * gr + t + 1)
                    A(zs[:, t, :], xbc[:, 4 * gr + t, :], ACT.Square).then_inc(ysq_done, 1)
            group_norm(3)
            act.wait_ge(low_done, 16)
            act.dma_start(bt, toeplitz[0]).then_inc(bt_in, 16)
            residual("so", 1, 8, lambda s: [(s, PL.G["so"] + s)])

            def ffn(f, norm_name, uses, shifts, r):
                norm(norm_name, uses, shifts)
                up, dn = f"up{f}", f"dn{f}"

                def stage(i, j):
                    s = RING * i + j
                    if inside(i, j, 0, NF):
                        split_hi(act, PL.S[up] + j + LEAD, i)
                    if inside(i, j, 1, NF):
                        given_back(act, tile_group(up, j - 1, 0), i)
                        A(gsil[:, (j - 1) % RING, :], pre[:, 2 * ((j - 1) % RING), :], ACT.Silu)\
                            .then_inc(gsil_done, 1)
                    if inside(i, j, 2, NF):
                        act.wait_ge(h_done, NF * f + s - 1)
                        dst = hh[:, bass.ds(s - 2, 1), :] if not isinstance(i, int) else hh[:, s - 2, :]
                        A(dst, hbuf[:, (j - 2) % RING, :], ACT.Copy).then_inc(hh_done, 1)
                    if inside(i, j, 0, NF):
                        for t in range(2):
                            wait_tile(act, up, i, j, t)
                            A(pre[:, 2 * (j % RING) + t, :], bank(tile_group(up, j, t))[:, 0:T], ACT.Identity,
                              scale=vdyn(f"up_w{f}", 88 + 2 * s + t), bias=vdyn(f"up_b{f}", 2 * s + t))\
                                .then_inc(pre_done, 1)

                repeat(act, NF, stage, 2)
                residual(dn, r + 1, 12, tiles_pair3(dn))

            ffn(0, "n1", [1], {}, 1)
            norm("n2", [2, 3])
            act.wait_ge(xl_done, 8 * 4)

            def kq_tiles(name, dst):
                for s in range(4):
                    hi(name, s)
                    for t in range(2):
                        m, g = 2 * s + t, PL.G[name] + 2 * s + t
                        wait_tile(act, name, s // RING, s % RING, t)
                        A(kq2[:, m, :], bank(g)[:, 0:T], ACT.Square).then_inc(kq2_done, 1)
                        give_back(A(dst[:, m, :], bank(g)[:, 0:T], ACT.Copy), g)

            def head_norm(name, n0):
                for h in range(8):
                    g = PL.G[name] + h
                    wait_misc(act, name, h)
                    if n0 + h >= 2:
                        act.wait_ge(arst_done, n0 + h - 1)
                    give_back(A(arms[:, h % 2, :], bank(g)[:, 0:T], ACT.Sqrt, scale=1.0 / 64, bias=eps_t[:, :]), g)

            kq_tiles("k", kf)
            for s in range(4):
                hi("v", s)
                for t in range(2):
                    g = PL.G["v"] + 2 * s + t
                    wait_tile(act, "v", s // RING, s % RING, t)
                    A(vt[:, t, 256 * s:256 * s + 256], bank(g)[:, 0:256], ACT.Copy).then_inc(vt_done, 1)
                    act.wait_ge(vt_done, 2 * s + t + 1)
                    act.sem_inc(free[g % PRING], 1)
            head_norm("kss", 0)
            kq_tiles("q", qf)
            head_norm("qss", 8)

            def exp_rows(lg, q, row, n, sums_):
                for i in range(2):
                    cols = slice(0, P) if i == 0 else slice(P, 384)
                    A(lg[:, cols], lg[:, cols], ACT.Exp, scale=-1.0, bias=mins[:, q, row + i:row + i + 1],
                      accum_out=sums_[:, row + i:row + i + 1]).then_inc(n, 1)

            for it in range(9):
                if it < 8:
                    q = it % 2
                    for c in range(2):
                        act.wait_ge(min_done, 4 * it + 2 * c + 2)
                        exp_rows(logit[:, 2 * q + c, :], q, 2 * c, exp_done, sums[:, q, :])
                if it >= 1:
                    h = it - 1
                    g = PL.G[f"at{h}"]
                    wait_misc(act, f"at{h}")
                    give_back(A(ATt[:, h % 2, :], bank(g)[:, 0:384], ACT.Copy), g)
                    g = PL.G[f"pv{h}"]
                    wait_misc(act, f"pv{h}")
                    A(kf[:, h, :], bank(g)[:, 0:T], ACT.Square).then_inc(osq_done, 1)
                    give_back(A(qf[:, h, :], bank(g)[:, 0:T], ACT.Copy), g)
            for h in range(8):
                g = PL.G["os"] + h
                wait_misc(act, "os", h)
                act.wait_ge(arst_done, 16 + h - 1)
                give_back(A(arms[:, h % 2, :], bank(g)[:, 0:T], ACT.Sqrt, scale=1.0 / P, bias=eps_t[:, :]), g)
                if h:
                    act.wait_ge(on_done, h)
                    A(oh[:, h - 1, :], onr[:, (h - 1) % 2, :], ACT.Copy).then_inc(oh_done, 1)
            act.wait_ge(on_done, 8)
            A(oh[:, 7, :], onr[:, 1, :], ACT.Copy).then_inc(oh_done, 1)
            residual("ao", 3, 4, tiles_two("ao"))
            ffn(1, "n3", [4], {}, 3)
            norm("n4", [5], {5: (0, 0)})
            for name, n in (("q2", 2), ("kk", 1), ("kiv", 1), ("qi", 2)):
                for s in range(n):
                    hi(name, s)
                    for t in range(2):
                        m, g = 2 * s + t, PL.G[name] + 2 * s + t
                        wait_tile(act, name, 0, s, t)
                        if name == "kiv" and t == 1:
                            continue
                        dst = {"q2": q2f, "kk": kkf, "qi": qif}[name][:, m, :] if name != "kiv" else kif
                        bias = {"q2": "b_q", "kk": "b_kk", "qi": "b_qi", "kiv": "b_ki"}[name]
                        A(dst, bank(g)[:, 0:T], ACT.Identity, bias=vec(bias, m)).then_inc(qkv2_done, 1)
                        act.wait_ge(qkv2_done, {"q2": 0, "kk": 4, "kiv": 6, "qi": 7}[name] + m + 1)
                        act.sem_inc(free[g % PRING], 1)
            for h in range(8):
                g = PL.G["ix"] + h
                wait_misc(act, "ix", h)
                if h >= 2:
                    act.wait_ge(score_step, 2 * (h - 1))
                give_back(A(rel[:, h % 2, :], bank(g)[:, 0:384], ACT.Relu, scale=64 ** -0.5), g)
            for s in range(4):
                hi("yr", s)
                for t in range(2):
                    m, g = 2 * s + t, PL.G["yr"] + 2 * s + t
                    wait_tile(act, "yr", s // RING, s % RING, t)
                    give_back(A(gyr[:, m, :], bank(g)[:, 0:T], ACT.Gelu_apprx_tanh, bias=vec("b_yr", m)), g)

            def lru(s):
                for w in range(2):
                    for t in range(2):
                        g = PL.G[f"ri{s}"] + 2 * w + t
                        wait_misc(act, f"ri{s}", 2 * w + t)
                        if s:
                            act.wait_ge(scan_done, 2 * s)
                        dst, bias = ((rg, "b_rg"), (ig, "b_ig"))[w]
                        give_back(A(dst[:, t, :], bank(g)[:, 0:T], ACT.Sigmoid, bias=vec(bias, 2 * s + t)), g)
                for t in range(2):
                    n = 2 * s + t
                    given_back(act, PL.G[f"ri{s}"] + t)
                    A(lra[:, t, :], rg[:, t, :], ACT.Exp, scale=negc[:, n:n + 1]).then_inc(lra_done, 1)
                    A(rg[:, t, :], rg[:, t, :], ACT.Tanh, scale=posc[:, n:n + 1]).then_inc(tanh_done, 1)
                for t in range(2):
                    act.wait_ge(m2_done, 2 * s + t + 1)
                    A(lrm[:, t, :], lrm[:, t, :], ACT.Sqrt).then_inc(mult_done, 1)
                for t in range(2):
                    act.wait_ge(rnn_done, 2 * s + t + 1)
                    A(rh[:, 2 * s + t, :], lrh[:, t, :], ACT.Copy).then_inc(rh_done, 1)

            for s in range(4):
                name = f"xr{s}"
                hi(name, 0)
                for t in range(2):
                    n = 2 * s + t
                    g = PL.G[name] + t
                    wait_tile(act, name, 0, 0, t)
                    if s:
                        act.wait_ge(xrc_done, 2 * s)
                    A(xrraw[:, t, :], bank(g)[:, 0:T], ACT.Identity, bias=vec("b_xr", n)).then_inc(xrraw_done, 1)
                    act.wait_ge(xrraw_done, n + 1)
                    act.sem_inc(free[g % PRING], 1)
                    A(xrc[:, n % 4, :], xrraw[:, t, :], ACT.Identity, scale=vec("rnn_w", 24 + n),
                      bias=vec("rnn_b", n)).then_inc(prer_done, 1)
                if s:
                    lru(s - 1)
            lru(3)
            act.dma_start(bt2, toeplitz[1]).then_inc(bt_in, 16)
            for name, dst, bias in (("ga", gaf, "b_ga"), ("gb", gbf, "b_gb")):
                for s in range(4):
                    hi(name, s)
                    for t in range(2):
                        m, g = 2 * s + t, PL.G[name] + 2 * s + t
                        wait_tile(act, name, s // RING, s % RING, t)
                        give_back(A(dst[:, m, :], bank(g)[:, 0:T], ACT.Sigmoid, bias=vec(bias, m)), g)
            for it in range(9):
                if it < 8:
                    q = it % 2
                    act.wait_ge(min2_done, 2 * it + 2)
                    exp_rows(logit2[:, q, :], q, 0, exp2_done, sums[:, q, :])
                if it >= 1:
                    h = it - 1
                    g = PL.G[f"pt{h}"]
                    wait_misc(act, f"pt{h}")
                    give_back(A(ATt2[:, h % 2, :], bank(g)[:, 0:384], ACT.Copy), g)
                    if h % 2:
                        wait_misc(act, f"po{h//2}")
                        A(ah[:, h // 2, :], bank(PL.G[f"po{h//2}"])[:, 0:T], ACT.Copy).then_inc(ah_done, 1)
            for s in range(2):
                hi("woa", s)
            for s in range(4):
                hi("wor", s)
                for t in range(2):
                    m = 2 * s + t
                    act.wait_ge(merged_done, m + 1)
                    A(mh[:, m, :], gaf[:, m, :], ACT.Copy).then_inc(mh_done, 1)
            residual("wout", 5, 4, tiles_two("wout"))
            ffn(2, "n5", [6], {6: (24, 8)}, 5)
            norm("n6", [])

        @block.vector
        def _(dve):
            step = Steps(dve, dve_step)
            V = nc.vector

            def lo(name, s):
                split_lo(dve, PL.S[name] + s + LEAD)

            def accumulate(r, m):
                if m == 0:
                    return
                dve.wait_ge(sq_done, 8 * r + m + 1)
                if m == 1:
                    V.tensor_tensor(acc, sq[:, 0, :], sq[:, 1, :], ALU.add).then_inc(acc_done, 1)
                else:
                    dve.wait_ge(acc_done, 7 * r + m - 1)
                    V.tensor_tensor(acc, acc, sq[:, m % 2, :], ALU.add).then_inc(acc_done, 1)

            def norm(name, use_gains, k):
                g = PL.G[name]
                given_back(dve, g)
                V.reciprocal(rstd, rms).then_inc(rstd_done, 1)
                dve.wait_ge(rstd_done, k + 1)
                for use, gain, shift in use_gains:
                    h_, l_ = (x2h, x2l) if use == 3 else (xh, xl)

                    def low(m):
                        dve.wait_ge(xh_done, 8 * use + m + 1)
                        V.tensor_tensor(l_[:, m, :], xn[:, m, :], h_[:, m, :].bitcast(F32), ALU.subtract)\
                            .then_inc(xl_done, 1)

                    for m in range(KD):
                        if use == 3:
                            dve.wait_ge(xl_done, 8 * 2 + m + 1)
                        V.scalar_tensor_tensor(xn[:, m, :], x[:, m, :], gain(m), rstd, ALU.mult, ALU.mult)\
                            .then_inc(xn_done, 1)
                        if m and use < 7:
                            low(m - 1)
                    if use < 7:
                        low(KD - 1)

            def residual(name, r, n, tiles, scale=None):
                for s in range(n):
                    lo(name, s)
                    for m, g, t, cnt in tiles(s):
                        wait_tile(dve, name, s // RING, s % RING, t, cnt)
                        if scale is None:
                            ins = V.tensor_tensor(x[:, m, :], bank(g)[:, 0:T], x[:, m, :], ALU.add)
                        else:
                            ins = V.scalar_tensor_tensor(x[:, m, :], bank(g)[:, 0:T], scale(m), x[:, m, :],
                                                         ALU.mult, ALU.add)
                        give_back(ins, g)
                        if m:
                            accumulate(r, m - 1)
                accumulate(r, 7)

            def tiles_two(name):
                return lambda s: [(2 * s + t, PL.G[name] + 2 * s + t, t, 2) for t in range(2)]

            def residual3(name, r, scale=None):
                for s in range(12):
                    lo(name, s)
                    if s % 3 == 2:
                        p = s // 3
                        for t in range(2):
                            m, g = 2 * p + t, PL.G[name] + 2 * p + t
                            if t:
                                dve.wait_ge(slab_done, PL.S[name] + s + 1)
                            else:
                                dve.wait_ge(half_done, PL.H[name] + p + 1)
                            if scale is None:
                                ins = V.tensor_tensor(x[:, m, :], bank(g)[:, 0:T], x[:, m, :], ALU.add)
                            else:
                                ins = V.scalar_tensor_tensor(x[:, m, :], bank(g)[:, 0:T], scale(m), x[:, m, :],
                                                             ALU.mult, ALU.add)
                            give_back(ins, g)
                            if m:
                                accumulate(r, m - 1)
                accumulate(r, 7)

            def softplus(v, e, w, w2, p):
                step.add(V.tensor_scalar(w, e, 2.0, None, ALU.add))
                step.wait()
                step.add(V.reciprocal(w2, w))
                step.wait()
                step.add(V.tensor_tensor(w, e, w2, ALU.mult))
                step.wait()
                step.add(V.tensor_tensor(w2, w, w, ALU.mult))
                step.wait()
                step.add(V.tensor_scalar(p, w2, 1.0 / 15, None, ALU.mult))
                for n in (13, 11, 9, 7, 5, 3):
                    step.wait()
                    step.add(V.scalar_tensor_tensor(p, p, 1.0 / n, w2, ALU.add, ALU.mult))
                step.wait()
                step.add(V.scalar_tensor_tensor(p, p, 1.0, w, ALU.add, ALU.mult))
                step.add(V.tensor_scalar(e, v, 0.0, None, ALU.max))
                step.wait()
                step.add(V.scalar_tensor_tensor(e, p, 2.0, e, ALU.mult, ALU.add))
                step.wait()

            dve.wait_ge(vecs_in, 16)
            lamv = lam_in
            dve.wait_ge(lam_in_sem, 16)
            for c in range(2):
                step.add(V.tensor_tensor(ytok[0][:, 64 * c:64 * c + 64], lamv[:, 2 * c, :], lamv[:, 2 * c + 1, :],
                                         ALU.mult))
            step.wait()
            for c in range(2):
                V.tensor_reduce(lam2[:, c:c + 1], ytok[0][:, 64 * c:64 * c + 64], AX.X, ALU.add).then_inc(lam_done, 1)
            for m in range(KD):
                accumulate(0, m)
            split_lo(dve, 0)
            split_lo(dve, 1)
            step.add(V.tensor_scalar(lp1, vec("lru", 0, 8), -1.0, None, ALU.mult))
            dve.wait_ge(ea_done, 2)
            step.wait()
            softplus(lp1, lp2, lp3, lp4, posc)
            step.add(V.tensor_scalar(negc, lp2, -8.0, None, ALU.mult))
            step.add(V.tensor_scalar(posc, lp2, 8.0, None, ALU.mult))
            dve.wait_ge(ea_done, 3)
            step.add(V.tensor_tensor(negl, lam4[:, 1:2], lam4[:, 0:1], ALU.subtract))
            step.wait()
            step.add(V.tensor_scalar(negl, negl, -LAM_INIT, None, ALU.add))
            step.add(V.tensor_scalar(sgs, vec("subln"), 1.0 - LAM_INIT, None, ALU.mult))
            norm("n0", [(0, lambda m: vec("ssm_ln", m), None)], 0)
            g = PL.G["dt"]
            wait_misc(dve, "dt")
            give_back(V.tensor_tensor(sp1.rearrange("p (c h) -> p c h", c=2),
                                      bank(g)[:, 0:64].rearrange("p (c h) -> p c h", c=2),
                                      vec("dt_bias", 0, 32).rearrange("p (c h) -> p c h", c=1).to_broadcast([P, 2, 32]),
                                      ALU.add), g)
            given_back(dve, g)
            dve.wait_ge(spe_done, 1)
            softplus(sp1, sp3, sp2, sp4, dt_t.rearrange("p c h -> p (c h)"))
            step.add(V.tensor_copy(dt_t.rearrange("p c h -> p (c h)"), sp3))
            dve.wait_ge(ea_done, 1)
            step.wait()
            V.scalar_tensor_tensor(a_t, dt_t, -1.0, ea.rearrange("p (c h) -> p c h", c=1).to_broadcast([P, 2, 32]),
                                   ALU.mult, ALU.mult).then_inc(a_done, 1)

            def tap(dst, src, w, d):
                return V.scalar_tensor_tensor(dst[:, d:T], src[:, 0:T - d], w, dst[:, d:T], ALU.mult, ALU.add)

            def xbc_stage(i, j):
                split_lo(dve, PL.S["xbc"] + j + LEAD, i)
                s = RING * i + j
                for d in (1, 2, 3):
                    for t in range(2):
                        dst = pre[:, 2 * (j % RING) + t, :]
                        src = bank(tile_group("xbc", j, t))
                        if d == 1:
                            dve.wait_ge(pre_done, 2 * s + t + 1)
                        else:
                            dve.wait_ge(conv_step, 4 * s + 2 * (d - 2) + t + 1)
                        ins = tap(dst, src, vdyn("conv_w", 24 * (3 - d) + 2 * s + t), d)
                        if d == 3:
                            give_back(ins, tile_group("xbc", j, t))
                        else:
                            ins.then_inc(conv_step, 1)

            repeat(dve, 12, xbc_stage)
            for gr in range(4):
                g = PL.G["cb"] + gr
                wait_misc(dve, "cb", gr)
                give_back(V.tensor_tensor(cbm[:, gr, :], bank(g)[:, 0:384],
                                          tri[:, :, :].rearrange("p a b -> p (a b)"), ALU.mult), g)
            for gr in range(4):
                given_back(dve, PL.G["cb"] + gr)

            def heads(a):
                return a.rearrange("p (h c) -> p h c", c=64)

            def over(v):
                return v.rearrange("p (h c) -> p h c", c=1).to_broadcast([P, 8, 64])

            def group_norm(gr):
                given_back(dve, PL.G[f"gn{gr}"])
                V.reciprocal(grst, grms).then_inc(grst_done, 1)
                dve.wait_ge(grst_done, gr + 1)

                def low(t):
                    m = 4 * gr + t
                    dve.wait_ge(yh_done, m + 1)
                    V.tensor_tensor(yl[:, m, :], ynr[:, t % 2, :], yh[:, m, :].bitcast(F32), ALU.subtract)\
                        .then_inc(low_done, 1)

                for t in range(4):
                    m = 4 * gr + t
                    if m >= 2:
                        dve.wait_ge(low_done, m - 1)
                    V.scalar_tensor_tensor(ynr[:, t % 2, :], xbc[:, m, :], vec("ssm_norm", m), grst,
                                           ALU.mult, ALU.mult).then_inc(yn_done, 1)
                    if t:
                        low(t - 1)
                low(3)

            def seg_weights(gr, c):
                for q in range(2):
                    if c or gr:
                        wait_misc(dve, f"sega{gr}" if c else f"segb{gr-1}", q)
                    for t in range(4):
                        h = 8 * gr + 4 * q + t
                        V.tensor_scalar(segl[:, 4 * q + t, :], later[:, :], a_t[:, c, h:h + 1], None, ALU.mult)\
                            .then_inc(segl_done, 1)

            def decays(gr, c):
                for q in range(2):
                    given_back(dve, PL.G[f"seg{'ab'[c]}{gr}"] + q)
                    m = cbm[:, gr, 2 * P * c:2 * P * c + P].rearrange("p (a b) -> p a b", a=1).to_broadcast([P, 4, P])
                    d4 = decay[:, q, :].rearrange("p (a b) -> p a b", a=4)
                    V.tensor_tensor(d4, d4, m, ALU.mult).then_inc(decay_done, 1)

            dve.wait_ge(a_done, 1)
            given_back(dve, PL.G["e12"])
            for gr in range(4):
                for c in range(2):
                    g = PL.G[f"xt{gr}"] + c
                    wait_misc(dve, f"xt{gr}", c)
                    give_back(V.tensor_tensor(heads(xdt[:, c, :]), heads(bank(g)), over(dt_t[:, c, 8 * gr:8 * gr + 8]),
                                              ALU.mult), g)
                given_back(dve, PL.G[f"xt{gr}"])
                V.tensor_tensor(heads(xdte), heads(xdt[:, 0, :]), over(e12[:, 8 * gr:8 * gr + 8]), ALU.mult)\
                    .then_inc(xdte_done, 1)
                seg_weights(gr, 0)
                if gr:
                    group_norm(gr - 1)
                lo(f"za{gr}", 0)
                decays(gr, 0)
                seg_weights(gr, 1)
                g = PL.G[f"yo{gr}"]
                decays(gr, 1)
                wait_misc(dve, f"yo{gr}")
                give_back(V.tensor_tensor(heads(yoffs), heads(bank(g)), over(e12[:, 32 + 8 * gr:40 + 8 * gr]),
                                          ALU.mult), g)
                lo(f"zb{gr}", 0)
                given_back(dve, g)
                g = PL.G[f"y1{gr}"]
                wait_misc(dve, f"y1{gr}")
                V.tensor_tensor(ytok[1], bank(g), yoffs, ALU.add).then_inc(ytok_done[1], 1)
                dve.wait_ge(ytok_done[1], gr + 1)
                dve.sem_inc(free[g % PRING], 1)
                for c in range(2):
                    g = PL.G[f"yt{gr}"] + c
                    wait_misc(dve, f"yt{gr}", c)
                    for t in range(4):
                        m = 4 * gr + t
                        y_ = xbc[:, m, c * P:(c + 1) * P]
                        ins = V.scalar_tensor_tensor(y_, y_, vec("ssm_d", m), bank(g)[:, t * P:(t + 1) * P],
                                                     ALU.mult, ALU.add)
                        if t == 3:
                            give_back(ins, g)
                        else:
                            step.add(ins)
                step.wait()
                for c in range(2):
                    given_back(dve, PL.G[f"yt{gr}"] + c)
                for t in range(4):
                    given_back(dve, PL.G[f"z{'aabb'[t]}{gr}"] + t % 2)
                    V.tensor_tensor(xbc[:, 4 * gr + t, :], xbc[:, 4 * gr + t, :], zs[:, t, :], ALU.mult)\
                        .then_inc(gated_done, 1)
            dve.wait_ge(gated_done, 16)
            group_norm(3)
            residual("so", 1, 8, lambda s: [(s, PL.G["so"] + s, 0, 1)])

            def ffn(f, norm_args, r, scale=None):
                norm(*norm_args)
                up, dn = f"up{f}", f"dn{f}"
                pre0 = 24 + 44 * f
                cs0 = 4 * 12 + 2 * NF * f

                def stage(i, j):
                    s = RING * i + j
                    if inside(i, j, 0, NF):
                        split_lo(dve, PL.S[up] + j + LEAD, i)
                    if inside(i, j, 1, NF):
                        dve.wait_ge(gsil_done, NF * f + s)
                        given_back(dve, tile_group(up, j - 1, 1), i)
                        if not isinstance(i, int) or s >= 4:
                            dve.wait_ge(low_done, LOW0 + NF * f + s - 3)
                        V.tensor_tensor(hbuf[:, (j - 1) % RING, :], gsil[:, (j - 1) % RING, :],
                                        pre[:, 2 * ((j - 1) % RING) + 1, :], ALU.mult).then_inc(h_done, 1)
                    if inside(i, j, 2, NF):
                        dve.wait_ge(hh_done, NF * f + s - 1)
                        at = s - 2
                        dst = hl[:, bass.ds(at, 1), :] if not isinstance(i, int) else hl[:, at, :]
                        src = hh[:, bass.ds(at, 1), :] if not isinstance(i, int) else hh[:, at, :]
                        V.tensor_tensor(dst, hbuf[:, (j - 2) % RING, :], src.bitcast(F32), ALU.subtract)\
                            .then_inc(low_done, 1)
                    if inside(i, j, 0, NF):
                        for d in (1, 2):
                            for t in range(2):
                                if d == 1:
                                    dve.wait_ge(pre_done, pre0 + 2 * s + t + 1)
                                else:
                                    dve.wait_ge(conv_step, cs0 + 2 * s + t + 1)
                                ins = tap(pre[:, 2 * (j % RING) + t, :], bank(tile_group(up, j, t)),
                                          vdyn(f"up_w{f}", 44 * (2 - d) + 2 * s + t), d)
                                if d == 2:
                                    give_back(ins, tile_group(up, j, t))
                                else:
                                    ins.then_inc(conv_step, 1)

                repeat(dve, NF, stage, 2)
                residual3(dn, r + 1, scale)

            ffn(0, ("n1", [(1, lambda m: vec("ffn_ln0", m), None)], 1), 1)
            norm("n2", [(2, lambda m: vec("kv_ln", m), None), (3, lambda m: vec("attn_ln", m), None)], 2)
            for s in range(4):
                lo("k", s)
            for s in range(4):
                lo("v", s)

            def head_norm(name, f, gain, n0):
                for h in range(8):
                    given_back(dve, PL.G[name] + h)
                    if n0 + h >= 2:
                        dve.wait_ge(kqn_done, n0 + h - 1)
                    V.reciprocal(arst[:, h % 2, :], arms[:, h % 2, :]).then_inc(arst_done, 1)
                    dve.wait_ge(arst_done, n0 + h + 1)
                    V.scalar_tensor_tensor(f[:, h, :], f[:, h, :], gain, arst[:, h % 2, :], ALU.mult, ALU.mult)\
                        .then_inc(kqn_done, 1)

            for h in range(8):
                given_back(dve, PL.G["k"] + h)
            head_norm("kss", kf, vec("k_norm"), 0)
            for s in range(4):
                lo("q", s)
            for h in range(8):
                given_back(dve, PL.G["q"] + h)
            head_norm("qss", qf, vec("q_norm"), 8)

            def negated(lg, g, bias):
                step.add(V.scalar_tensor_tensor(lg[:, 0:P], bank(g)[:, 0:P], -(64 ** -0.5), bias[:, P:T],
                                                ALU.mult, ALU.subtract))
                return V.scalar_tensor_tensor(lg[:, P:384], bank(g)[:, P:384], -(64 ** -0.5), bias,
                                              ALU.mult, ALU.subtract)

            def row_mins(lg, q, row, done):
                for i in range(2):
                    cols = slice(0, P) if i == 0 else slice(P, 384)
                    V.tensor_reduce(mins[:, q, row + i:row + i + 1], lg[:, cols], AX.X, ALU.min).then_inc(done, 1)

            dve.wait_ge(bt_in, 16)
            for it in range(9):
                if it < 8:
                    q = it % 2
                    for c in range(2):
                        g = PL.G[f"sc{it}"] + c
                        lg = logit[:, 2 * q + c, :]
                        if it >= 2:
                            dve.wait_ge(attn_done, it - 1)
                        wait_misc(dve, f"sc{it}", c)
                        give_back(negated(lg, g, bt[:, it, :]), g)
                        step.wait()
                        given_back(dve, g)
                        row_mins(lg, q, 2 * c, min_done)
                if it >= 1:
                    h = it - 1
                    q = h % 2
                    dve.wait_ge(exp_done, 4 * (h + 1))
                    step.add(V.reciprocal(recs[:, q, :], sums[:, q, :]))
                    step.wait()
                    step.add(V.tensor_scalar(coef[:, q, :], recs[:, q, 2:4], negl, None, ALU.mult))
                    if h >= 2:
                        wait_misc(dve, f"at{h-2}")
                    for i in range(2):
                        cols = slice(0, P) if i == 0 else slice(P, 384)
                        step.add(V.tensor_scalar(At[:, q, cols], logit[:, 2 * q, cols], recs[:, q, i:i + 1], None,
                                                 ALU.mult))
                    step.wait()
                    for i in range(2):
                        cols = slice(0, P) if i == 0 else slice(P, 384)
                        ins = V.scalar_tensor_tensor(At[:, q, cols], logit[:, 2 * q + 1, cols], coef[:, q, i:i + 1],
                                                     At[:, q, cols], ALU.mult, ALU.add)
                        if i:
                            ins.then_inc(attn_done, 1)
                        else:
                            step.add(ins)
            for h in range(8):
                given_back(dve, PL.G["os"] + h)
                if h >= 2:
                    dve.wait_ge(on_done, h - 1)
                V.reciprocal(arst[:, h % 2, :], arms[:, h % 2, :]).then_inc(arst_done, 1)
                dve.wait_ge(arst_done, 16 + h + 1)
                if h >= 2:
                    dve.wait_ge(ol_done, h - 1)
                V.scalar_tensor_tensor(onr[:, h % 2, :], qf[:, h, :], sgs, arst[:, h % 2, :], ALU.mult, ALU.mult)\
                    .then_inc(on_done, 1)
                if h:
                    dve.wait_ge(oh_done, h)
                    V.tensor_tensor(ol[:, h - 1, :], onr[:, (h - 1) % 2, :], oh[:, h - 1, :].bitcast(F32),
                                    ALU.subtract).then_inc(ol_done, 1)
            dve.wait_ge(oh_done, 8)
            V.tensor_tensor(ol[:, 7, :], onr[:, 1, :], oh[:, 7, :].bitcast(F32), ALU.subtract).then_inc(ol_done, 1)
            residual("ao", 3, 4, tiles_two("ao"))
            ffn(1, ("n3", [(4, lambda m: vec("ffn_ln1", m), None)], 3), 3)
            dve.wait_ge(ada_used, 96)
            step.add(V.tensor_tensor(mod, adaP[:, 0:48], vec("b_ada", 0, 48), ALU.add))
            step.wait()
            step.add(V.scalar_tensor_tensor(gs1, mod[:, 8:16], 1.0, vec("g_mix", 0, 8), ALU.add, ALU.mult))
            step.add(V.scalar_tensor_tensor(gs2, mod[:, 32:40], 1.0, vec("g_ffn", 0, 8), ALU.add, ALU.mult))
            step.wait()
            norm("n4", [(5, lambda m: gs1[:, m:m + 1], None)], 4)
            g = PL.G["wi"]
            wait_misc(dve, "wi")
            give_back(V.tensor_tensor(wi_s, bank(g)[:, 0:16].rearrange("p (c h) -> p c h", c=2),
                                      vec("b_wi", 0, 8).rearrange("p (c h) -> p c h", c=1).to_broadcast([P, 2, 8]),
                                      ALU.add), g)
            given_back(dve, g)
            step.add(V.tensor_scalar(wi_s, wi_s, 8 ** -0.5, None, ALU.mult))
            for name, n in (("q2", 2), ("kk", 1)):
                for s in range(n):
                    lo(name, s)
            lo("kiv", 0)
            g = PL.G["kiv"] + 1
            wait_tile(dve, "kiv", 0, 0, 1)
            V.tensor_tensor(v2t, bank(g)[:, 0:T].rearrange("p (c h) -> p c h", c=2),
                            vec("b_v", 0, P).rearrange("p (c h) -> p c h", c=1).to_broadcast([P, 2, P]),
                            ALU.add).then_inc(qkv2_done2, 1)
            dve.wait_ge(qkv2_done2, 1)
            dve.sem_inc(free[g % PRING], 1)
            for s in range(2):
                lo("qi", s)
            step.wait()
            for h in range(8):
                given_back(dve, PL.G["ix"] + h)
                if h:
                    dve.wait_ge(score_step, 2 * h)
                for i in range(2):
                    cols = slice(0, P) if i == 0 else slice(P, 384)
                    if h == 0:
                        ins = V.tensor_scalar(score[:, 0, cols], rel[:, 0, cols], wi_s[:, i, 0:1], None, ALU.mult)
                    else:
                        ins = V.scalar_tensor_tensor(score[:, 0, cols], rel[:, h % 2, cols], wi_s[:, i, h:h + 1],
                                                     score[:, 0, cols], ALU.mult, ALU.add)
                    ins.then_inc(score_step, 1)
            dve.wait_ge(score_step, 16)
            dve.wait_ge(mask_done, 1)
            step.add(V.tensor_tensor(score[:, 0, 0:P], score[:, 0, 0:P], mneg[:, P:T], ALU.add))
            step.add(V.tensor_tensor(score[:, 0, P:384], score[:, 0, P:384], mneg, ALU.add))
            step.wait()

            def take(i, r):
                cols = slice(0, P) if i == 0 else slice(P, 384)
                m = m8s[:, i, :]
                step.add(V.max(m, score[:, r % 2, cols]))
                step.wait()
                step.add(V.match_replace(score[:, (r + 1) % 2, cols], m, score[:, r % 2, cols], TAKEN))
                step.wait()

            for r in range(TOPK // 8):
                if r < 4:
                    lo("yr", r)
                for i in range(2):
                    take(i, r)
            step.add(V.tensor_scalar(selb, score[:, 0, :], -2.0e38, NEG, ALU.is_ge, ALU.mult))

            def lru(s):
                for t in range(2):
                    n = 2 * s + t
                    dve.wait_ge(lra_done, n + 1)
                    step.add(V.tensor_tensor(lrm[:, t, :], lra[:, t, :], lra[:, t, :], ALU.mult))
                step.wait()
                for t in range(2):
                    n = 2 * s + t
                    dve.wait_ge(tanh_done, n + 1)
                    V.scalar_tensor_tensor(lrm[:, t, :], lrm[:, t, :], 1.0, rg[:, t, :], ALU.add, ALU.mult)\
                        .then_inc(m2_done, 1)
                for t in range(2):
                    n = 2 * s + t
                    given_back(dve, PL.G[f"ri{s}"] + 2 + t)
                    step.add(V.tensor_tensor(ig[:, t, :], ig[:, t, :], xrc[:, n % 4, :], ALU.mult))
                step.wait()
                for t in range(2):
                    n = 2 * s + t
                    dve.wait_ge(mult_done, n + 1)
                    step.add(V.tensor_tensor(ig[:, t, :], ig[:, t, :], lrm[:, t, :], ALU.mult))
                step.wait()
                for t in range(2):
                    V.tensor_tensor_scan(lrh[:, t, :], lra[:, t, :], ig[:, t, :], 0.0, ALU.mult, ALU.add)\
                        .then_inc(scan_done, 1)
                for t in range(2):
                    n = 2 * s + t
                    dve.wait_ge(scan_done, n + 1)
                    given_back(dve, PL.G["yr"] + n)
                    V.tensor_tensor(lrh[:, t, :], lrh[:, t, :], gyr[:, n, :], ALU.mult).then_inc(rnn_done, 1)
                for t in range(2):
                    n = 2 * s + t
                    dve.wait_ge(rh_done, n + 1)
                    V.tensor_tensor(rl[:, n, :], lrh[:, t, :], rh[:, n, :].bitcast(F32), ALU.subtract)\
                        .then_inc(rl_done, 1)

            for s in range(4):
                lo(f"xr{s}", 0)
                for d in (1, 2, 3):
                    for t in range(2):
                        n = 2 * s + t
                        if d == 1:
                            dve.wait_ge(prer_done, n + 1)
                        else:
                            step.wait()
                        ins = tap(xrc[:, n % 4, :], xrraw[:, t, :], vec("rnn_w", 8 * (3 - d) + n), d)
                        if d == 3:
                            ins.then_inc(xrc_done, 1)
                        else:
                            step.add(ins)
                if s:
                    lru(s - 1)
            dve.wait_ge(xrc_done, 8)
            lru(3)
            for name in ("ga", "gb"):
                for s in range(4):
                    lo(name, s)
            step.wait()
            dve.wait_ge(bt_in, 32)
            for it in range(9):
                if it < 8:
                    q = it % 2
                    g = PL.G[f"lg{it}"]
                    lg = logit2[:, q, :]
                    if it >= 2:
                        dve.wait_ge(attn2_done, it - 1)
                    wait_misc(dve, f"lg{it}")
                    give_back(negated(lg, g, bt2[:, it, :]), g)
                    step.wait()
                    given_back(dve, g)
                    step.add(V.tensor_tensor(lg, lg, selb, ALU.subtract))
                    step.wait()
                    row_mins(lg, q, 0, min2_done)
                if it >= 1:
                    h = it - 1
                    q = h % 2
                    dve.wait_ge(exp2_done, 2 * (h + 1))
                    step.add(V.reciprocal(recs[:, q, 0:2], sums[:, q, 0:2]))
                    step.wait()
                    if h >= 2:
                        wait_misc(dve, f"pt{h-2}")
                    for i in range(2):
                        cols = slice(0, P) if i == 0 else slice(P, 384)
                        ins = V.tensor_scalar(At2[:, q, cols], logit2[:, q, cols], recs[:, q, i:i + 1], None, ALU.mult)
                        if i:
                            ins.then_inc(attn2_done, 1)
                        else:
                            step.add(ins)
                    if h % 2:
                        n = h // 2
                        g = PL.G[f"po{n}"]
                        dve.wait_ge(ah_done, n + 1)
                        V.tensor_tensor(al[:, n, :], bank(g)[:, 0:T], ah[:, n, :].bitcast(F32), ALU.subtract)\
                            .then_inc(al_done, 1)
                        dve.wait_ge(al_done, n + 1)
                        dve.sem_inc(free[g % PRING], 1)
            for s in range(2):
                lo("woa", s)
                for t in range(4):
                    m, g = 4 * s + t, PL.G["woa"] + 4 * s + t
                    wait_tile(dve, "woa", 0, s, t, 4)
                    given_back(dve, PL.G["ga"] + m)
                    give_back(V.tensor_tensor(gaf[:, m, :], bank(g)[:, 0:T], gaf[:, m, :], ALU.mult), g)
            for s in range(4):
                lo("wor", s)
                for t in range(2):
                    m, g = 2 * s + t, PL.G["wor"] + 2 * s + t
                    wait_tile(dve, "wor", s // RING, s % RING, t)
                    given_back(dve, PL.G["gb"] + m)
                    give_back(V.tensor_tensor(gbf[:, m, :], bank(g)[:, 0:T], gbf[:, m, :], ALU.mult), g)
                    given_back(dve, g)
                    given_back(dve, PL.G["woa"] + m)
                    V.tensor_tensor(gaf[:, m, :], gaf[:, m, :], gbf[:, m, :], ALU.add).then_inc(merged_done, 1)
                for t in range(2):
                    m = 2 * s + t
                    dve.wait_ge(mh_done, m + 1)
                    V.tensor_tensor(ml[:, m, :], gaf[:, m, :], mh[:, m, :].bitcast(F32), ALU.subtract)\
                        .then_inc(ml_done, 1)
            residual("wout", 5, 4, tiles_two("wout"), lambda m: mod[:, 16 + m:17 + m])
            ffn(2, ("n5", [(6, lambda m: gs2[:, m:m + 1], None)], 5), 5, lambda m: mod[:, 40 + m:41 + m])
            norm("n6", [(7, lambda m: vec("g_final", m), None)], 6)


def layout(i):

    def slabs(w, cols):
        k, n = w.shape
        return w.reshape(k // P, P, n // cols, cols).transpose(2, 1, 0, 3).reshape(n // cols, P, k // P * cols)

    def tiles(v):
        return v.reshape(-1, P).T

    def rows(v):
        return np.broadcast_to(v.reshape(1, -1), (P, v.size))

    def pairs(w, gate, up):
        k = w.shape[0]
        a, b = w[:, gate * FF:(gate + 1) * FF], w[:, up * FF:(up + 1) * FF]
        return np.stack([a.reshape(k, NF, P), b.reshape(k, NF, P)], 2).reshape(k, 2 * FF)

    a = {}
    a["x"] = i["x"][0].T.reshape(KD, P, T).transpose(1, 0, 2)
    w = i["ssm_in_w"][0]
    a["xbc"], a["z"] = slabs(w[:, DI:DI + XBC], 256), slabs(w[:, :DI], 256)
    a["w_dt"] = w[:, DI + XBC:].reshape(KD, P, 32).transpose(1, 0, 2)
    a["so"] = slabs(i["ssm_out_w"][0], P)
    a["k"], a["v"] = slabs(i["kv_w"][:, :1024], 256), slabs(i["kv_w"][:, 1024:], 256)
    a["q"], a["ao"] = slabs(i["q_w"][0], 256), slabs(i["attn_out_w"][0], 256)
    ffns = [(i["ffn_up_w"][0], i["ffn_conv_w"][0], i["ffn_conv_b"][0], i["ffn_down_w"][0], 0, 1),
            (i["ffn_up_w"][1], i["ffn_conv_w"][1], i["ffn_conv_b"][1], i["ffn_down_w"][1], 0, 1),
            (i["w_up_2"][0], i["conv_ffn_w_2"][0], i["conv_ffn_b_2"][0], i["w_down_2"][0], 1, 0)]
    v = {}
    for n, (up, cw, cb, dn, g_, u_) in enumerate(ffns):
        a[f"up{n}"] = slabs(pairs(up, g_, u_), 256)
        v[f"up_w{n}"], v[f"up_b{n}"] = tiles(pairs(cw, g_, u_)), tiles(pairs(cb[None], g_, u_))
        a[f"dn{n}a"] = dn[:2048].reshape(2, 8, P, 4, 256).transpose(3, 0, 2, 1, 4).reshape(8, P, SLOT)
        a[f"dn{n}b"] = dn[2048:].reshape(6, P, 4, 256).transpose(2, 1, 0, 3).reshape(4, P, 6 * 256)
    w, b = i["w_in_2"][0], i["b_in_2"][0]
    k0, k1, ki = slice(512, 576), slice(576, 640), slice(1280, 1344)

    def cols(m, *parts):
        return np.concatenate([m[..., p] for p in parts], -1)

    a["q2"] = slabs(w[:, 0:512], 256)
    a["kk"] = slabs(cols(w, k0, k0, k1, k1), 256)
    a["kiv"] = slabs(cols(w, ki, ki, slice(640, 768)), 256)
    a["qi"] = slabs(w[:, 768:1280], 256)
    a["w_wi"] = w[:, 1344:1352].reshape(KD, P, 8).transpose(1, 0, 2)
    for n, name in enumerate(("xr", "yr", "ga", "gb")):
        part = slice(1352 + 1024 * n, 2376 + 1024 * n)
        a[name], v["b_" + name] = slabs(w[:, part], 256), tiles(b[part])
    a["w_ada"] = slabs(i["w_ada_2"][0], P)
    a["w_rg"], a["w_ig"] = (i[n][0].transpose(1, 0, 2).reshape(P, 1024) for n in ("w_rg_2", "w_ig_2"))
    a["woa"] = slabs(i["w_o_attn_2"][0], 512)
    a["wor"], a["wout"] = slabs(i["w_o_rnn_2"][0], 256), slabs(i["w_out_2"][0], 256)
    v.update(ssm_ln=tiles(i["ssm_ln_g"]), conv_w=tiles(i["ssm_conv_w"][0]), conv_b=tiles(i["ssm_conv_b"]),
             ssm_d=tiles(np.repeat(i["ssm_d"][0], 64)), ssm_norm=tiles(i["ssm_norm_g"]), kv_ln=tiles(i["kv_ln_g"]),
             k_norm=tiles(np.tile(i["k_norm_g"], 2)), attn_ln=tiles(i["attn_ln_g"]),
             q_norm=tiles(np.tile(i["q_norm_g"][0], 2)), subln=tiles(i["subln_g"]),
             ffn_ln0=tiles(i["ffn_ln_g"][0]), ffn_ln1=tiles(i["ffn_ln_g"][1]), b_ada=tiles(i["b_ada_2"]),
             g_mix=tiles(i["g_mix_2"]), b_q=tiles(b[0:512]), b_kk=tiles(cols(b, k0, k0, k1, k1)),
             b_ki=tiles(cols(b, ki, ki)), b_qi=tiles(b[768:1280]), rnn_w=tiles(i["conv_rnn_w_2"][0]),
             rnn_b=tiles(i["conv_rnn_b_2"]), b_rg=tiles(i["b_rg_2"]), b_ig=tiles(i["b_ig_2"]),
             lru=tiles(i["lru_lambda_2"]), g_ffn=tiles(i["g_ffn_2"]), g_final=tiles(i["g_final_2"]),
             c=tiles(i["c_2"]), dt_bias=rows(i["ssm_dt_bias"]), a_log=rows(i["ssm_a_log"]),
             b_wi=rows(b[1344:1352]), b_v=rows(b[640:768]))
    for name, n in VECS:
        assert v[name].shape == (P, n), (name, v[name].shape)
    a["lam"] = rows(i["lam_vecs"]).reshape(P, 4, 64)
    a["vecs"] = np.concatenate([v[name] for name, _ in VECS], 1)
    d = 255 - np.arange(384)
    n = np.maximum(d, 1).astype(np.float32)
    large = 16 + (np.log(n / 16) / np.float32(np.log(8.0)) * 16).astype(np.int32)
    bucket = np.where(d < 16, np.maximum(d, 0), np.minimum(large, 31))
    onehot = np.zeros((33, 384), np.float32)
    onehot[bucket[d >= 0], np.arange(384)[d >= 0]] = 1.0
    onehot[32, d < 0] = NEG
    a["onehot"] = onehot
    one = np.ones((1, 8), np.float32)
    a["rel"] = np.stack([np.concatenate([i[r], one]) for r in ("rel_bias", "rel_bias_2")], 1)
    return {k_: np.ascontiguousarray(m) for k_, m in a.items()}


def kernel(**inputs):
    import concourse.bacc as bacc
    from concourse.bass_utils import run_bass_kernel_spmd

    arrays = layout({k: np.asarray(a) for k, a in inputs.items()})
    nc = bacc.Bacc("TRN2", target_bir_lowering=False, num_devices=1)
    io = {k: nc.dram_tensor(f"in_{k}", a.shape, mybir.dt.from_np(a.dtype), kind="ExternalInput").ap()
          for k, a in arrays.items()}
    out = nc.dram_tensor("out_0", (P, KD, T), F32, kind="ExternalOutput").ap()
    build_program(nc, io, out)
    r = run_bass_kernel_spmd(nc, [{f"in_{k}": a for k, a in arrays.items()}], core_ids=[0])
    o = r.results[0]["out_0"]
    return o.transpose(1, 0, 2).reshape(D, T).T.reshape(1, T, D)
```

```python
from contextlib import ExitStack

import numpy as np

import concourse.bass as bass
from concourse import mybir

F32 = mybir.dt.float32
F32R = mybir.dt.float32r
ACT = mybir.ActivationFunctionType
ALU = mybir.AluOpType
AX = mybir.AxisListType

P = 128
D = 1024
T = 256
KD = D // P
DI = 2048
XBC = DI + 2 * 4 * 128
SSM_H = 32
FF = 2816
NF = FF // P
SLOT = 2048
RING = 3
ARING = 2
LEAD = 2
PRING = 6
EPS = 1e-6
NEG = -1.0e30
TAKEN = -3.0e38
LAM_INIT = 0.8 - 0.6 * float(np.exp(-0.3 * 1))
TOPK = 64

VECS = [
    ("ssm_ln", 8), ("conv_w", 4 * 24), ("conv_b", 24), ("ssm_d", 16), ("ssm_norm", 16),
    ("kv_ln", 8), ("k_norm", 1), ("attn_ln", 8), ("q_norm", 1), ("subln", 1),
    ("ffn_ln0", 8), ("ffn_ln1", 8),
    ("up_w0", 3 * 44), ("up_b0", 44), ("up_w1", 3 * 44), ("up_b1", 44), ("up_w2", 3 * 44), ("up_b2", 44),
    ("b_ada", 48), ("g_mix", 8), ("b_q", 4), ("b_kk", 2), ("b_ki", 1), ("b_qi", 4),
    ("b_xr", 8), ("b_yr", 8), ("b_ga", 8), ("b_gb", 8),
    ("rnn_w", 4 * 8), ("rnn_b", 8), ("b_rg", 8), ("b_ig", 8), ("lru", 8), ("g_ffn", 8),
    ("g_final", 8), 
    ("dt_bias", 32), ("a_log", 32), ("b_wi", 8), ("b_v", 128),
]
VOFF = {}
_at = 0
for _name, _n in VECS:
    VOFF[_name] = _at
    _at += _n
NVEC = _at

TWO, ONE, FOUR, PAIR3 = "two", "one", "four", "pair3"


class Plan:

    def __init__(self):
        self.slabs, self.groups, self.halves, self.miscs = 0, 0, 0, 0
        self.S, self.G, self.H, self.M, self.N, self.kind = {}, {}, {}, {}, {}, {}
        self.size = []
        self.order = []

    def stream(self, name, n, kind, source=None):
        self.S[name], self.G[name], self.H[name], self.N[name], self.kind[name] = (
            self.slabs, self.groups, self.halves, n, kind)
        self.slabs += n
        self.order.append((name, n))
        if kind == TWO:
            self.groups += 2 * n
            self.halves += n
            self.size += [SLOT] * n
        elif kind == FOUR:
            self.groups += 4 * n
            self.halves += 3 * n
            self.size += [SLOT] * n
        elif kind == ONE:
            self.groups += n
            self.size += [SLOT] * n
        else:
            self.groups += 2 * (n // 3)
            self.halves += n // 3
            self.size += [SLOT, SLOT, 6 * 256] * (n // 3)

    def misc(self, name, n=1):
        self.G[name], self.M[name] = self.groups, self.miscs
        self.groups += n
        self.miscs += n

    def open(self, name):
        self.G[name] = self.groups
        self.groups += 1

    def close(self, name):
        self.M[name] = self.miscs
        self.miscs += 1


def make_plan():
    pl = Plan()
    pl.misc("n0", 2)
    pl.misc("tz", 2)
    pl.misc("dt")
    pl.stream("xbc", 12, TWO)
    pl.misc("e12")
    pl.misc("cb", 4)
    pl.misc("sega0", 2)
    pl.misc("xt0", 2)
    for g in range(4):
        pl.stream(f"za{g}", 1, TWO)
        pl.misc(f"y0{g}")
        pl.misc(f"segb{g}", 2)
        pl.misc(f"yo{g}")
        if g:
            pl.misc(f"gn{g-1}")
        pl.stream(f"zb{g}", 1, TWO)
        pl.misc(f"y1{g}")
        if g < 3:
            pl.misc(f"sega{g+1}", 2)
            pl.misc(f"xt{g+1}", 2)
        pl.misc(f"yt{g}", 2)
    pl.misc("gn3")
    pl.stream("so", 8, ONE)
    pl.misc("n1", 2)
    pl.stream("up0", NF, TWO)
    pl.stream("dn0", 12, PAIR3)
    pl.misc("n2", 2)
    for s in range(6):
        if s < 4:
            pl.stream(f"k{s}", 1, TWO)
        if s >= 3:
            pl.misc(f"or{s-3}", 2)
        if s >= 2:
            pl.misc(f"at{2*s-3}")
            pl.misc(f"pv{2*s-3}")
        if 1 <= s < 5:
            pl.misc(f"sc{2*s-2}", 2)
        if s < 4:
            pl.stream(f"q{s}", 1, TWO)
        if 1 <= s < 5:
            pl.misc(f"sc{2*s-1}", 2)
        if s < 4:
            pl.misc(f"kss{s}")
            pl.stream(f"v{s}", 1, TWO)
            pl.misc(f"kr{s}", 2)
        if 1 <= s < 5:
            pl.misc(f"at{2*s-2}")
            pl.misc(f"pv{2*s-2}")
        if s < 4:
            pl.misc(f"qss{s}")
        if s >= 2:
            pl.misc(f"os{s-2}")
    pl.misc("or3", 2)
    pl.stream("ao", 4, TWO)
    pl.misc("n3", 2)
    pl.stream("up1", NF, TWO)
    pl.stream("dn1", 12, PAIR3)
    pl.misc("n4", 2)
    pl.misc("wi")
    pl.stream("qb", 2, TWO)
    pl.stream("kk", 1, TWO)
    pl.stream("kiv", 1, TWO)
    pl.stream("qi", 2, TWO)
    pl.misc("ix", 8)
    for s in range(4):
        pl.stream(f"yr{s}", 1, TWO)
        if s:
            pl.misc(f"ri{s-1}", 4)
        pl.stream(f"xr{s}", 1, TWO)
    for h in range(9):
        if h < 8:
            pl.stream(f"{'ga' if h < 4 else 'gb'}{h%4}", 1, TWO)
        if h == 0:
            pl.misc("ri3", 4)
        if h >= 1:
            pl.misc(f"pt{h-1}")
            if (h - 1) % 2 == 0:
                pl.open(f"po{(h-1)//2}")
            else:
                pl.close(f"po{(h-1)//2}")
        if h < 8:
            pl.misc(f"lg{h}")
    pl.stream("woa", 2, FOUR)
    pl.stream("wor", 4, TWO)
    pl.stream("wout", 4, TWO)
    pl.misc("n5", 2)
    pl.stream("up2", NF, TWO)
    pl.stream("dn2", 12, PAIR3)
    pl.misc("n6", 2)
    return pl


PL = make_plan()


ADA = {**{f"z{half}{gr}": 1 for gr in range(4) for half in "ab"}, "so": 5, "dn0": 10,
       **{f"{w}{s}": 1 for w in "kv" for s in range(4)}, "q0": 1, "q1": 1, "q2": 1, "q3": 1, "ao": 3, "dn1": 10}
assert sum(ADA.values()) == 48


def repeat(eng, n, stage, lag=0, rolled=True):
    full = n // RING
    if rolled and full >= 3:
        for s in range(RING):
            stage(0, s)
        with eng.Fori(1, full) as i:
            for j in range(RING):
                stage(i, j)
        for s in range(full * RING, n + lag):
            stage(s // RING, s % RING)
    else:
        for s in range(n + lag):
            stage(s // RING, s % RING)


def inside(i, j, back, n):
    return not isinstance(i, int) or 0 <= RING * i + j - back < n


def build_program(nc, io, out):
    with ExitStack() as ctx:
        def sb(name, shape, dt=F32):
            return ctx.enter_context(nc.sbuf_tensor(name, shape, dt))

        def sem(name):
            return ctx.enter_context(nc.semaphore(name))

        raw = sb("raw", [P, RING, SLOT])
        wwi = sb("wwi", [P, KD, 8])
        rel_sb = sb("rel_sb", [33, 2, 8])
        blk = sb("blk", [P, P])
        m8s = sb("m8s", [P, 2, 8])
        wh = sb("wh", [P, RING, SLOT], F32R)
        wl = sb("wl", [P, RING, SLOT], F32R)
        x = sb("x", [P, KD, T])
        xh = sb("xh", [P, KD, T], F32R)
        xl = sb("xl", [P, KD, T], F32R)
        actr = sb("actr", [P, 2 * NF * T], F32R)
        FN = 50 * 256
        work = sb("work", [P, FN])
        cact = sb("cact", [P, D])
        ada_sum = sb("ada_sum", [P, 96])
        ada_w = sb("ada_w", [P, ARING, 512])
        vecs = sb("vecs", [P, NVEC])
        ident = sb("ident", [P, P])
        tri = sb("tri", [P, 3, P])
        ones = tri[:, 1, :]
        later = sb("later", [P, P])
        eps_t = sb("eps_t", [P, 1])
        small = sb("small", [P, 424])
        ps = ctx.enter_context(nc.psum_tensor("ps", [P, PRING, 512], F32))

        def vec(name, i=0, n=1):
            return vecs[:, VOFF[name] + i:VOFF[name] + i + n]

        def vdyn(name, i):
            return vecs[:, bass.ds(i + VOFF[name], 1)] if not isinstance(i, int) else vec(name, i)

        def W(off, *dims):
            n = int(np.prod(dims))
            assert off + n <= FN, (off, dims)
            a = work[:, off:off + n]
            if len(dims) == 2:
                a = a.rearrange("p (a b) -> p a b", b=dims[1])
            if len(dims) == 3:
                a = a.rearrange("p (a b c) -> p a b c", b=dims[1], c=dims[2])
            return a

        def R(off, a, b):
            return actr[:, off:off + a * b].rearrange("p (a b) -> p a b", b=b)

        KB = 256
        landed = [sem(f"landed{r}") for r in range(RING)]
        hi_done, lo_done = sem("hi_done"), sem("lo_done")
        slab_done, half_done = sem("slab_done"), sem("half_done")
        misc_done = sem("misc_done")
        free = [sem(f"free{r}") for r in range(PRING)]
        vecs_in, x_in, small_in = sem("vecs_in"), sem("x_in"), sem("small_in")
        ada_in = [sem(f"ada_in{r}") for r in range(ARING)]
        ada_used = sem("ada_used")
        const_pool, const_done = sem("const_pool"), sem("const_done")
        sq_done, acc_done = sem("sq_done"), sem("acc_done")
        rstd_done, xn_done, xs_done = sem("rstd_done"), sem("xn_done"), sem("xs_done")
        xh_done, xl_done = sem("xh_done"), sem("xl_done")
        c_in, lam_in_sem, wri_in = sem("c_in"), sem("lam_in"), sem("wri_in")
        out_done = sem("out_done")
        (cact_done, ea_done, lam_done, spe_done, tz_out, pre_done, conv_step, xbc_done, a_done,
         ysq_done, segl_done, decay_done, xdte_done, low_done, yh_done, yn_done, gated_done, grst_done,
         bt_in, gsil_done, h_done, hh_done, kq2_done, kqn_done, krinv_done, orinv_done, vt_done, min_done,
         exp_done, attn_done, osq_done, on_done, oh_done, ol_done, wwi_in, qkv2_done, qkv2_done2,
         score_step, mask_done, xrraw_done, prer_done, xrc_done, lra_done, tanh_done, m2_done, mult_done,
         scan_done, rnn_done, rh_done, rl_done, min2_done, exp2_done, attn2_done, ah_done, al_done,
         merged_done, mh_done, ml_done) = [sem(n) for n in (
            "cact_done ea_done lam_done spe_done tz_out pre_done conv_step xbc_done a_done "
            "ysq_done segl_done decay_done xdte_done low_done yh_done yn_done gated_done grst_done "
            "bt_in gsil_done h_done hh_done kq2_done kqn_done krinv_done orinv_done vt_done min_done "
            "exp_done attn_done osq_done on_done oh_done ol_done wwi_in qkv2_done qkv2_done2 "
            "score_step mask_done xrraw_done prer_done xrc_done lra_done tanh_done m2_done mult_done "
            "scan_done rnn_done rh_done rl_done min2_done exp2_done attn2_done ah_done al_done "
            "merged_done mh_done ml_done").split()]
        bt2_in = [sem("bt2_in0"), sem("bt2_in1")]
        ytok_done = [sem("ytok0_done"), sem("ytok1_done")]
        dve_step, act_step, pool_step = sem("dve_step"), sem("act_step"), sem("pool_step")

        class Steps:

            def __init__(self, eng, s):
                self.eng, self.s, self.n = eng, s, 0

            def add(self, ins):
                self.n += 1
                ins.then_inc(self.s, 1)
                return self.n

            def wait(self, n=None):
                self.eng.wait_ge(self.s, self.n if n is None else n)

        def bank(g):
            return ps[:, g % PRING, :]

        def acquire(eng, g0, i=0):
            if not (isinstance(i, int) and g0 // PRING + i == 0):
                eng.wait_ge(free[g0 % PRING], g0 // PRING + i)

        def given_back(eng, g0, i=0):
            eng.wait_ge(free[g0 % PRING], g0 // PRING + i + 1)

        def give_back(ins, g0):
            ins.then_inc(free[g0 % PRING], 1)

        def wait_misc(eng, name, n=0):
            eng.wait_ge(misc_done, PL.M[name] + n + 1)

        def wait_tile(eng, name, i, j, t, tiles=2):
            if t == tiles - 1:
                eng.wait_ge(slab_done, PL.S[name] + RING * i + j + 1)
            else:
                eng.wait_ge(half_done, PL.H[name] + (tiles - 1) * (RING * i + j) + t + 1)

        def tile_group(name, j, t, tiles=2):
            return PL.G[name] + tiles * j + t

        total = PL.slabs

        def split_hi(act, b, i=0):
            if isinstance(i, int) and b + RING * i >= total:
                return
            n = PL.size[b + (RING * i if isinstance(i, int) else RING)]
            act.wait_ge(landed[b % RING], 16 * (b // RING + i + 1))
            if not isinstance(i, int) or b + RING * i >= RING:
                act.wait_ge(slab_done, b + RING * i - RING + 1)
            nc.scalar.activation(wh[:, b % RING, 0:n], raw[:, b % RING, 0:n], ACT.Copy).then_inc(hi_done, 1)

        def split_lo(dve, b, i=0):
            if isinstance(i, int) and b + RING * i >= total:
                return
            n = PL.size[b + (RING * i if isinstance(i, int) else RING)]
            dve.wait_ge(hi_done, b + RING * i + 1)
            nc.vector.tensor_tensor(wl[:, b % RING, 0:n], raw[:, b % RING, 0:n],
                                    wh[:, b % RING, 0:n].bitcast(F32), ALU.subtract).then_inc(lo_done, 1)

        xn = W(0, KD, T)
        sq = W(8 * KB, 2, T)
        acc = W(10 * KB, T)
        onehot = W(19 * KB, 384)
        wdt = W(21 * KB, KD, 32)
        lam_in = W(22 * KB, 4, 64)
        sp1, sp2, sp3, sp4 = (W(24 * KB + 64 * n, 64) for n in range(4))
        pre = W(13 * KB, 6, T)
        gsil = W(19 * KB, 3, T)
        hbuf = W(22 * KB, 3, T)
        hh, hl = R(0, NF, T), R(NF * T, NF, T)
        bvr = W(8 * KB, 2, 384)
        xbc = W(26 * KB, 24, T)
        cbm = W(0, 4, 384)
        xdte = W(6 * KB, 512)
        yoffs = W(8 * KB, 512)
        zs = W(13 * KB, 4, T)
        ynr = W(17 * KB, 2, T)
        xdt = W(19 * KB, 2, 512)
        segl = W(42 * KB, 8, P)
        decay = W(46 * KB, 2, 512)

        def ysq(t):
            return ynr[:, t, :] if t < 2 else zs[:, t, :]

        ytok = [W(23 * KB, 512), W(10 * KB, 512)]
        grms, grst = W(12 * KB, T), W(25 * KB, T)
        yh, yl = R(0, 16, T), R(16 * T, 16, T)
        kf, qf = W(13 * KB, 8, T), W(21 * KB, 8, T)
        vt = W(29 * KB, 2, 1024)
        bt = W(37 * KB, 8, T)
        qrms, krms, orms = W(45 * KB, 2, 8), W(45 * KB + 32, 2, 8), W(45 * KB + 64, 2, 4)
        logit = W(0, 4, 384)
        At = W(6 * KB, 2, 384)
        ATt = W(9 * KB, 2, 384)

        def squares(what, h):
            return (kf if what == "k" else qf)[:, (h + 2) % 8, :]

        x2h, x2l = R(0, 8, T), R(8 * T, 8, T)
        oh, ol = R(16 * T, 8, T), R(24 * T, 8, T)
        q2f = W(13 * KB, 4, T)
        kkf = W(17 * KB, 2, T)
        kif = W(19 * KB, T)
        v2t = W(20 * KB, 2, P)
        qif = W(21 * KB, 4, T)
        score = W(25 * KB, 2, 384)
        mneg = W(28 * KB, T)
        rel = W(29 * KB, 2, 384)
        selb = W(32 * KB, 384)
        gyr = W(34 * KB, 8, T)
        bt2 = [W(46 * KB, 4, T), W(42 * KB, 4, T)]
        wri = W(0, 2, 1024)
        gaf, gbf = W(0, 8, T), W(34 * KB, 8, T)
        xrraw = W(21 * KB, 2, T)
        xrc = W(42 * KB, 4, T)
        rg = W(8 * KB, 2, T)
        ig = W(10 * KB, 2, T)
        lra = W(29 * KB, 2, T)
        lrm = W(23 * KB, 2, T)
        lrh = W(26 * KB, 2, T)
        logit2 = W(8 * KB, 2, 384)
        At2 = W(26 * KB, 2, 384)
        ATt2 = W(22 * KB, 2, 384)
        rh, rl = R(0, 8, T), R(8 * T, 8, T)
        ah, al = R(16 * T, 4, T), R(20 * T, 4, T)
        mh, ml = R(24 * T, 8, T), R(32 * T, 8, T)
        taken = [0]

        def S(*dims):
            n = int(np.prod(dims))
            a = small[:, taken[0]:taken[0] + n]
            taken[0] += n
            return a.rearrange("p (a b) -> p a b", b=dims[1]) if len(dims) == 2 else a

        dt_t, a_t = S(2, 32), S(2, 32)
        e12, ea = S(64), S(32)
        lam2, lam4, negl, sgs = S(2), S(2), S(1), S(1)
        mod, gs1, gs2 = S(48), S(8), S(8)
        negc, posc = S(8), S(8)
        lp1, lp2, lp3, lp4, lpa = S(8), S(8), S(8), S(8), S(8)
        wi_s = S(2, 8)
        rms_t, rinv_t = S(2), S(2)
        warm = S(1)
        mins, sums, recs, coef = S(2, 4), S(2, 4), S(2, 4), S(2, 2)
        scratch = nc.dram_tensor("bias_by_distance", (2, 8, P, 384), F32, kind="Internal")
        def toeplitz(b_, h0, n):
            return bass.AP(scratch_t, (8 * b_ + h0) * P * 384 + 127, [[383, P], [P * 384, n], [1, T]])

        scratch_t, scratch = scratch, scratch.ap()

        def sources():
            out_ = []
            for name, n in PL.order:
                key, at = name, 0
                if name[-1].isdigit() and name[:-1] in ("za", "zb", "xr", "yr", "ga", "gb", "k", "q", "v"):
                    key, at = name[:-1], int(name[-1])
                if key in ("za", "zb"):
                    key, at = "z", 2 * at + (key == "zb")
                out_.append((name, n, key, at))
            return out_

        block = ctx.enter_context(nc.Block())

        @block.sync
        def _(sp):
            sp.dma_start(x[:, :, :], io["x"]).then_inc(x_in, 16)
            sp.dma_start(wdt, io["w_dt"]).then_inc(small_in, 16)
            sp.dma_start(rel_sb[:, :, :], io["rel"]).then_inc(small_in, 16)
            sp.dma_start(onehot[0:33, :], io["onehot"]).then_inc(small_in, 16)
            sp.dma_start(wwi[:, :, :], io["w_wi"]).then_inc(wwi_in, 16)
            for name, n, key, at in sources():
                base = PL.S[name]

                def load(i, j):
                    b = base + j
                    if not isinstance(i, int) or b + RING * i >= RING:
                        sp.wait_ge(lo_done, b + RING * i - RING + 1)
                    s = RING * i + j
                    if PL.kind[name] == PAIR3:
                        src = io[key + "a"][2 * i + j] if j < 2 else io[key + "b"][i]
                    else:
                        src = io[key][s + at]
                    sp.dma_start(raw[:, b % RING, 0:src.shape[-1]], src).then_inc(landed[b % RING], 16)

                if PL.kind[name] == PAIR3:
                    for s in range(n):
                        load(s // RING, s % RING)
                else:
                    repeat(sp, n, load)
            sp.wait_ge(xn_done, 8 * 8)
            sp.dma_start(out, xn[:, :, :]).then_inc(out_done, 16)
            sp.wait_ge(out_done, 16)

        LOW0 = 16
        NCONST = 6

        @block.gpsimd
        def _(pool):
            step = Steps(pool, pool_step)
            step.add(nc.gpsimd.memset(tri[:, :, :], 1.0))
            step.add(nc.gpsimd.memset(ident[:, :], 0.0))
            step.add(nc.gpsimd.memset(blk[:, :], 0.0))
            step.add(nc.gpsimd.memset(eps_t[:, :], EPS))
            step.wait()
            for c in (0, 2):
                nc.gpsimd.affine_select(out=tri[:, c, :], in_=ones, pattern=[[1, P]], compare_op=ALU.is_ge,
                                        fill=0.0, base=0, channel_multiplier=-1).then_inc(const_done, 1)
            nc.gpsimd.affine_select(out=later[:, :], in_=ones, pattern=[[-1, P]], compare_op=ALU.is_ge,
                                    fill=0.0, base=-1, channel_multiplier=1).then_inc(const_done, 1)
            nc.gpsimd.affine_select(out=ident[:, :], in_=ident[:, :], pattern=[[-1, P]], compare_op=ALU.not_equal,
                                    fill=1.0, base=0, channel_multiplier=1).then_inc(const_done, 1)
            pool.dma_start(cact[:, :], io["c"].to_broadcast([P, D])).then_inc(c_in, 16)
            pool.wait_ge(const_done, NCONST - 2)
            nc.gpsimd.memset(blk[0:64, 0:64], 1.0).then_inc(const_done, 1)
            nc.gpsimd.memset(blk[64:128, 64:128], 1.0).then_inc(const_done, 1)
            for a in range(96):
                if a >= ARING:
                    pool.wait_ge(ada_used, a - ARING + 1)
                pool.dma_start(ada_w[:, a % ARING, :], io["w_ada"][a // 2][:, 512 * (a % 2):512 * (a % 2) + 512])\
                    .then_inc(ada_in[a % ARING], 16)
            pool.wait_ge(acc_done, 7 * 5)
            step.add(nc.gpsimd.memset(mneg, 0.0))
            step.wait()
            nc.gpsimd.affine_select(out=mneg, in_=mneg, pattern=[[-1, T]], compare_op=ALU.is_ge,
                                    fill=NEG, base=P, channel_multiplier=1).then_inc(mask_done, 1)
            pool.wait_ge(xl_done, 8 * 6)
            wait_misc(pool, "wi")
            pool.dma_start(wri[:, 0, :], io["w_rg"]).then_inc(wri_in, 16)
            pool.dma_start(wri[:, 1, :], io["w_ig"]).then_inc(wri_in, 16)


        @block.tensor
        def _(pe):
            def mm3(o, w, xp, start, stop, tok):
                (w_h, w_l), (x_h, x_l) = w, xp
                for n, (a, b) in enumerate(((w_l, x_h), (w_h, x_l), (w_h, x_h))):
                    l, r = (b, a) if tok else (a, b)
                    mm = nc.tensor.matmul(o, l, r, start=start and n == 0, stop=stop and n == 2)
                return mm

            def stream(name, X, ready=None):
                n, kind = PL.N[name], PL.kind[name]
                base, g0 = PL.S[name], PL.G[name]
                tiles = {TWO: 2, ONE: 1, FOUR: 4, PAIR3: 2}[kind]
                kts = {TWO: 8, ONE: 16, FOUR: 4}.get(kind)

                def stage(i, j):
                    b = base + j
                    pe.wait_ge(lo_done, b + RING * i + 1)
                    r = b % RING
                    width = SLOT // kts if kind != PAIR3 else 256
                    if kind == TWO and ready and isinstance(i, int) and i == 0 and j == 0:
                        acquire(pe, g0)
                        acquire(pe, g0 + 1)
                        for k in range(kts):
                            ready(k)
                            for t in range(2):
                                off = k * width + t * P
                                mm = mm3(bank(g0 + t)[:, 0:T], (wh[:, r, off:off + P], wl[:, r, off:off + P]),
                                         (X[0][:, k, :], X[1][:, k, :]), k == 0, k == kts - 1, False)
                                if k == kts - 1:
                                    mm.then_inc(half_done if t == 0 else slab_done, 1)
                        return
                    for t in range(tiles):
                        first = isinstance(i, int) and i == 0 and j == 0 and t == 0
                        if kind == PAIR3:
                            g, gi = g0 + 2 * i + t, 0
                            if j == 0:
                                acquire(pe, g)
                            ks = range(8 * j, min(8 * j + 8, NF))
                            begin, end = j == 0, j == 2
                        else:
                            g, gi = g0 + tiles * j + t, i
                            if tiles * RING % PRING:
                                g, gi = g0 + tiles * (RING * i + j) + t, 0
                            acquire(pe, g, gi)
                            ks = range(kts)
                            begin = end = True
                        for k in ks:
                            if ready and (isinstance(i, int) and i == 0 and t == 0 and (first or kind == PAIR3)):
                                ready(k)
                            off = (k - ks[0]) * width + t * P
                            st, en = begin and k == ks[0], end and k == ks[-1]
                            wp = (wh[:, r, off:off + P], wl[:, r, off:off + P])
                            mm = mm3(bank(g)[:, 0:T], wp, (X[0][:, k, :], X[1][:, k, :]), st, en, False)
                        if t == tiles - 1:
                            mm.then_inc(slab_done, 1)
                        elif end:
                            mm.then_inc(half_done, 1)

                repeat(pe, n, stage, rolled=kind == TWO)

            def stream_tok(name, X):
                for s in range(PL.N[name]):
                    b = PL.S[name] + s
                    pe.wait_ge(lo_done, b + 1)
                    r = b % RING
                    for t in range(2):
                        g = PL.G[name] + 2 * s + t
                        acquire(pe, g)
                        for k in range(KD):
                            mm = mm3(bank(g)[:, 0:256],
                                     (wh[:, r, k * 256:k * 256 + 256], wl[:, r, k * 256:k * 256 + 256]),
                                     (X[0][:, k, P * t:P * t + P], X[1][:, k, P * t:P * t + P]),
                                     k == 0, k == KD - 1, True)
                        mm.then_inc(half_done if t == 0 else slab_done, 1)

            def by_token(o, tile, cols):
                n = cols.shape[-1]
                for b_ in range(2):
                    mm = nc.tensor.matmul(o[:, n * b_:n * b_ + n], tile[:, P * b_:P * b_ + P], cols,
                                          start=True, stop=True)
                return mm

            def over_features(o, v, parts=1):
                n = P // parts
                for b_ in range(2):
                    for part in range(parts):
                        c = parts * b_ + part
                        mm = nc.tensor.matmul(o[n * part:n * part + n, P * b_:P * b_ + P],
                                              v[:, c:c + 1].to_broadcast([P, n]), ident[:, :], start=True, stop=True)
                return mm

            def norm_sum(name, r):
                g = PL.G[name]
                acquire(pe, g)
                pe.wait_ge(acc_done, 7 * (r + 1))
                by_token(bank(g), acc, ones[:, 0:1]).then_inc(misc_done, 1)
                acquire(pe, g + 1)
                pe.wait_ge(rstd_done, r + 1)
                over_features(bank(g + 1), rinv_t).then_inc(misc_done, 1)

            def x_ready(use):
                return lambda k: pe.wait_ge(xl_done, 8 * use + k + 1)

            pe.wait_ge(const_done, NCONST)
            norm_sum("n0", 0)
            pe.wait_ge(small_in, 48)
            for b_ in range(2):
                acquire(pe, PL.G["tz"] + b_)
                nc.tensor.matmul(bank(PL.G["tz"] + b_)[0:8, 0:384], rel_sb[0:33, b_, :], onehot[0:33, :],
                                 start=True, stop=True).then_inc(misc_done, 1)
            g = PL.G["dt"]
            acquire(pe, g)
            for c in range(2):
                for k in range(KD):
                    pe.wait_ge(xn_done, k + 1)
                    mm = nc.tensor.matmul(bank(g)[:, 32 * c:32 * c + 32], xn[:, k, P * c:P * c + P],
                                          wdt[:, k, :], start=(k == 0), stop=(k == KD - 1))
            mm.then_inc(misc_done, 1)
            stream("xbc", (xh, xl), x_ready(0))
            g = PL.G["e12"]
            acquire(pe, g)
            pe.wait_ge(a_done, 1)
            nc.tensor.matmul(bank(g)[:, 0:32], later[:, :], a_t[:, 0, :], start=True, stop=True)
            nc.tensor.matmul(bank(g)[:, 32:64], tri[:, 0, :], a_t[:, 1, :], start=True, stop=True)\
                .then_inc(misc_done, 1)
            pe.wait_ge(xbc_done, 24)
            for gr in range(4):
                g = PL.G["cb"] + gr
                acquire(pe, g)
                B, C = xbc[:, 16 + gr, :], xbc[:, 20 + gr, :]
                nc.tensor.matmul(bank(g)[:, 0:T], B[:, 0:P], C, start=True, stop=True)
                nc.tensor.matmul(bank(g)[:, T:384], B[:, P:T], C[:, P:T], start=True, stop=True)\
                    .then_inc(misc_done, 1)

            def group_norm_sum(gr):
                g = PL.G[f"gn{gr}"]
                acquire(pe, g)
                for t in range(4):
                    pe.wait_ge(ysq_done, 4 * gr + t + 1)
                    mm = nc.tensor.matmul(bank(g)[:, 0:T], ones, ysq(t), start=(t == 0), stop=(t == 3))
                mm.then_inc(misc_done, 1)

            def x_by_token(gr):
                for c in range(2):
                    g = PL.G[f"xt{gr}"] + c
                    acquire(pe, g)
                    for t in range(4):
                        mm = nc.tensor.transpose(bank(g)[:, t * P:(t + 1) * P],
                                                 xbc[:, 4 * gr + t, c * P:(c + 1) * P], ident[:, :])
                    mm.then_inc(misc_done, 1)

            def segs(gr, part):
                for q in range(2):
                    g = PL.G[f"seg{part}{gr}"] + q
                    acquire(pe, g)
                    qq = 4 * gr + 2 * (part == "b") + q
                    pe.wait_ge(segl_done, 4 * (qq + 1))
                    for t in range(4):
                        mm = nc.tensor.matmul(bank(g)[:, t * P:(t + 1) * P], segl[:, 4 * (q % 2) + t, :],
                                              tri[:, 0, :], start=True, stop=True)
                    mm.then_inc(misc_done, 1)

            def y_heads(gr, c):
                g = PL.G[f"y{c}{gr}"]
                acquire(pe, g)
                for q in range(2):
                    pe.wait_ge(decay_done, 4 * gr + 2 * c + q + 1)
                    for t in range(4):
                        h = 4 * q + t
                        mm = nc.tensor.matmul(bank(g)[:, 64 * h:64 * h + 64], decay[:, q, t * P:(t + 1) * P],
                                              xdt[:, c, 64 * h:64 * h + 64], start=True, stop=True)
                mm.then_inc(misc_done, 1)

            segs(0, "a")
            x_by_token(0)
            for gr in range(4):
                stream(f"za{gr}", (xh, xl))
                y_heads(gr, 0)
                segs(gr, "b")
                g = PL.G[f"yo{gr}"]
                acquire(pe, g)
                pe.wait_ge(xdte_done, gr + 1)
                nc.tensor.matmul(bank(g), cbm[:, gr, P:T], xdte, start=True, stop=True).then_inc(misc_done, 1)
                if gr:
                    group_norm_sum(gr - 1)
                stream(f"zb{gr}", (xh, xl))
                y_heads(gr, 1)
                if gr < 3:
                    segs(gr + 1, "a")
                    x_by_token(gr + 1)
                for c in range(2):
                    g = PL.G[f"yt{gr}"] + c
                    acquire(pe, g)
                    pe.wait_ge(ytok_done[c], gr + 1)
                    for t in range(4):
                        mm = nc.tensor.transpose(bank(g)[:, t * P:(t + 1) * P], ytok[c][:, t * P:(t + 1) * P],
                                                 ident[:, :])
                    mm.then_inc(misc_done, 1)
            group_norm_sum(3)
            stream("so", (yh, yl), lambda k: pe.wait_ge(low_done, k + 1))

            def ffn(f, norm, use, r):
                norm_sum(norm, r)
                stream(f"up{f}", (xh, xl), x_ready(use))
                stream(f"dn{f}", (hh, hl), lambda k: pe.wait_ge(low_done, LOW0 + NF * f + k + 1))

            ffn(0, "n1", 1, 1)
            norm_sum("n2", 2)

            def sums_by_token(name, s, tile, cols):
                g = PL.G[f"{name}{s}"]
                acquire(pe, g)
                n = 2 * cols.shape[-1]
                for t in range(2):
                    pe.wait_ge(*tile(2 * s + t)[0])
                    mm = by_token(bank(g)[:, n * t:n * t + n], tile(2 * s + t)[1], cols)
                mm.then_inc(misc_done, 1)

            def k_squares(h):
                return (kq2_done, 4 * (h // 2) + h % 2 + 1), squares("k", h)

            def q_squares(h):
                return (kq2_done, 4 * (h // 2) + 2 + h % 2 + 1), squares("q", h)

            def o_squares(h):
                return (osq_done, h + 1), kf[:, h, :]

            halves = blk[:, 0:P:64]

            def inverses(name, s, v, done, parts):
                pe.wait_ge(done, s + 1)
                for t in range(2):
                    g = PL.G[f"{name}{s}"] + t
                    acquire(pe, g)
                    over_features(bank(g), v[:, s % 2, 2 * parts * t:2 * parts * t + 2 * parts], parts)\
                        .then_inc(misc_done, 1)

            def transposes(name, A, done, n):
                g = PL.G[name]
                acquire(pe, g)
                pe.wait_ge(done, n)
                for t in range(3):
                    mm = nc.tensor.transpose(bank(g)[:, t * P:(t + 1) * P], A[:, t * P:(t + 1) * P], ident[:, :])
                mm.then_inc(misc_done, 1)

            def scores(h):
                for c in range(2):
                    g = PL.G[f"sc{h}"] + c
                    acquire(pe, g)
                    pe.wait_ge(kqn_done, h + 1)
                    given_back(pe, PL.G[f"q{h//2}"] + h % 2)
                    rows = slice(64 * c, 64 * c + 64)
                    nc.tensor.matmul(bank(g)[:, 0:P], qf[rows, h, 0:P], kf[rows, h, 0:P], start=True, stop=True)
                    nc.tensor.matmul(bank(g)[:, P:384], qf[rows, h, P:T], kf[rows, h, :],
                                     start=True, stop=True).then_inc(misc_done, 1)

            def attend(h):
                transposes(f"at{h}", At[:, h % 2, :], attn_done, h + 1)
                g = PL.G[f"pv{h}"]
                acquire(pe, g)
                pe.wait_ge(vt_done, 2 * (h // 2) + 2)
                given_back(pe, PL.G[f"at{h}"])
                nc.tensor.matmul(bank(g)[:, 0:T], vt[:, 0, P * h:P * h + P], ATt[:, h % 2, 0:T],
                                 start=True, stop=False)
                nc.tensor.matmul(bank(g)[:, P:T], vt[:, 1, P * h:P * h + P], ATt[:, h % 2, T:384],
                                 start=False, stop=True).then_inc(misc_done, 1)

            for s in range(6):
                if s < 4:
                    stream(f"k{s}", (xh, xl), x_ready(2) if s == 0 else None)
                if s >= 3:
                    inverses("or", s - 3, orms, orinv_done, 1)
                if s >= 2:
                    attend(2 * s - 3)
                if 1 <= s < 5:
                    scores(2 * s - 2)
                if s < 4:
                    stream(f"q{s}", (x2h, x2l), x_ready(3) if s == 0 else None)
                if 1 <= s < 5:
                    scores(2 * s - 1)
                if s < 4:
                    sums_by_token("kss", s, k_squares, halves)
                    stream_tok(f"v{s}", (xh, xl))
                    inverses("kr", s, krms, krinv_done, 2)
                if 1 <= s < 5:
                    attend(2 * s - 2)
                if s < 4:
                    sums_by_token("qss", s, q_squares, halves)
                if s >= 2:
                    sums_by_token("os", s - 2, o_squares, ones[:, 0:1])
            inverses("or", 3, orms, orinv_done, 1)
            stream("ao", (oh, ol), lambda k: pe.wait_ge(ol_done, k + 1))
            ffn(1, "n3", 4, 3)
            norm_sum("n4", 4)
            pe.wait_ge(wwi_in, 16)
            g = PL.G["wi"]
            acquire(pe, g)
            for c in range(2):
                for k in range(KD):
                    pe.wait_ge(xs_done, k + 1)
                    mm = nc.tensor.matmul(bank(g)[:, 8 * c:8 * c + 8], xn[:, k, P * c:P * c + P], wwi[:, k, :],
                                          start=(k == 0), stop=(k == KD - 1))
            mm.then_inc(misc_done, 1)
            stream("qb", (xh, xl), x_ready(5))
            stream("kk", (xh, xl))
            b, g = PL.S["kiv"], PL.G["kiv"]
            pe.wait_ge(lo_done, b + 1)
            acquire(pe, g)
            acquire(pe, g + 1)
            for k in range(KD):
                o = k * 256
                mm = mm3(bank(g)[:, 0:T], (wh[:, b % RING, o:o + P], wl[:, b % RING, o:o + P]),
                         (xh[:, k, :], xl[:, k, :]), k == 0, k == KD - 1, False)
            mm.then_inc(half_done, 1)
            for c in range(2):
                for k in range(KD):
                    o = k * 256 + P
                    mm = mm3(bank(g + 1)[:, P * c:P * c + P], (wh[:, b % RING, o:o + P], wl[:, b % RING, o:o + P]),
                             (xh[:, k, P * c:P * c + P], xl[:, k, P * c:P * c + P]), k == 0, k == KD - 1, True)
            mm.then_inc(slab_done, 1)
            stream("qi", (xh, xl))

            def dots(g, q_rows, k_rows):
                acquire(pe, g)
                nc.tensor.matmul(bank(g)[:, 0:P], q_rows[:, 0:P], k_rows[:, 0:P], start=True, stop=True)
                nc.tensor.matmul(bank(g)[:, P:384], q_rows[:, P:T], k_rows, start=True, stop=True)\
                    .then_inc(misc_done, 1)

            pe.wait_ge(qkv2_done, 11)
            for h in range(8):
                rows = slice(64 * (h % 2), 64 * (h % 2) + 64)
                dots(PL.G["ix"] + h, qif[rows, h // 2, :], kif[rows, :])

            def gates(s):
                if s == 0:
                    pe.wait_ge(wri_in, 32)
                for w in range(2):
                    for t in range(2):
                        n = 2 * s + t
                        g = PL.G[f"ri{s}"] + 2 * w + t
                        acquire(pe, g)
                        pe.wait_ge(xrc_done, n + 1)
                        nc.tensor.matmul(bank(g)[:, 0:T], wri[:, w, n * P:(n + 1) * P], xrc[:, n % 4, :],
                                         start=True, stop=True).then_inc(misc_done, 1)

            for s in range(4):
                stream(f"yr{s}", (xh, xl))
                if s:
                    gates(s - 1)
                stream(f"xr{s}", (xh, xl))
            for it in range(9):
                if it < 8:
                    stream(f"{'ga' if it < 4 else 'gb'}{it%4}", (xh, xl))
                if it == 0:
                    gates(3)
                if it >= 1:
                    h = it - 1
                    transposes(f"pt{h}", At2[:, h % 2, :], attn2_done, h + 1)
                    g = PL.G[f"po{h//2}"]
                    if h % 2 == 0:
                        acquire(pe, g)
                    given_back(pe, PL.G[f"pt{h}"])
                    o = bank(g)[64 * (h % 2):64 * (h % 2) + 64, :]
                    kv = h // 4
                    nc.tensor.matmul(o[:, 0:T], v2t[:, 0, 64 * kv:64 * kv + 64], ATt2[:, h % 2, 0:T],
                                     start=True, stop=False)
                    mm = nc.tensor.matmul(o[:, P:T], v2t[:, 1, 64 * kv:64 * kv + 64], ATt2[:, h % 2, T:384],
                                          start=False, stop=True)
                    if h % 2:
                        mm.then_inc(misc_done, 1)
                if it < 8:
                    rows = slice(64 * (it % 2), 64 * (it % 2) + 64)
                    dots(PL.G[f"lg{it}"], q2f[rows, it // 2, :], kkf[rows, it // 4, :])
            stream("woa", (ah, al), lambda k: pe.wait_ge(al_done, k + 1))
            pe.wait_ge(rl_done, 8)
            stream("wor", (rh, rl))
            stream("wout", (mh, ml), lambda k: pe.wait_ge(ml_done, k + 1))
            ffn(2, "n5", 6, 5)
            norm_sum("n6", 6)

        @block.scalar
        def _(act):
            step = Steps(act, act_step)
            A = nc.scalar.activation

            def hi(name, s):
                split_hi(act, PL.S[name] + s + LEAD)

            def square(r, m, g=None):
                if g is None:
                    act.wait_ge(x_in, 16)
                else:
                    given_back(act, g)
                if m >= 2:
                    act.wait_ge(acc_done, 7 * r + max(1, m - 2))
                A(sq[:, m % 2, :], x[:, m, :], ACT.Square).then_inc(sq_done, 1)

            def norm(name, uses, shifts={}):
                g = PL.G[name]
                wait_misc(act, name)
                give_back(A(rms_t, bank(g)[:, 0:2], ACT.Sqrt, scale=1.0 / D, bias=eps_t[:, :]), g)
                for use in uses:
                    xo = (x2h if use == 3 else xh)
                    for m in range(KD):
                        act.wait_ge(xn_done, 8 * use + m + 1)
                        if use in shifts:
                            s0, n0 = shifts[use]
                            A(xn[:, m, :], xn[:, m, :], ACT.Identity, bias=mod[:, s0 + m:s0 + m + 1])\
                                .then_inc(xs_done, 1)
                            act.wait_ge(xs_done, n0 + m + 1)
                        A(xo[:, m, :], xn[:, m, :], ACT.Copy).then_inc(xh_done, 1)

            def residual(name, r, n, last_of):
                A(warm, eps_t[:, :], ACT.Sqrt)
                for s in range(n):
                    if s < n - 1:
                        hi(name, s)
                    for m, g in last_of(s):
                        square(r, m, g)
                hi(name, n - 1)

            def tiles_two(name):
                return lambda s: [(2 * s + t, PL.G[name] + 2 * s + t) for t in range(2)]

            def tiles_pair3(name):
                return lambda s: [(2 * (s // 3) + t, PL.G[name] + 2 * (s // 3) + t) for t in range(2)] if s % 3 == 2 else []

            act.dma_start(vecs[:, :], io["vecs"]).then_inc(vecs_in, 16)
            act.dma_start(lam_in, io["lam"]).then_inc(lam_in_sem, 16)
            act.wait_ge(const_done, NCONST)
            A(warm, eps_t[:, :], ACT.Sqrt)
            for m in range(KD):
                square(0, m)
            split_hi(act, 0)
            norm("n0", [0])
            split_hi(act, 1)
            act.wait_ge(vecs_in, 16)
            A(ea, vec("a_log", 0, 32), ACT.Exp).then_inc(ea_done, 1)
            for b_ in range(2):
                wait_misc(act, "tz", b_)
                give_back(A(bvr[0:8, b_, :], bank(PL.G["tz"] + b_)[0:8, 0:384], ACT.Copy), PL.G["tz"] + b_)
            given_back(act, PL.G["tz"])
            given_back(act, PL.G["tz"] + 1)
            for b_ in range(2):
                act.dma_start(scratch[b_], bvr[0:8, b_, :].rearrange("h (a j) -> h a j", a=1).to_broadcast([8, P, 384]))\
                    .then_inc(tz_out, 16)
            given_back(act, PL.G["dt"])
            step.add(A(sp2, sp1, ACT.Abs))
            step.wait()
            A(sp3, sp2, ACT.Exp, scale=-1.0).then_inc(spe_done, 1)
            act.wait_ge(c_in, 16)
            A(cact[:, :], cact[:, :], ACT.Silu).then_inc(cact_done, 1)

            def xbc_stage(i, j):
                if inside(i, j, 0, 12):
                    split_hi(act, PL.S["xbc"] + j + LEAD, i)
                if inside(i, j, 1, 12):
                    for t in range(2):
                        given_back(act, tile_group("xbc", j - 1, t), i)
                        A(xbc[:, bass.ds(2 * (RING * i + j - 1) + t, 1), :] if not isinstance(i, int)
                          else xbc[:, 2 * (RING * i + j - 1) + t, :],
                          pre[:, 2 * ((j - 1) % RING) + t, :], ACT.Silu).then_inc(xbc_done, 1)
                if inside(i, j, 0, 12):
                    for t in range(2):
                        wait_tile(act, "xbc", i, j, t)
                        c = 2 * (RING * i + j) + t
                        A(pre[:, 2 * (j % RING) + t, :], bank(tile_group("xbc", j, t))[:, 0:T], ACT.Identity,
                          scale=vdyn("conv_w", 3 * 24 + c), bias=vdyn("conv_b", c)).then_inc(pre_done, 1)

            repeat(act, 12, xbc_stage, 1)
            act.wait_ge(tz_out, 32)
            g = PL.G["e12"]
            wait_misc(act, "e12")
            give_back(A(e12, bank(g)[:, 0:64], ACT.Exp), g)

            def exps(gr, part):
                for q in range(2):
                    g = PL.G[f"seg{part}{gr}"] + q
                    wait_misc(act, f"seg{part}{gr}", q)
                    if part == "b":
                        wait_misc(act, f"y0{gr}")
                    elif gr:
                        wait_misc(act, f"y1{gr-1}")
                    give_back(A(decay[:, q, :], bank(g), ACT.Exp), g)

            def group_norm(gr):
                g = PL.G[f"gn{gr}"]
                wait_misc(act, f"gn{gr}")
                give_back(A(grms, bank(g)[:, 0:T], ACT.Sqrt, scale=1.0 / 512, bias=eps_t[:, :]), g)
                for t in range(4):
                    act.wait_ge(yn_done, 4 * gr + t + 1)
                    A(yh[:, 4 * gr + t, :], ynr[:, t % 2, :], ACT.Copy).then_inc(yh_done, 1)

            def silu_z(name, o):
                for t in range(2):
                    wait_tile(act, name, 0, 0, t)
                    give_back(A(zs[:, o + t, :], bank(PL.G[name] + t)[:, 0:T], ACT.Silu), PL.G[name] + t)

            def y_squares(gr):
                if gr:
                    act.wait_ge(low_done, 4 * gr)
                for t in range(4):
                    act.wait_ge(gated_done, 4 * gr + t + 1)
                    A(ysq(t), xbc[:, 4 * gr + t, :], ACT.Square).then_inc(ysq_done, 1)

            for gr in range(4):
                exps(gr, "a")
                hi(f"za{gr}", 0)
                if gr:
                    y_squares(gr - 1)
                silu_z(f"za{gr}", 0)
                g = PL.G[f"y0{gr}"]
                wait_misc(act, f"y0{gr}")
                A(ytok[0], bank(g), ACT.Copy).then_inc(ytok_done[0], 1)
                act.wait_ge(ytok_done[0], gr + 1)
                act.sem_inc(free[g % PRING], 1)
                exps(gr, "b")
                hi(f"zb{gr}", 0)
                if gr:
                    group_norm(gr - 1)
                silu_z(f"zb{gr}", 2)
            y_squares(3)
            group_norm(3)
            step.add(A(lpa, vec("lru", 0, 8), ACT.Abs))
            step.wait()
            A(lp2, lpa, ACT.Exp, scale=-1.0).then_inc(ea_done, 1)
            act.wait_ge(lam_done, 2)
            A(lam4, lam2, ACT.Exp).then_inc(ea_done, 1)
            act.wait_ge(low_done, 16)
            act.dma_start(bt, toeplitz(0, 0, 8)).then_inc(bt_in, 16)
            residual("so", 1, 8, lambda s: [(s, PL.G["so"] + s)])

            def ffn(f, norm_name, uses, shifts, r):
                norm(norm_name, uses, shifts)
                up, dn = f"up{f}", f"dn{f}"

                def stage(i, j):
                    s = RING * i + j
                    if inside(i, j, 0, NF):
                        split_hi(act, PL.S[up] + j + LEAD, i)
                    if inside(i, j, 1, NF):
                        given_back(act, tile_group(up, j - 1, 0), i)
                        A(gsil[:, (j - 1) % RING, :], pre[:, 2 * ((j - 1) % RING), :], ACT.Silu)\
                            .then_inc(gsil_done, 1)
                    if inside(i, j, 2, NF):
                        act.wait_ge(h_done, NF * f + s - 1)
                        dst = hh[:, bass.ds(s - 2, 1), :] if not isinstance(i, int) else hh[:, s - 2, :]
                        A(dst, hbuf[:, (j - 2) % RING, :], ACT.Copy).then_inc(hh_done, 1)
                    if inside(i, j, 0, NF):
                        for t in range(2):
                            wait_tile(act, up, i, j, t)
                            A(pre[:, 2 * (j % RING) + t, :], bank(tile_group(up, j, t))[:, 0:T], ACT.Identity,
                              scale=vdyn(f"up_w{f}", 88 + 2 * s + t), bias=vdyn(f"up_b{f}", 2 * s + t))\
                                .then_inc(pre_done, 1)

                repeat(act, NF, stage, 2)
                residual(dn, r + 1, 12, tiles_pair3(dn))

            ffn(0, "n1", [1], {}, 1)
            norm("n2", [2, 3])

            def kq_tiles(what, s, dst):
                name = f"{what}{s}"
                hi(name, 0)
                for t in range(2):
                    m, g = 2 * s + t, PL.G[name] + t
                    wait_tile(act, name, 0, 0, t)
                    if what == "q" and s == 3:
                        act.wait_ge(ol_done, 2)
                    A(squares(what, m), bank(g)[:, 0:T], ACT.Square).then_inc(kq2_done, 1)
                    give_back(A(dst[:, m, :], bank(g)[:, 0:T], ACT.Copy,
                                scale=1.0 if what == "k" else vec("q_norm")), g)

            def head_rms(name, s, v, cols, n):
                g = PL.G[f"{name}{s}"]
                wait_misc(act, f"{name}{s}")
                give_back(A(v[:, s % 2, :], bank(g)[:, 0:cols], ACT.Sqrt, scale=1.0 / n, bias=eps_t[:, :]), g)

            def exp_rows(lg, q, row, n, sums_):
                for i in range(2):
                    cols = slice(0, P) if i == 0 else slice(P, 384)
                    A(lg[:, cols], lg[:, cols], ACT.Exp, scale=-1.0, bias=mins[:, q, row + i:row + i + 1],
                      accum_out=sums_[:, row + i:row + i + 1]).then_inc(n, 1)

            def exps1(h):
                q = h % 2
                for c in range(2):
                    act.wait_ge(min_done, 4 * h + 2 * c + 2)
                    exp_rows(logit[:, 2 * q + c, :], q, 2 * c, exp_done, sums[:, q, :])

            def attend(h):
                g = PL.G[f"at{h}"]
                wait_misc(act, f"at{h}")
                give_back(A(ATt[:, h % 2, :], bank(g)[:, 0:384], ACT.Copy), g)
                g = PL.G[f"pv{h}"]
                wait_misc(act, f"pv{h}")
                A(kf[:, h, :], bank(g)[:, 0:T], ACT.Square).then_inc(osq_done, 1)
                give_back(A(qf[:, h, :], bank(g)[:, 0:T], ACT.Copy), g)

            def output_high(s):
                for h in (2 * s, 2 * s + 1):
                    act.wait_ge(on_done, h + 1)
                    A(oh[:, h, :], qf[:, h, :], ACT.Copy).then_inc(oh_done, 1)

            for s in range(6):
                if s < 4:
                    kq_tiles("k", s, kf)
                if s >= 3:
                    output_high(s - 3)
                if s >= 2:
                    attend(2 * s - 3)
                if 1 <= s < 5:
                    exps1(2 * s - 2)
                if s < 4:
                    kq_tiles("q", s, qf)
                if 1 <= s < 5:
                    exps1(2 * s - 1)
                if s < 4:
                    head_rms("kss", s, krms, 8, 64)
                    name = f"v{s}"
                    hi(name, 0)
                    for t in range(2):
                        g = PL.G[name] + t
                        wait_tile(act, name, 0, 0, t)
                        A(vt[:, t, 256 * s:256 * s + 256], bank(g)[:, 0:256], ACT.Copy).then_inc(vt_done, 1)
                        act.wait_ge(vt_done, 2 * s + t + 1)
                        act.sem_inc(free[g % PRING], 1)
                if 1 <= s < 5:
                    attend(2 * s - 2)
                if s < 4:
                    head_rms("qss", s, qrms, 8, 64)
                if s >= 2:
                    head_rms("os", s - 2, orms, 4, P)
                if s == 5:
                    output_high(3)
            residual("ao", 3, 4, tiles_two("ao"))
            ffn(1, "n3", [4], {}, 3)
            norm("n4", [5], {5: (0, 0)})
            for name, n in (("qb", 2), ("kk", 1), ("kiv", 1), ("qi", 2)):
                for s in range(n):
                    hi(name, s)
                    for t in range(2):
                        m, g = 2 * s + t, PL.G[name] + 2 * s + t
                        wait_tile(act, name, 0, s, t)
                        if name == "kiv" and t == 1:
                            continue
                        dst = {"qb": q2f, "kk": kkf, "qi": qif}[name][:, m, :] if name != "kiv" else kif
                        bias = {"qb": "b_q", "kk": "b_kk", "qi": "b_qi", "kiv": "b_ki"}[name]
                        A(dst, bank(g)[:, 0:T], ACT.Identity, bias=vec(bias, m)).then_inc(qkv2_done, 1)
                        act.wait_ge(qkv2_done, {"qb": 0, "kk": 4, "kiv": 6, "qi": 7}[name] + m + 1)
                        act.sem_inc(free[g % PRING], 1)
            for h in range(8):
                g = PL.G["ix"] + h
                wait_misc(act, "ix", h)
                if h >= 2:
                    act.wait_ge(score_step, 2 * (h - 1))
                give_back(A(rel[:, h % 2, :], bank(g)[:, 0:384], ACT.Relu, scale=64 ** -0.5), g)
            def lru(s):
                for w in range(2):
                    for t in range(2):
                        g = PL.G[f"ri{s}"] + 2 * w + t
                        wait_misc(act, f"ri{s}", 2 * w + t)
                        if s:
                            act.wait_ge(scan_done, 2 * s)
                        dst, bias = ((rg, "b_rg"), (ig, "b_ig"))[w]
                        give_back(A(dst[:, t, :], bank(g)[:, 0:T], ACT.Sigmoid, bias=vec(bias, 2 * s + t)), g)
                for t in range(2):
                    n = 2 * s + t
                    given_back(act, PL.G[f"ri{s}"] + t)
                    A(lra[:, t, :], rg[:, t, :], ACT.Exp, scale=negc[:, n:n + 1]).then_inc(lra_done, 1)
                    A(rg[:, t, :], rg[:, t, :], ACT.Tanh, scale=posc[:, n:n + 1]).then_inc(tanh_done, 1)
                for t in range(2):
                    act.wait_ge(m2_done, 2 * s + t + 1)
                    A(lrm[:, t, :], lrm[:, t, :], ACT.Sqrt).then_inc(mult_done, 1)
                for t in range(2):
                    act.wait_ge(rnn_done, 2 * s + t + 1)
                    A(rh[:, 2 * s + t, :], lrh[:, t, :], ACT.Copy).then_inc(rh_done, 1)

            act.dma_start(bt2[0], toeplitz(1, 0, 4)).then_inc(bt2_in[0], 16)
            for s in range(4):
                hi(f"yr{s}", 0)
                for t in range(2):
                    m, g = 2 * s + t, PL.G[f"yr{s}"] + t
                    wait_tile(act, f"yr{s}", 0, 0, t)
                    give_back(A(gyr[:, m, :], bank(g)[:, 0:T], ACT.Gelu_apprx_tanh, bias=vec("b_yr", m)), g)
                name = f"xr{s}"
                hi(name, 0)
                if s:
                    lru(s - 1)
                for t in range(2):
                    n = 2 * s + t
                    g = PL.G[name] + t
                    wait_tile(act, name, 0, 0, t)
                    if s:
                        act.wait_ge(xrc_done, 2 * s)
                    A(xrraw[:, t, :], bank(g)[:, 0:T], ACT.Identity, bias=vec("b_xr", n)).then_inc(xrraw_done, 1)
                    act.wait_ge(xrraw_done, n + 1)
                    act.sem_inc(free[g % PRING], 1)
                    A(xrc[:, n % 4, :], xrraw[:, t, :], ACT.Identity, scale=vec("rnn_w", 24 + n),
                      bias=vec("rnn_b", n)).then_inc(prer_done, 1)
            for it in range(9):
                if it < 8:
                    name, dst, bias = ("ga", gaf, "b_ga") if it < 4 else ("gb", gbf, "b_gb")
                    name = f"{name}{it%4}"
                    for t in range(2):
                        m, g = 2 * (it % 4) + t, PL.G[name] + t
                        wait_tile(act, name, 0, 0, t)
                        give_back(A(dst[:, m, :], bank(g)[:, 0:T], ACT.Tanh, scale=0.5, bias=vec(bias, m)), g)
                if it >= 1:
                    h = it - 1
                    g = PL.G[f"pt{h}"]
                    wait_misc(act, f"pt{h}")
                    give_back(A(ATt2[:, h % 2, :], bank(g)[:, 0:384], ACT.Copy), g)
                    if h % 2:
                        wait_misc(act, f"po{h//2}")
                        A(ah[:, h // 2, :], bank(PL.G[f"po{h//2}"])[:, 0:T], ACT.Copy).then_inc(ah_done, 1)
                if it < 8:
                    hi(name, 0)
                    if it == 0:
                        lru(3)
                        act.dma_start(bt2[1], toeplitz(1, 4, 4)).then_inc(bt2_in[1], 16)
                    q = it % 2
                    act.wait_ge(min2_done, 2 * it + 2)
                    exp_rows(logit2[:, q, :], q, 0, exp2_done, sums[:, q, :])
            for s in range(2):
                hi("woa", s)
            for s in range(4):
                hi("wor", s)
                for t in range(2):
                    m = 2 * s + t
                    act.wait_ge(merged_done, m + 1)
                    A(mh[:, m, :], gaf[:, m, :], ACT.Copy).then_inc(mh_done, 1)
            residual("wout", 5, 4, tiles_two("wout"))
            ffn(2, "n5", [6], {6: (24, 8)}, 5)
            norm("n6", [])

        @block.vector
        def _(dve):
            step = Steps(dve, dve_step)
            V = nc.vector

            def lo(name, s):
                ada(name, s)
                split_lo(dve, PL.S[name] + s + LEAD)
                ada(name, s)

            ada_n = [0]

            def ada(name, s):
                if s < ADA.get(name, 0):
                    a = ada_n[0]
                    ada_n[0] += 1
                    half, w = a % 2, ada_w[:, a % ARING, :]
                    if a == 0:
                        dve.wait_ge(cact_done, 1)
                    dve.wait_ge(ada_in[a % ARING], 16 * (a // ARING + 1))
                    V.tensor_tensor_reduce(out=w, in0=w, in1=cact[:, 512 * half:512 * half + 512], scale=1.0,
                                           scalar=0.0, op0=ALU.mult, op1=ALU.add,
                                           accum_out=ada_sum[:, a:a + 1]).then_inc(ada_used, 1)

            def accumulate(r, m):
                if m == 0:
                    return
                dve.wait_ge(sq_done, 8 * r + m + 1)
                if m == 1:
                    V.tensor_tensor(acc, sq[:, 0, :], sq[:, 1, :], ALU.add).then_inc(acc_done, 1)
                else:
                    dve.wait_ge(acc_done, 7 * r + m - 1)
                    V.tensor_tensor(acc, acc, sq[:, m % 2, :], ALU.add).then_inc(acc_done, 1)

            def norm(name, use_gains, k, late=None):
                g = PL.G[name] + 1
                given_back(dve, g - 1)
                V.reciprocal(rinv_t, rms_t).then_inc(rstd_done, 1)
                wait_misc(dve, name, 1)
                for use, gain, shift in use_gains:
                    h_, l_ = (x2h, x2l) if use == 3 else (xh, xl)

                    def low(m):
                        dve.wait_ge(xh_done, 8 * use + m + 1)
                        V.tensor_tensor(l_[:, m, :], xn[:, m, :], h_[:, m, :].bitcast(F32), ALU.subtract)\
                            .then_inc(xl_done, 1)

                    for m in range(KD):
                        if use == 3:
                            dve.wait_ge(xl_done, 8 * 2 + m + 1)
                        V.scalar_tensor_tensor(xn[:, m, :], x[:, m, :], gain(m), bank(g)[:, 0:T],
                                               ALU.mult, ALU.mult).then_inc(xn_done, 1)
                        if m and use < 7:
                            low(m - 1)
                    if use < 7:
                        low(KD - 1)
                    if late:
                        lo(*late)
                        late = None
                dve.wait_ge(xn_done, 8 * use_gains[-1][0] + KD)
                dve.sem_inc(free[g % PRING], 1)

            def residual(name, r, n, tiles, scale=None):
                for s in range(n):
                    if s < n - 1:
                        lo(name, s)
                    for m, g, t, cnt in tiles(s):
                        wait_tile(dve, name, s // RING, s % RING, t, cnt)
                        if scale is None:
                            ins = V.tensor_tensor(x[:, m, :], bank(g)[:, 0:T], x[:, m, :], ALU.add)
                        else:
                            ins = V.scalar_tensor_tensor(x[:, m, :], bank(g)[:, 0:T], scale(m), x[:, m, :],
                                                         ALU.mult, ALU.add)
                        give_back(ins, g)
                        if m:
                            accumulate(r, m - 1)
                accumulate(r, 7)

            def tiles_two(name):
                return lambda s: [(2 * s + t, PL.G[name] + 2 * s + t, t, 2) for t in range(2)]

            def residual3(name, r, scale=None):
                for s in range(12):
                    if s < 11:
                        lo(name, s)
                    if s % 3 == 2:
                        p = s // 3
                        for t in range(2):
                            m, g = 2 * p + t, PL.G[name] + 2 * p + t
                            if t:
                                dve.wait_ge(slab_done, PL.S[name] + s + 1)
                            else:
                                dve.wait_ge(half_done, PL.H[name] + p + 1)
                            if scale is None:
                                ins = V.tensor_tensor(x[:, m, :], bank(g)[:, 0:T], x[:, m, :], ALU.add)
                            else:
                                ins = V.scalar_tensor_tensor(x[:, m, :], bank(g)[:, 0:T], scale(m), x[:, m, :],
                                                             ALU.mult, ALU.add)
                            give_back(ins, g)
                            if m:
                                accumulate(r, m - 1)
                accumulate(r, 7)

            def softplus(v, e, w, w2, p):
                step.add(V.tensor_scalar(w, e, 2.0, None, ALU.add))
                step.wait()
                step.add(V.reciprocal(w2, w))
                step.wait()
                step.add(V.tensor_tensor(w, e, w2, ALU.mult))
                step.wait()
                step.add(V.tensor_tensor(w2, w, w, ALU.mult))
                step.wait()
                step.add(V.tensor_scalar(p, w2, 1.0 / 15, None, ALU.mult))
                for n in (13, 11, 9, 7, 5, 3):
                    step.wait()
                    step.add(V.scalar_tensor_tensor(p, p, 1.0 / n, w2, ALU.add, ALU.mult))
                step.wait()
                step.add(V.scalar_tensor_tensor(p, p, 1.0, w, ALU.add, ALU.mult))
                step.add(V.tensor_scalar(e, v, 0.0, None, ALU.max))
                step.wait()
                step.add(V.scalar_tensor_tensor(e, p, 2.0, e, ALU.mult, ALU.add))
                step.wait()

            for m in range(KD):
                accumulate(0, m)
            split_lo(dve, 0)
            dve.wait_ge(vecs_in, 16)
            norm("n0", [(0, lambda m: vec("ssm_ln", m), None)], 0)
            split_lo(dve, 1)
            lamv = lam_in
            dve.wait_ge(lam_in_sem, 16)
            for c in range(2):
                step.add(V.tensor_tensor(ytok[0][:, 64 * c:64 * c + 64], lamv[:, 2 * c, :], lamv[:, 2 * c + 1, :],
                                         ALU.mult))
            step.wait()
            for c in range(2):
                V.tensor_reduce(lam2[:, c:c + 1], ytok[0][:, 64 * c:64 * c + 64], AX.X, ALU.add).then_inc(lam_done, 1)
            g = PL.G["dt"]
            wait_misc(dve, "dt")
            give_back(V.tensor_tensor(sp1.rearrange("p (c h) -> p c h", c=2),
                                      bank(g)[:, 0:64].rearrange("p (c h) -> p c h", c=2),
                                      vec("dt_bias", 0, 32).rearrange("p (c h) -> p c h", c=1).to_broadcast([P, 2, 32]),
                                      ALU.add), g)
            given_back(dve, g)
            dve.wait_ge(spe_done, 1)
            softplus(sp1, sp3, sp2, sp4, dt_t.rearrange("p c h -> p (c h)"))
            step.add(V.tensor_copy(dt_t.rearrange("p c h -> p (c h)"), sp3))
            dve.wait_ge(ea_done, 1)
            step.wait()
            V.scalar_tensor_tensor(a_t, dt_t, -1.0, ea.rearrange("p (c h) -> p c h", c=1).to_broadcast([P, 2, 32]),
                                   ALU.mult, ALU.mult).then_inc(a_done, 1)

            def tap(dst, src, w, d):
                return V.scalar_tensor_tensor(dst[:, d:T], src[:, 0:T - d], w, dst[:, d:T], ALU.mult, ALU.add)

            def xbc_stage(i, j):
                split_lo(dve, PL.S["xbc"] + j + LEAD, i)
                s = RING * i + j
                for d in (1, 2, 3):
                    for t in range(2):
                        dst = pre[:, 2 * (j % RING) + t, :]
                        src = bank(tile_group("xbc", j, t))
                        if d == 1:
                            dve.wait_ge(pre_done, 2 * s + t + 1)
                        else:
                            dve.wait_ge(conv_step, 4 * s + 2 * (d - 2) + t + 1)
                        ins = tap(dst, src, vdyn("conv_w", 24 * (3 - d) + 2 * s + t), d)
                        if d == 3:
                            give_back(ins, tile_group("xbc", j, t))
                        else:
                            ins.then_inc(conv_step, 1)

            repeat(dve, 12, xbc_stage)
            for gr in range(4):
                g = PL.G["cb"] + gr
                wait_misc(dve, "cb", gr)
                give_back(V.tensor_tensor(cbm[:, gr, :], bank(g)[:, 0:384],
                                          tri[:, :, :].rearrange("p a b -> p (a b)"), ALU.mult), g)
            for gr in range(4):
                given_back(dve, PL.G["cb"] + gr)

            def heads(a):
                return a.rearrange("p (h c) -> p h c", c=64)

            def over(v):
                return v.rearrange("p (h c) -> p h c", c=1).to_broadcast([P, 8, 64])

            def group_norm(gr):
                given_back(dve, PL.G[f"gn{gr}"])
                V.reciprocal(grst, grms).then_inc(grst_done, 1)
                dve.wait_ge(grst_done, gr + 1)

                def low(t):
                    m = 4 * gr + t
                    dve.wait_ge(yh_done, m + 1)
                    V.tensor_tensor(yl[:, m, :], ynr[:, t % 2, :], yh[:, m, :].bitcast(F32), ALU.subtract)\
                        .then_inc(low_done, 1)

                for t in range(4):
                    m = 4 * gr + t
                    if m >= 2:
                        dve.wait_ge(low_done, m - 1)
                    V.scalar_tensor_tensor(ynr[:, t % 2, :], xbc[:, m, :], vec("ssm_norm", m), grst,
                                           ALU.mult, ALU.mult).then_inc(yn_done, 1)
                    if t:
                        low(t - 1)
                low(3)

            def seg_weights(gr, c):
                for q in range(2):
                    if c or gr:
                        wait_misc(dve, f"sega{gr}" if c else f"segb{gr-1}", q)
                    for t in range(4):
                        h = 8 * gr + 4 * q + t
                        V.tensor_scalar(segl[:, 4 * q + t, :], later[:, :], a_t[:, c, h:h + 1], None, ALU.mult)\
                            .then_inc(segl_done, 1)

            def decays(gr, c):
                for q in range(2):
                    given_back(dve, PL.G[f"seg{'ab'[c]}{gr}"] + q)
                    m = cbm[:, gr, 2 * P * c:2 * P * c + P].rearrange("p (a b) -> p a b", a=1).to_broadcast([P, 4, P])
                    d4 = decay[:, q, :].rearrange("p (a b) -> p a b", a=4)
                    V.tensor_tensor(d4, d4, m, ALU.mult).then_inc(decay_done, 1)

            dve.wait_ge(a_done, 1)
            given_back(dve, PL.G["e12"])
            def x_dt(gr):
                for c in range(2):
                    g = PL.G[f"xt{gr}"] + c
                    wait_misc(dve, f"xt{gr}", c)
                    give_back(V.tensor_tensor(heads(xdt[:, c, :]), heads(bank(g)), over(dt_t[:, c, 8 * gr:8 * gr + 8]),
                                              ALU.mult), g)
                given_back(dve, PL.G[f"xt{gr}"])
                V.tensor_tensor(heads(xdte), heads(xdt[:, 0, :]), over(e12[:, 8 * gr:8 * gr + 8]), ALU.mult)\
                    .then_inc(xdte_done, 1)

            seg_weights(0, 0)
            x_dt(0)
            for gr in range(4):
                lo(f"za{gr}", 0)
                decays(gr, 0)
                seg_weights(gr, 1)
                decays(gr, 1)
                g = PL.G[f"yo{gr}"]
                wait_misc(dve, f"yo{gr}")
                give_back(V.tensor_tensor(heads(yoffs), heads(bank(g)), over(e12[:, 32 + 8 * gr:40 + 8 * gr]),
                                          ALU.mult), g)
                if gr < 3:
                    seg_weights(gr + 1, 0)
                lo(f"zb{gr}", 0)
                if gr:
                    group_norm(gr - 1)
                given_back(dve, g)
                g = PL.G[f"y1{gr}"]
                wait_misc(dve, f"y1{gr}")
                V.tensor_tensor(ytok[1], bank(g), yoffs, ALU.add).then_inc(ytok_done[1], 1)
                dve.wait_ge(ytok_done[1], gr + 1)
                dve.sem_inc(free[g % PRING], 1)
                if gr < 3:
                    x_dt(gr + 1)
                for c in range(2):
                    g = PL.G[f"yt{gr}"] + c
                    wait_misc(dve, f"yt{gr}", c)
                    for t in range(4):
                        m = 4 * gr + t
                        y_ = xbc[:, m, c * P:(c + 1) * P]
                        ins = V.scalar_tensor_tensor(y_, y_, vec("ssm_d", m), bank(g)[:, t * P:(t + 1) * P],
                                                     ALU.mult, ALU.add)
                        if t == 3:
                            give_back(ins, g)
                        else:
                            step.add(ins)
                step.wait()
                for c in range(2):
                    given_back(dve, PL.G[f"yt{gr}"] + c)
                for t in range(4):
                    given_back(dve, PL.G[f"z{'aabb'[t]}{gr}"] + t % 2)
                    V.tensor_tensor(xbc[:, 4 * gr + t, :], xbc[:, 4 * gr + t, :], zs[:, t, :], ALU.mult)\
                        .then_inc(gated_done, 1)
            dve.wait_ge(gated_done, 16)
            group_norm(3)
            step.add(V.tensor_scalar(lp1, vec("lru", 0, 8), -1.0, None, ALU.mult))
            dve.wait_ge(ea_done, 2)
            step.wait()
            softplus(lp1, lp2, lp3, lp4, posc)
            step.add(V.tensor_scalar(negc, lp2, -8.0, None, ALU.mult))
            step.add(V.tensor_scalar(posc, lp2, 8.0, None, ALU.mult))
            dve.wait_ge(ea_done, 3)
            step.add(V.tensor_tensor(negl, lam4[:, 1:2], lam4[:, 0:1], ALU.subtract))
            step.wait()
            step.add(V.tensor_scalar(negl, negl, -LAM_INIT, None, ALU.add))
            step.add(V.tensor_scalar(sgs, vec("subln"), 1.0 - LAM_INIT, None, ALU.mult))
            residual("so", 1, 8, lambda s: [(s, PL.G["so"] + s, 0, 1)])

            def ffn(f, norm_args, r, scale=None):
                norm(*norm_args)
                up, dn = f"up{f}", f"dn{f}"
                pre0 = 24 + 44 * f
                cs0 = 4 * 12 + 2 * NF * f

                def stage(i, j):
                    s = RING * i + j
                    if inside(i, j, 0, NF):
                        split_lo(dve, PL.S[up] + j + LEAD, i)
                    if inside(i, j, 1, NF):
                        dve.wait_ge(gsil_done, NF * f + s)
                        given_back(dve, tile_group(up, j - 1, 1), i)
                        if not isinstance(i, int) or s >= 4:
                            dve.wait_ge(low_done, LOW0 + NF * f + s - 3)
                        V.tensor_tensor(hbuf[:, (j - 1) % RING, :], gsil[:, (j - 1) % RING, :],
                                        pre[:, 2 * ((j - 1) % RING) + 1, :], ALU.mult).then_inc(h_done, 1)
                    if inside(i, j, 2, NF):
                        dve.wait_ge(hh_done, NF * f + s - 1)
                        at = s - 2
                        dst = hl[:, bass.ds(at, 1), :] if not isinstance(i, int) else hl[:, at, :]
                        src = hh[:, bass.ds(at, 1), :] if not isinstance(i, int) else hh[:, at, :]
                        V.tensor_tensor(dst, hbuf[:, (j - 2) % RING, :], src.bitcast(F32), ALU.subtract)\
                            .then_inc(low_done, 1)
                    if inside(i, j, 0, NF):
                        for d in (1, 2):
                            for t in range(2):
                                if d == 1:
                                    dve.wait_ge(pre_done, pre0 + 2 * s + t + 1)
                                else:
                                    dve.wait_ge(conv_step, cs0 + 2 * s + t + 1)
                                ins = tap(pre[:, 2 * (j % RING) + t, :], bank(tile_group(up, j, t)),
                                          vdyn(f"up_w{f}", 44 * (2 - d) + 2 * s + t), d)
                                if d == 2:
                                    give_back(ins, tile_group(up, j, t))
                                else:
                                    ins.then_inc(conv_step, 1)

                repeat(dve, NF, stage, 2)
                residual3(dn, r + 1, scale)

            ffn(0, ("n1", [(1, lambda m: vec("ffn_ln0", m), None)], 1, ("so", 7)), 1)
            norm("n2", [(2, lambda m: vec("kv_ln", m), None), (3, lambda m: vec("attn_ln", m), None)], 2, ("dn0", 11))

            def inverse_rms(name, s, v, done=None):
                given_back(dve, PL.G[f"{name}{s}"])
                ins = V.reciprocal(v[:, s % 2, :], v[:, s % 2, :])
                if done is None:
                    step.add(ins)
                    step.wait()
                else:
                    ins.then_inc(done, 1)

            def head_norm(name, s, f, gain, done):
                for t in range(2):
                    h, g = 2 * s + t, PL.G[f"{name}{s}"] + t
                    wait_misc(dve, f"{name}{s}", t)
                    V.scalar_tensor_tensor(f[:, h, :], f[:, h, :], gain, bank(g)[:, 0:T], ALU.mult, ALU.mult)\
                        .then_inc(done, 1)
                    dve.wait_ge(done, h + 1)
                    dve.sem_inc(free[g % PRING], 1)

            def q_norm(s):
                inverse_rms("qss", s, qrms)
                step.add(V.tensor_scalar(qrms[:, s % 2, :], qrms[:, s % 2, :], -(64 ** -0.5), None, ALU.mult))
                step.wait()

            def output_low(s):
                for t in range(2):
                    h = 2 * s + t
                    dve.wait_ge(oh_done, h + 1)
                    V.tensor_tensor(ol[:, h, :], qf[:, h, :], oh[:, h, :].bitcast(F32), ALU.subtract)\
                        .then_inc(ol_done, 1)

            def negated(lg, g, bias, factors):
                step.add(V.scalar_tensor_tensor(lg[:, 0:P], bank(g)[:, 0:P], factors[0], bias[:, P:T],
                                                ALU.mult, ALU.subtract))
                return V.scalar_tensor_tensor(lg[:, P:384], bank(g)[:, P:384], factors[1], bias,
                                              ALU.mult, ALU.subtract)

            def row_mins(lg, q, row, done):
                for i in range(2):
                    cols = slice(0, P) if i == 0 else slice(P, 384)
                    V.tensor_reduce(mins[:, q, row + i:row + i + 1], lg[:, cols], AX.X, ALU.min).then_inc(done, 1)

            def scores(h):
                q = h % 2
                if h == 0:
                    dve.wait_ge(bt_in, 16)
                    dve.wait_ge(xl_done, 8 * 4)
                for c in range(2):
                    g = PL.G[f"sc{h}"] + c
                    lg = logit[:, 2 * q + c, :]
                    if h >= 2:
                        dve.wait_ge(attn_done, h - 1)
                    wait_misc(dve, f"sc{h}", c)
                    o = 4 * (h % 2) + c
                    give_back(negated(lg, g, bt[:, h, :], [qrms[:, h // 2 % 2, o + 2 * b_:o + 2 * b_ + 1]
                                                           for b_ in range(2)]), g)
                    step.wait()
                    given_back(dve, g)
                    row_mins(lg, q, 2 * c, min_done)

            def combine(h):
                q = h % 2
                dve.wait_ge(exp_done, 4 * (h + 1))
                step.add(V.reciprocal(recs[:, q, :], sums[:, q, :]))
                step.wait()
                step.add(V.tensor_scalar(coef[:, q, :], recs[:, q, 2:4], negl, None, ALU.mult))
                if h >= 2:
                    wait_misc(dve, f"at{h-2}")
                for i in range(2):
                    cols = slice(0, P) if i == 0 else slice(P, 384)
                    step.add(V.tensor_scalar(At[:, q, cols], logit[:, 2 * q, cols], recs[:, q, i:i + 1], None,
                                             ALU.mult))
                step.wait()
                for i in range(2):
                    cols = slice(0, P) if i == 0 else slice(P, 384)
                    ins = V.scalar_tensor_tensor(At[:, q, cols], logit[:, 2 * q + 1, cols], coef[:, q, i:i + 1],
                                                 At[:, q, cols], ALU.mult, ALU.add)
                    if i:
                        ins.then_inc(attn_done, 1)
                    else:
                        step.add(ins)

            for s in range(6):
                if s < 4:
                    lo(f"k{s}", 0)
                if s >= 3:
                    head_norm("or", s - 3, qf, sgs, on_done)
                    output_low(s - 3)
                if 1 <= s < 5:
                    scores(2 * s - 2)
                if s < 4:
                    lo(f"q{s}", 0)
                if 1 <= s < 5:
                    scores(2 * s - 1)
                    combine(2 * s - 2)
                if s < 4:
                    inverse_rms("kss", s, krms, krinv_done)
                    lo(f"v{s}", 0)
                if 1 <= s < 5:
                    combine(2 * s - 1)
                if s < 4:
                    head_norm("kr", s, kf, vec("k_norm"), kqn_done)
                    q_norm(s)
                if s >= 2:
                    inverse_rms("os", s - 2, orms, orinv_done)
            head_norm("or", 3, qf, sgs, on_done)
            output_low(3)
            residual("ao", 3, 4, tiles_two("ao"))
            ffn(1, ("n3", [(4, lambda m: vec("ffn_ln1", m), None)], 3, ("ao", 3)), 3)
            dve.wait_ge(ada_used, 96)
            halves = ada_sum[:, :].rearrange("p (n two) -> p n two", two=2)
            step.add(V.tensor_tensor(mod, halves[:, :, 0], vec("b_ada", 0, 48), ALU.add))
            step.wait()
            step.add(V.tensor_tensor(mod, mod, halves[:, :, 1], ALU.add))
            step.wait()
            step.add(V.scalar_tensor_tensor(gs1, mod[:, 8:16], 1.0, vec("g_mix", 0, 8), ALU.add, ALU.mult))
            step.add(V.tensor_scalar(vec("b_ga", 0, 16), vec("b_ga", 0, 16), 0.5, None, ALU.mult))
            step.add(V.tensor_scalar(mod[:, 16:24], mod[:, 16:24], 0.5, None, ALU.mult))
            step.add(V.scalar_tensor_tensor(gs2, mod[:, 32:40], 1.0, vec("g_ffn", 0, 8), ALU.add, ALU.mult))
            step.wait()
            norm("n4", [(5, lambda m: gs1[:, m:m + 1], None)], 4, ("dn1", 11))
            g = PL.G["wi"]
            wait_misc(dve, "wi")
            give_back(V.tensor_tensor(wi_s, bank(g)[:, 0:16].rearrange("p (c h) -> p c h", c=2),
                                      vec("b_wi", 0, 8).rearrange("p (c h) -> p c h", c=1).to_broadcast([P, 2, 8]),
                                      ALU.add), g)
            given_back(dve, g)
            step.add(V.tensor_scalar(wi_s, wi_s, 8 ** -0.5, None, ALU.mult))
            for name, n in (("qb", 2), ("kk", 1)):
                for s in range(n):
                    lo(name, s)
            lo("kiv", 0)
            g = PL.G["kiv"] + 1
            wait_tile(dve, "kiv", 0, 0, 1)
            V.tensor_tensor(v2t, bank(g)[:, 0:T].rearrange("p (c h) -> p c h", c=2),
                            vec("b_v", 0, P).rearrange("p (c h) -> p c h", c=1).to_broadcast([P, 2, P]),
                            ALU.add).then_inc(qkv2_done2, 1)
            dve.wait_ge(qkv2_done2, 1)
            dve.sem_inc(free[g % PRING], 1)
            for s in range(2):
                lo("qi", s)
            step.wait()
            for h in range(8):
                given_back(dve, PL.G["ix"] + h)
                if h:
                    dve.wait_ge(score_step, 2 * h)
                for i in range(2):
                    cols = slice(0, P) if i == 0 else slice(P, 384)
                    if h == 0:
                        ins = V.tensor_scalar(score[:, 0, cols], rel[:, 0, cols], wi_s[:, i, 0:1], None, ALU.mult)
                    else:
                        ins = V.scalar_tensor_tensor(score[:, 0, cols], rel[:, h % 2, cols], wi_s[:, i, h:h + 1],
                                                     score[:, 0, cols], ALU.mult, ALU.add)
                    ins.then_inc(score_step, 1)
            dve.wait_ge(score_step, 16)
            dve.wait_ge(mask_done, 1)
            step.add(V.tensor_tensor(score[:, 0, 0:P], score[:, 0, 0:P], mneg[:, P:T], ALU.add))
            step.add(V.tensor_tensor(score[:, 0, P:384], score[:, 0, P:384], mneg, ALU.add))
            step.wait()

            def take(i, r):
                cols = slice(0, P) if i == 0 else slice(P, 384)
                m = m8s[:, i, :]
                step.add(V.max(m, score[:, r % 2, cols]))
                step.wait()
                step.add(V.match_replace(score[:, (r + 1) % 2, cols], m, score[:, r % 2, cols], TAKEN))
                step.wait()

            def top(first, last):
                for r in range(first, last):
                    for i in range(2):
                        take(i, r)


            def lru(s):
                for t in range(2):
                    n = 2 * s + t
                    dve.wait_ge(lra_done, n + 1)
                    step.add(V.tensor_tensor(lrm[:, t, :], lra[:, t, :], lra[:, t, :], ALU.mult))
                step.wait()
                for t in range(2):
                    n = 2 * s + t
                    dve.wait_ge(tanh_done, n + 1)
                    V.scalar_tensor_tensor(lrm[:, t, :], lrm[:, t, :], 1.0, rg[:, t, :], ALU.add, ALU.mult)\
                        .then_inc(m2_done, 1)
                for t in range(2):
                    n = 2 * s + t
                    given_back(dve, PL.G[f"ri{s}"] + 2 + t)
                    step.add(V.tensor_tensor(ig[:, t, :], ig[:, t, :], xrc[:, n % 4, :], ALU.mult))
                step.wait()
                for t in range(2):
                    n = 2 * s + t
                    dve.wait_ge(mult_done, n + 1)
                    step.add(V.tensor_tensor(ig[:, t, :], ig[:, t, :], lrm[:, t, :], ALU.mult))
                step.wait()
                for t in range(2):
                    V.tensor_tensor_scan(lrh[:, t, :], lra[:, t, :], ig[:, t, :], 0.0, ALU.mult, ALU.add)\
                        .then_inc(scan_done, 1)
                for t in range(2):
                    n = 2 * s + t
                    dve.wait_ge(scan_done, n + 1)
                    given_back(dve, PL.G[f"yr{s}"] + t)
                    V.tensor_tensor(lrh[:, t, :], lrh[:, t, :], gyr[:, n, :], ALU.mult).then_inc(rnn_done, 1)
                for t in range(2):
                    n = 2 * s + t
                    dve.wait_ge(rh_done, n + 1)
                    V.tensor_tensor(rl[:, n, :], lrh[:, t, :], rh[:, n, :].bitcast(F32), ALU.subtract)\
                        .then_inc(rl_done, 1)

            for s in range(4):
                lo(f"yr{s}", 0)
                if s == 0:
                    top(0, 4)
                lo(f"xr{s}", 0)
                if s:
                    lru(s - 1)
                for d in (1, 2, 3):
                    for t in range(2):
                        n = 2 * s + t
                        if d == 1:
                            dve.wait_ge(prer_done, n + 1)
                        else:
                            step.wait()
                        ins = tap(xrc[:, n % 4, :], xrraw[:, t, :], vec("rnn_w", 8 * (3 - d) + n), d)
                        if d == 3:
                            ins.then_inc(xrc_done, 1)
                        else:
                            step.add(ins)
                if s == 0:
                    top(4, TOPK // 8)
                    step.add(V.tensor_scalar(selb, score[:, 0, :], -2.0e38, NEG, ALU.is_ge, ALU.mult))
            dve.wait_ge(xrc_done, 8)
            lo("ga0", 0)
            lru(3)
            step.wait()
            for it in range(9):
                if it >= 1:
                    h = it - 1
                    q = h % 2
                    dve.wait_ge(exp2_done, 2 * (h + 1))
                    step.add(V.reciprocal(recs[:, q, 0:2], sums[:, q, 0:2]))
                    step.wait()
                    if h >= 2:
                        wait_misc(dve, f"pt{h-2}")
                    for i in range(2):
                        cols = slice(0, P) if i == 0 else slice(P, 384)
                        ins = V.tensor_scalar(At2[:, q, cols], logit2[:, q, cols], recs[:, q, i:i + 1], None, ALU.mult)
                        if i:
                            ins.then_inc(attn2_done, 1)
                        else:
                            step.add(ins)
                if it >= 1 and h % 2:
                    n = h // 2
                    g = PL.G[f"po{n}"]
                    dve.wait_ge(ah_done, n + 1)
                    V.tensor_tensor(al[:, n, :], bank(g)[:, 0:T], ah[:, n, :].bitcast(F32), ALU.subtract)\
                        .then_inc(al_done, 1)
                    dve.wait_ge(al_done, n + 1)
                    dve.sem_inc(free[g % PRING], 1)
                if it < 8:
                    if it % 4 == 0:
                        dve.wait_ge(bt2_in[it // 4], 16)
                    q = it % 2
                    g = PL.G[f"lg{it}"]
                    lg = logit2[:, q, :]
                    if it >= 2:
                        dve.wait_ge(attn2_done, it - 1)
                    wait_misc(dve, f"lg{it}")
                    give_back(negated(lg, g, bt2[it // 4][:, it % 4, :], [-(64 ** -0.5)] * 2), g)
                    step.wait()
                    given_back(dve, g)
                    step.add(V.tensor_tensor(lg, lg, selb, ALU.subtract))
                    step.wait()
                    row_mins(lg, q, 0, min2_done)
                    if it:
                        lo(f"{'ga' if it < 4 else 'gb'}{it%4}", 0)
            for s in range(2):
                lo("woa", s)
                for t in range(4):
                    m, g = 4 * s + t, PL.G["woa"] + 4 * s + t
                    wait_tile(dve, "woa", 0, s, t, 4)
                    given_back(dve, PL.G[f"ga{m//2}"] + m % 2)
                    give_back(V.scalar_tensor_tensor(gaf[:, m, :], gaf[:, m, :], 1.0, bank(g)[:, 0:T],
                                                     ALU.add, ALU.mult), g)
            for s in range(4):
                lo("wor", s)
                for t in range(2):
                    m, g = 2 * s + t, PL.G["wor"] + 2 * s + t
                    wait_tile(dve, "wor", s // RING, s % RING, t)
                    given_back(dve, PL.G[f"gb{m//2}"] + m % 2)
                    give_back(V.scalar_tensor_tensor(gbf[:, m, :], gbf[:, m, :], 1.0, bank(g)[:, 0:T],
                                                     ALU.add, ALU.mult), g)
                    given_back(dve, g)
                    given_back(dve, PL.G["woa"] + m)
                    V.tensor_tensor(gaf[:, m, :], gaf[:, m, :], gbf[:, m, :], ALU.add).then_inc(merged_done, 1)
                for t in range(2):
                    m = 2 * s + t
                    dve.wait_ge(mh_done, m + 1)
                    V.tensor_tensor(ml[:, m, :], gaf[:, m, :], mh[:, m, :].bitcast(F32), ALU.subtract)\
                        .then_inc(ml_done, 1)
            residual("wout", 5, 4, tiles_two("wout"), lambda m: mod[:, 16 + m:17 + m])
            ffn(2, ("n5", [(6, lambda m: gs2[:, m:m + 1], None)], 5, ("wout", 3)), 5, lambda m: mod[:, 40 + m:41 + m])
            norm("n6", [(7, lambda m: vec("g_final", m), None)], 6)


def layout(i):

    def slabs(w, cols):
        k, n = w.shape
        return w.reshape(k // P, P, n // cols, cols).transpose(2, 1, 0, 3).reshape(n // cols, P, k // P * cols)

    def tiles(v):
        return v.reshape(-1, P).T

    def rows(v):
        return np.broadcast_to(v.reshape(1, -1), (P, v.size))

    def pairs(w, gate, up):
        k = w.shape[0]
        a, b = w[:, gate * FF:(gate + 1) * FF], w[:, up * FF:(up + 1) * FF]
        return np.stack([a.reshape(k, NF, P), b.reshape(k, NF, P)], 2).reshape(k, 2 * FF)

    a = {}
    a["x"] = i["x"][0].T.reshape(KD, P, T).transpose(1, 0, 2)
    w = i["ssm_in_w"][0]
    a["xbc"], a["z"] = slabs(w[:, DI:DI + XBC], 256), slabs(w[:, :DI], 256)
    a["w_dt"] = w[:, DI + XBC:].reshape(KD, P, 32).transpose(1, 0, 2)
    a["so"] = slabs(i["ssm_out_w"][0], P)
    a["k"], a["v"] = slabs(i["kv_w"][:, :1024], 256), slabs(i["kv_w"][:, 1024:], 256)
    a["q"], a["ao"] = slabs(i["q_w"][0], 256), slabs(i["attn_out_w"][0], 256)
    ffns = [(i["ffn_up_w"][0], i["ffn_conv_w"][0], i["ffn_conv_b"][0], i["ffn_down_w"][0], 0, 1),
            (i["ffn_up_w"][1], i["ffn_conv_w"][1], i["ffn_conv_b"][1], i["ffn_down_w"][1], 0, 1),
            (i["w_up_2"][0], i["conv_ffn_w_2"][0], i["conv_ffn_b_2"][0], i["w_down_2"][0], 1, 0)]
    v = {}
    for n, (up, cw, cb, dn, g_, u_) in enumerate(ffns):
        a[f"up{n}"] = slabs(pairs(up, g_, u_), 256)
        v[f"up_w{n}"], v[f"up_b{n}"] = tiles(pairs(cw, g_, u_)), tiles(pairs(cb[None], g_, u_))
        a[f"dn{n}a"] = dn[:2048].reshape(2, 8, P, 4, 256).transpose(3, 0, 2, 1, 4).reshape(8, P, SLOT)
        a[f"dn{n}b"] = dn[2048:].reshape(6, P, 4, 256).transpose(2, 1, 0, 3).reshape(4, P, 6 * 256)
    w, b = i["w_in_2"][0], i["b_in_2"][0]
    k0, k1, ki = slice(512, 576), slice(576, 640), slice(1280, 1344)

    def cols(m, *parts):
        return np.concatenate([m[..., p] for p in parts], -1)

    a["qb"] = slabs(w[:, 0:512], 256)
    a["kk"] = slabs(cols(w, k0, k0, k1, k1), 256)
    a["kiv"] = slabs(cols(w, ki, ki, slice(640, 768)), 256)
    a["qi"] = slabs(w[:, 768:1280], 256)
    a["w_wi"] = w[:, 1344:1352].reshape(KD, P, 8).transpose(1, 0, 2)
    for n, name in enumerate(("xr", "yr", "ga", "gb")):
        part = slice(1352 + 1024 * n, 2376 + 1024 * n)
        a[name], v["b_" + name] = slabs(w[:, part], 256), tiles(b[part])
    a["w_ada"] = i["w_ada_2"][0].T.reshape(48, P, D)
    a["c"] = i["c_2"]
    a["w_rg"], a["w_ig"] = (i[n][0].transpose(1, 0, 2).reshape(P, 1024) for n in ("w_rg_2", "w_ig_2"))
    a["woa"] = slabs(i["w_o_attn_2"][0], 512)
    a["wor"], a["wout"] = slabs(i["w_o_rnn_2"][0], 256), slabs(i["w_out_2"][0], 256)
    v.update(ssm_ln=tiles(i["ssm_ln_g"]), conv_w=tiles(i["ssm_conv_w"][0]), conv_b=tiles(i["ssm_conv_b"]),
             ssm_d=tiles(np.repeat(i["ssm_d"][0], 64)), ssm_norm=tiles(i["ssm_norm_g"]), kv_ln=tiles(i["kv_ln_g"]),
             k_norm=tiles(np.tile(i["k_norm_g"], 2)), attn_ln=tiles(i["attn_ln_g"]),
             q_norm=tiles(np.tile(i["q_norm_g"][0], 2)), subln=tiles(i["subln_g"]),
             ffn_ln0=tiles(i["ffn_ln_g"][0]), ffn_ln1=tiles(i["ffn_ln_g"][1]), b_ada=tiles(i["b_ada_2"]),
             g_mix=tiles(i["g_mix_2"]), b_q=tiles(b[0:512]), b_kk=tiles(cols(b, k0, k0, k1, k1)),
             b_ki=tiles(cols(b, ki, ki)), b_qi=tiles(b[768:1280]), rnn_w=tiles(i["conv_rnn_w_2"][0]),
             rnn_b=tiles(i["conv_rnn_b_2"]), b_rg=tiles(i["b_rg_2"]), b_ig=tiles(i["b_ig_2"]),
             lru=tiles(i["lru_lambda_2"]), g_ffn=tiles(i["g_ffn_2"]), g_final=tiles(i["g_final_2"]),
             dt_bias=rows(i["ssm_dt_bias"]), a_log=rows(i["ssm_a_log"]),
             b_wi=rows(b[1344:1352]), b_v=rows(b[640:768]))
    for name, n in VECS:
        assert v[name].shape == (P, n), (name, v[name].shape)
    a["lam"] = rows(i["lam_vecs"]).reshape(P, 4, 64)
    a["vecs"] = np.concatenate([v[name] for name, _ in VECS], 1)
    d = 255 - np.arange(384)
    n = np.maximum(d, 1).astype(np.float32)
    large = 16 + (np.log(n / 16) / np.float32(np.log(8.0)) * 16).astype(np.int32)
    bucket = np.where(d < 16, np.maximum(d, 0), np.minimum(large, 31))
    onehot = np.zeros((33, 384), np.float32)
    onehot[bucket[d >= 0], np.arange(384)[d >= 0]] = 1.0
    onehot[32, d < 0] = NEG
    a["onehot"] = onehot
    one = np.ones((1, 8), np.float32)
    a["rel"] = np.stack([np.concatenate([i[r], one]) for r in ("rel_bias", "rel_bias_2")], 1)
    return {k_: np.ascontiguousarray(m) for k_, m in a.items()}


def kernel(**inputs):
    import concourse.bacc as bacc
    from concourse.bass_utils import run_bass_kernel_spmd

    arrays = layout({k: np.asarray(a) for k, a in inputs.items()})
    nc = bacc.Bacc("TRN2", target_bir_lowering=False, num_devices=1)
    io = {k: nc.dram_tensor(f"in_{k}", a.shape, mybir.dt.from_np(a.dtype), kind="ExternalInput").ap()
          for k, a in arrays.items()}
    out = nc.dram_tensor("out_0", (P, KD, T), F32, kind="ExternalOutput").ap()
    build_program(nc, io, out)
    r = run_bass_kernel_spmd(nc, [{f"in_{k}": a for k, a in arrays.items()}], core_ids=[0])
    o = r.results[0]["out_0"]
    return o.transpose(1, 0, 2).reshape(D, T).T.reshape(1, T, D)
```
